# Optimizing a Trainium2 kernel written in Bass

```python
import math
import jax
import jax.numpy as jnp
from jax import lax
import numpy as np

D_MODEL = 1024
BATCH = 1
SEQ = 256
DEPTH = 2

SSM_HEAD_DIM = 64
SSM_HEADS = 16
SSM_INNER = SSM_HEADS * SSM_HEAD_DIM
SSM_GROUPS = 2
SSM_STATE = 128
SSM_CHUNK = 64
GDN_HEADS = 8
GDN_HEAD_DIM = 128
GDN_INNER = GDN_HEADS * GDN_HEAD_DIM
GDN_CHUNK = 64
RWKV_HEAD_DIM = 64
RWKV_HEADS = 16
RWKV_INNER = RWKV_HEADS * RWKV_HEAD_DIM
RWKV_DECAY_LORA = 64
RWKV_ICLR_LORA = 64
RWKV_GATE_LORA = 128
RWKV_GN_EPS = 64e-5
CONV_K = 4
N_BRANCH = 3
FFN_DIM = 2816
N_EXPERTS = 8
TOP_K = 2
N_DENSE = (DEPTH + 1) // 2
N_MOE = DEPTH // 2
NORM_EPS = 1e-6

CONV_CH = SSM_INNER + 2 * SSM_GROUPS * SSM_STATE + 3 * GDN_INNER
RWKV_COLS = 3 * RWKV_INNER + RWKV_DECAY_LORA + RWKV_ICLR_LORA + RWKV_GATE_LORA
IN_SPLITS = (CONV_CH, SSM_INNER, SSM_HEADS, GDN_INNER, GDN_HEADS, GDN_HEADS, RWKV_COLS, N_BRANCH * D_MODEL)
N_IN = CONV_CH + SSM_INNER + SSM_HEADS + GDN_INNER + 2 * GDN_HEADS + RWKV_COLS + N_BRANCH * D_MODEL

kernel_name = 'hybrid_ssd_gdn_rwkv7_moe_trunk'

def split_cols(t, sizes):
    idx = np.cumsum(sizes)[:-1].tolist()
    return jnp.split(t, idx, axis=-1)

def rms_norm(x, w, eps=NORM_EPS):
    xf = x.astype(jnp.float32)
    y = xf * lax.rsqrt(jnp.mean(xf * xf, axis=-1, keepdims=True) + eps)
    return (y * w.astype(jnp.float32)).astype(x.dtype)

def l2_normalize(x, eps=1e-6):
    return x * lax.rsqrt(jnp.sum(x * x, axis=-1, keepdims=True) + eps)

def causal_depthwise_conv(u, w, b):
    ch = u.shape[-1]
    y = lax.conv_general_dilated(u, w[:, None, :].astype(u.dtype), window_strides=(1,),
                                 padding=[(CONV_K - 1, 0)],
                                 dimension_numbers=('NWC', 'WIO', 'NWC'),
                                 feature_group_count=ch)
    return y + b.astype(u.dtype)

def segsum(a):
    t = a.shape[-1]
    cs = jnp.cumsum(a, axis=-1)
    diff = cs[..., :, None] - cs[..., None, :]
    mask = jnp.tril(jnp.ones((t, t), dtype=bool))
    return jnp.where(mask, diff, -jnp.inf)

def ssd_chunked(x, a, b, c, chunk):
    bsz, seq, h, p = x.shape
    n = b.shape[-1]
    nc = seq // chunk
    x = x.reshape(bsz, nc, chunk, h, p)
    b = b.reshape(bsz, nc, chunk, h, n)
    c = c.reshape(bsz, nc, chunk, h, n)
    a = a.reshape(bsz, nc, chunk, h).transpose(0, 3, 1, 2)
    a_cum = jnp.cumsum(a, axis=-1)
    decay_in = jnp.exp(segsum(a))
    scores = jnp.einsum('bclhn,bcshn->bhcls', c, b) * decay_in
    y_diag = jnp.einsum('bhcls,bcshp->bclhp', scores, x)
    decay_states = jnp.exp(a_cum[..., -1:] - a_cum)
    states = jnp.einsum('bclhn,bhcl,bclhp->bchpn', b, decay_states, x)
    states = jnp.concatenate([jnp.zeros_like(states[:, :1]), states], axis=1)
    decay_chunk = jnp.exp(segsum(jnp.pad(a_cum[..., -1], ((0, 0), (0, 0), (1, 0)))))
    states = jnp.einsum('bhzc,bchpn->bzhpn', decay_chunk, states)[:, :-1]
    y_off = jnp.einsum('bclhn,bchpn,bhcl->bclhp', c, states, jnp.exp(a_cum))
    return (y_diag + y_off).reshape(bsz, seq, h, p)

def gated_delta_chunked(q, k, v, g, beta, chunk):
    bsz, seq, h, dk = q.shape
    dv = v.shape[-1]
    nc = seq // chunk

    def to_chunks(t):
        return t.reshape(bsz, nc, chunk, h, -1).transpose(0, 3, 1, 2, 4)

    q, k, v = to_chunks(q), to_chunks(k), to_chunks(v)
    g = g.reshape(bsz, nc, chunk, h).transpose(0, 3, 1, 2)
    beta = beta.reshape(bsz, nc, chunk, h).transpose(0, 3, 1, 2)
    g_cum = jnp.cumsum(g, axis=-1)
    tri = jnp.tril(jnp.ones((chunk, chunk), dtype=bool))
    strict = jnp.tril(jnp.ones((chunk, chunk), dtype=bool), -1)
    decay_mat = jnp.exp(jnp.where(tri, g_cum[..., :, None] - g_cum[..., None, :], -jnp.inf))
    k_beta = k * beta[..., None]
    v_beta = v * beta[..., None]
    m = jnp.where(strict, jnp.einsum('bhcld,bhcsd->bhcls', k_beta, k) * decay_mat, 0.0)
    eye = jnp.eye(chunk, dtype=m.dtype)
    t_inv = lax.linalg.triangular_solve(eye + m, jnp.broadcast_to(eye, m.shape),
                                        left_side=True, lower=True)
    u = jnp.einsum('bhcls,bhcsv->bhclv', t_inv, v_beta)
    w = jnp.einsum('bhcls,bhcsk->bhclk', t_inv, k_beta * jnp.exp(g_cum)[..., None])
    qk = jnp.where(tri, jnp.einsum('bhcld,bhcsd->bhcls', q, k) * decay_mat, 0.0)

    def step(s, inp):
        q_c, k_c, u_c, w_c, qk_c, g_c = inp
        v_new = u_c - jnp.einsum('bhlk,bhkv->bhlv', w_c, s)
        o = jnp.einsum('bhlk,bhkv->bhlv', q_c * jnp.exp(g_c)[..., None], s) + jnp.einsum('bhls,bhsv->bhlv', qk_c, v_new)
        g_last = g_c[..., -1]
        k_dec = k_c * jnp.exp(g_last[..., None] - g_c)[..., None]
        s = s * jnp.exp(g_last)[..., None, None] + jnp.einsum('bhlk,bhlv->bhkv', k_dec, v_new)
        return s, o

    xs = tuple(jnp.moveaxis(t, 2, 0) for t in (q, k, u, w, qk, g_cum))
    s0 = jnp.zeros((bsz, h, dk, dv), dtype=q.dtype)
    _, o = lax.scan(step, s0, xs)
    return o.transpose(1, 0, 3, 2, 4).reshape(bsz, seq, h, dv)

def rwkv7_scan(r, w, k, v, a, b):
    bsz, seq, h, n = r.shape

    def step(s, inp):
        r_t, w_t, k_t, v_t, a_t, b_t = inp
        sa = jnp.einsum('bhij,bhj->bhi', s, a_t)
        s = s * w_t[:, :, None, :] + sa[..., None] * b_t[:, :, None, :] + v_t[..., None] * k_t[:, :, None, :]
        return s, jnp.einsum('bhij,bhj->bhi', s, r_t)

    xs = tuple(t.transpose(1, 0, 2, 3) for t in (r, w, k, v, a, b))
    s0 = jnp.zeros((bsz, h, n, n), dtype=r.dtype)
    _, y = lax.scan(step, s0, xs)
    return y.transpose(1, 0, 2, 3)

def mamba2_branch(xs, bs, cs, z, dt_raw, a_log, dt_bias, d_skip, norm_w):
    bsz, seq, _ = xs.shape
    f32 = jnp.float32
    dt = jax.nn.softplus(dt_raw.astype(f32) + dt_bias.astype(f32))
    a = -jnp.exp(a_log.astype(f32))
    x = xs.astype(f32).reshape(bsz, seq, SSM_HEADS, SSM_HEAD_DIM)
    rep = SSM_HEADS // SSM_GROUPS
    b = jnp.repeat(bs.astype(f32).reshape(bsz, seq, SSM_GROUPS, SSM_STATE), rep, axis=2)
    c = jnp.repeat(cs.astype(f32).reshape(bsz, seq, SSM_GROUPS, SSM_STATE), rep, axis=2)
    y = ssd_chunked(x * dt[..., None], a * dt, b, c, SSM_CHUNK)
    y = y + d_skip.astype(f32)[:, None] * x
    y = y.reshape(bsz, seq, SSM_INNER) * jax.nn.silu(z.astype(f32))
    yg = y.reshape(bsz, seq, SSM_GROUPS, SSM_INNER // SSM_GROUPS)
    yg = yg * lax.rsqrt(jnp.mean(yg * yg, axis=-1, keepdims=True) + NORM_EPS)
    y = yg.reshape(bsz, seq, SSM_INNER) * norm_w.astype(f32)
    return y.astype(xs.dtype)

def gdn_branch(q, k, v, z, a_raw, b_raw, a_log, dt_bias, norm_w):
    bsz, seq, _ = q.shape
    f32 = jnp.float32
    shp = (bsz, seq, GDN_HEADS, GDN_HEAD_DIM)
    qh = l2_normalize(q.astype(f32).reshape(shp)) * (GDN_HEAD_DIM ** -0.5)
    kh = l2_normalize(k.astype(f32).reshape(shp))
    vh = v.astype(f32).reshape(shp)
    g = -jnp.exp(a_log.astype(f32)) * jax.nn.softplus(a_raw.astype(f32) + dt_bias.astype(f32))
    beta = jax.nn.sigmoid(b_raw.astype(f32))
    o = gated_delta_chunked(qh, kh, vh, g, beta, GDN_CHUNK)
    o = rms_norm(o, norm_w) * jax.nn.silu(z.astype(f32).reshape(shp))
    return o.reshape(bsz, seq, GDN_INNER).astype(q.dtype)

def rwkv7_branch(u, mu, w0, w2, a0, a2, g2, k_k, k_a, r_k, ln_w, ln_b):
    bsz, seq, _ = u.shape
    f32 = jnp.float32
    uf = u.astype(f32)
    u_prev = jnp.pad(uf, ((0, 0), (1, 0), (0, 0)))[:, :-1]
    uf = uf + (u_prev - uf) * mu.astype(f32)
    r, k, v, dw, da, dg = split_cols(uf, (RWKV_INNER, RWKV_INNER, RWKV_INNER,
                                          RWKV_DECAY_LORA, RWKV_ICLR_LORA, RWKV_GATE_LORA))
    w_log = -jax.nn.softplus(-(w0.astype(f32) + jnp.tanh(dw) @ w2.astype(f32))) - 0.5
    decay = jnp.exp(-jnp.exp(w_log))
    a = jax.nn.sigmoid(a0.astype(f32) + da @ a2.astype(f32))
    g = jax.nn.sigmoid(dg) @ g2.astype(f32)

    def heads(t):
        return t.reshape(bsz, seq, RWKV_HEADS, RWKV_HEAD_DIM)

    kk = l2_normalize(heads(k * k_k.astype(f32)))
    k = k * (1.0 + (a - 1.0) * k_a.astype(f32))
    r_h, k_h, v_h, a_h, w_h = heads(r), heads(k), heads(v), heads(a), heads(decay)
    y = rwkv7_scan(r_h, w_h, k_h, v_h, -kk, kk * a_h)
    mean = jnp.mean(y, axis=-1, keepdims=True)
    var = jnp.mean(jnp.square(y - mean), axis=-1, keepdims=True)
    y = ((y - mean) * lax.rsqrt(var + RWKV_GN_EPS)).reshape(bsz, seq, RWKV_INNER)
    y = y * ln_w.astype(f32) + ln_b.astype(f32)
    bonus = jnp.sum(r_h * k_h * r_k.astype(f32), axis=-1, keepdims=True) * v_h
    y = (y + bonus.reshape(bsz, seq, RWKV_INNER)) * g
    return y.astype(u.dtype)

def token_mixer(h, w_in, conv_w, conv_b, ssm_a_log, ssm_dt_bias, ssm_d, ssm_norm_w,
                gdn_a_log, gdn_dt_bias, gdn_norm_w, rwkv_mu, rwkv_w0, rwkv_w2, rwkv_a0, rwkv_a2,
                rwkv_g2, rwkv_k_k, rwkv_k_a, rwkv_r_k, rwkv_ln_w, rwkv_ln_b,
                proj_ssm, proj_gdn, proj_rwkv, w_out):
    proj = h @ w_in
    conv_in, z_ssm, dt_raw, z_gdn, a_gdn, b_gdn, rwkv_in, gate_in = split_cols(proj, IN_SPLITS)
    conv_out = jax.nn.silu(causal_depthwise_conv(conv_in, conv_w, conv_b))
    xs, bs, cs, q, k, v = split_cols(conv_out, (SSM_INNER, SSM_GROUPS * SSM_STATE, SSM_GROUPS * SSM_STATE,
                                                GDN_INNER, GDN_INNER, GDN_INNER))
    y_ssm = mamba2_branch(xs, bs, cs, z_ssm, dt_raw, ssm_a_log, ssm_dt_bias, ssm_d, ssm_norm_w)
    y_gdn = gdn_branch(q, k, v, z_gdn, a_gdn, b_gdn, gdn_a_log, gdn_dt_bias, gdn_norm_w)
    y_rwkv = rwkv7_branch(rwkv_in, rwkv_mu, rwkv_w0, rwkv_w2, rwkv_a0, rwkv_a2, rwkv_g2,
                          rwkv_k_k, rwkv_k_a, rwkv_r_k, rwkv_ln_w, rwkv_ln_b)
    g_ssm, g_gdn, g_rwkv = split_cols(jax.nn.sigmoid(gate_in), (D_MODEL, D_MODEL, D_MODEL))
    merged = g_ssm * (y_ssm @ proj_ssm) + g_gdn * (y_gdn @ proj_gdn) + g_rwkv * (y_rwkv @ proj_rwkv)
    return merged @ w_out

def swiglu(h, w_gate, w_up, w_down):
    return (jax.nn.silu(h @ w_gate) * (h @ w_up)) @ w_down

def moe_swiglu(h, router, w_gate, w_up, w_down):
    logits = jnp.einsum('bsd,de->bse', h, router).astype(jnp.float32)
    top_logits, top_idx = lax.top_k(logits, TOP_K)
    top_p = jax.nn.softmax(top_logits, axis=-1)
    combine = jnp.einsum('bske,bsk->bse', jax.nn.one_hot(top_idx, N_EXPERTS, dtype=jnp.float32), top_p).astype(h.dtype)
    out = jnp.zeros_like(h)
    for e in range(N_EXPERTS):
        out = out + combine[..., e:e + 1] * swiglu(h, w_gate[e], w_up[e], w_down[e])
    return out

def setup_inputs(seed: int = 0) -> dict:
    key = jax.random.key(seed)
    ks = list(jax.random.split(key, 48))
    f32 = jnp.float32
    cnt = [0]

    def nk():
        cnt[0] += 1
        return ks[cnt[0] - 1]

    def nrm(shape, scale):
        return scale * jax.random.normal(nk(), shape, f32)

    def unif(shape, lo, hi):
        return jax.random.uniform(nk(), shape, f32, lo, hi)

    def gain(shape):
        return 1.0 + nrm(shape, 0.02)

    def dt_bias(shape):
        dt = jnp.exp(unif(shape, math.log(1e-3), math.log(1e-1)))
        return dt + jnp.log(-jnp.expm1(-dt))

    L = DEPTH
    return {
        'x': jax.random.normal(nk(), (BATCH, SEQ, D_MODEL), f32),
        'attn_norm_w': gain((L, D_MODEL)),
        'w_in': nrm((L, D_MODEL, N_IN), D_MODEL ** -0.5),
        'conv_w': nrm((L, CONV_K, CONV_CH), CONV_K ** -0.5),
        'conv_b': nrm((L, CONV_CH), 0.01),
        'ssm_a_log': jnp.log(unif((L, SSM_HEADS), 1.0, 16.0)),
        'ssm_dt_bias': dt_bias((L, SSM_HEADS)),
        'ssm_d': 1.0 + nrm((L, SSM_HEADS), 0.1),
        'ssm_norm_w': gain((L, SSM_INNER)),
        'gdn_a_log': jnp.log(unif((L, GDN_HEADS), 1.0, 16.0)),
        'gdn_dt_bias': dt_bias((L, GDN_HEADS)),
        'gdn_norm_w': gain((L, GDN_HEAD_DIM)),
        'rwkv_mu': unif((L, RWKV_COLS), 0.0, 1.0),
        'rwkv_w0': unif((L, RWKV_INNER), -5.0, -1.0),
        'rwkv_w2': nrm((L, RWKV_DECAY_LORA, RWKV_INNER), 0.1 * RWKV_DECAY_LORA ** -0.5),
        'rwkv_a0': nrm((L, RWKV_INNER), 0.1),
        'rwkv_a2': nrm((L, RWKV_ICLR_LORA, RWKV_INNER), RWKV_ICLR_LORA ** -0.5),
        'rwkv_g2': nrm((L, RWKV_GATE_LORA, RWKV_INNER), RWKV_GATE_LORA ** -0.5),
        'rwkv_k_k': 0.85 + nrm((L, RWKV_INNER), 0.02),
        'rwkv_k_a': gain((L, RWKV_INNER)),
        'rwkv_r_k': nrm((L, RWKV_HEADS, RWKV_HEAD_DIM), 0.1),
        'rwkv_ln_w': gain((L, RWKV_INNER)),
        'rwkv_ln_b': nrm((L, RWKV_INNER), 0.01),
        'proj_ssm': nrm((L, SSM_INNER, D_MODEL), SSM_INNER ** -0.5),
        'proj_gdn': nrm((L, GDN_INNER, D_MODEL), GDN_INNER ** -0.5),
        'proj_rwkv': nrm((L, RWKV_INNER, D_MODEL), RWKV_INNER ** -0.5),
        'w_out': nrm((L, D_MODEL, D_MODEL), D_MODEL ** -0.5),
        'ffn_norm_w': gain((L, D_MODEL)),
        'dense_w_gate': nrm((N_DENSE, D_MODEL, FFN_DIM), D_MODEL ** -0.5),
        'dense_w_up': nrm((N_DENSE, D_MODEL, FFN_DIM), D_MODEL ** -0.5),
        'dense_w_down': nrm((N_DENSE, FFN_DIM, D_MODEL), FFN_DIM ** -0.5),
        'moe_router': nrm((N_MOE, D_MODEL, N_EXPERTS), D_MODEL ** -0.5),
        'moe_w_gate': nrm((N_MOE, N_EXPERTS, D_MODEL, FFN_DIM), D_MODEL ** -0.5),
        'moe_w_up': nrm((N_MOE, N_EXPERTS, D_MODEL, FFN_DIM), D_MODEL ** -0.5),
        'moe_w_down': nrm((N_MOE, N_EXPERTS, FFN_DIM, D_MODEL), FFN_DIM ** -0.5),
        'final_norm_w': gain((D_MODEL,)),
    }

def reference(x, attn_norm_w, w_in, conv_w, conv_b, ssm_a_log, ssm_dt_bias, ssm_d, ssm_norm_w,
              gdn_a_log, gdn_dt_bias, gdn_norm_w, rwkv_mu, rwkv_w0, rwkv_w2, rwkv_a0, rwkv_a2,
              rwkv_g2, rwkv_k_k, rwkv_k_a, rwkv_r_k, rwkv_ln_w, rwkv_ln_b, proj_ssm, proj_gdn,
              proj_rwkv, w_out, ffn_norm_w, dense_w_gate, dense_w_up, dense_w_down, moe_router,
              moe_w_gate, moe_w_up, moe_w_down, final_norm_w):
    for i in range(DEPTH):
        h = rms_norm(x, attn_norm_w[i])
        x = x + token_mixer(h, w_in[i], conv_w[i], conv_b[i], ssm_a_log[i], ssm_dt_bias[i], ssm_d[i],
                            ssm_norm_w[i], gdn_a_log[i], gdn_dt_bias[i], gdn_norm_w[i], rwkv_mu[i],
                            rwkv_w0[i], rwkv_w2[i], rwkv_a0[i], rwkv_a2[i], rwkv_g2[i], rwkv_k_k[i],
                            rwkv_k_a[i], rwkv_r_k[i], rwkv_ln_w[i], rwkv_ln_b[i], proj_ssm[i],
                            proj_gdn[i], proj_rwkv[i], w_out[i])
        h = rms_norm(x, ffn_norm_w[i])
        j = i // 2
        if i % 2 == 0:
            x = x + swiglu(h, dense_w_gate[j], dense_w_up[j], dense_w_down[j])
        else:
            x = x + moe_swiglu(h, moe_router[j], moe_w_gate[j], moe_w_up[j], moe_w_down[j])
    return rms_norm(x, final_norm_w)


_drawn_inputs = setup_inputs


def setup_inputs(seed=0):
    import zlib

    import numpy as np

    out = dict(_drawn_inputs(seed))
    spreads = {}
    factors = {'gdn_norm_w': 11.404,
     'rwkv_w2': 8.0,
     'rwkv_k_k': 151.484,
     'rwkv_k_a': 3.338,
     'rwkv_ln_w': 11.265,
     'rwkv_ln_b': 26.158,
     'final_norm_w': 25.573,
     'ssm_norm_w': 3.271,
     'ffn_norm_w': 4.436}
    for name, (base, spread) in spreads.items():
        noise = np.random.default_rng([zlib.crc32(name.encode()), seed]).standard_normal(out[name].shape)
        drawn = base * np.exp(spread * noise) if base else spread * noise
        out[name] = jnp.asarray(drawn.astype(out[name].dtype))
    for name, factor in factors.items():
        out[name] = (out[name] * factor).astype(out[name].dtype)
    return out
```

```python
import math
from contextlib import ExitStack

import concourse.bass as bass
from concourse import mybir

F32 = mybir.dt.float32
F32R = mybir.dt.float32r
ALU = mybir.AluOpType
ACT = mybir.ActivationFunctionType
AX = mybir.AxisListType

P = 128
D_MODEL, SEQ, DEPTH = 1024, 256, 2
KT = D_MODEL // P
NT = SEQ // P
SSM_HEADS, SSM_P, SSM_GROUPS = 16, 64, 2
GDN_HEADS, GDN_D = 8, 128
RW_HEADS, RW_D, RW_CHUNK = 16, 64, 64
NCH = SEQ // RW_CHUNK
FFN, N_EXP = 2816, 8
FI = FFN // 256
EPS, GN_EPS = 1e-6, 64e-5
DECAY = -math.exp(-0.5)

CONV_COL, Z_COL, DT_COL = 0, 4608, 5632
ZG_COL, AB_COL, RW_COL = 5648, 6672, 6688
LORA_COL, GATE_COL = RW_COL + 3072, RW_COL + 3328
XS, BT_, CT_, QT, KTL, VT, ZT, ZGT, LT, RT, RKT, RVT, MIX_TILES = 0, 8, 10, 12, 20, 28, 36, 44, 52, 54, 62, 70, 78
SGW, AT, GT = QT, KTL, VT
N_CONV = 36

PCOL, _rows = {}, 0
for _name, _n in (("attn_norm_w", 8), ("ffn_norm_w", 8), ("rwkv_mu", 26), ("rwkv_w0", 8), ("rwkv_a0", 8),
                  ("rwkv_k_k", 8), ("rwkv_k_a", 8), ("rwkv_r_k", 8), ("rwkv_ln_w", 8), ("rwkv_ln_b", 8),
                  ("ssm_norm_w", 8), ("gdn_norm_w", 1)):
    PCOL[_name] = _rows
    _rows += _n
ROWS0 = _rows
PCOL["conv_b"], PCOL["conv_w0"], PCOL["conv_w1"], PCOL["final_norm_w"] = P, P + 36, P + 72, P + 108
ROWS1 = 116
PCOL["conv_w2"], PCOL["conv_w3"] = 2 * P, 2 * P + 36
ROWS2 = 72

LEVELS = (1, 2, 4, 8, 16, 32, 64)


class Steps:

    def __init__(self, sem, names, iters):
        assert len(set(names)) == len(names), names
        self.sem, self.names, self.iters, self.next = sem, list(names), iters, 0

    def at(self, it, name):
        return self.sem, it * len(self.names) + (self.names.index(name) + 1)

    def before(self, it):
        return self.sem, it * len(self.names)

    def step(self, name):
        assert self.names[self.next] == name, (self.names[self.next], name)
        self.next = (self.next + 1) % len(self.names)
        return self.sem


def inverse_steps(levels):
    pe, act, dve = ["x1t"], ["x1"], ["c1", "xt1"]
    for b in levels[1:]:
        pe += [f"p{b}", f"q{b}"]
        act += [f"p{b}"]
        dve += [f"c{b}"] + ([f"x{b}"] if b != levels[-1] else []) + [f"xt{b}"]
    return pe, act, dve


GDN_LEVELS, RW_LEVELS = LEVELS, LEVELS[:-1]
GDN_INV, RW_INV = inverse_steps(GDN_LEVELS), inverse_steps(RW_LEVELS)
NORM = dict(pe=["ss"], act=["sq", "ln", "rs", "hi"], dve=["var", "h", "lo"])
PHASES = {
    "setup": (1, dict(pe=["t"], dve=["pc", "mu1", "ka1"], pool=["const"])),
    "xin": (1, dict(pe=["t0", "t1"], dve=["c0", "c1"])),
    "norm1": (1, NORM),
    "scal": (1, dict(pe=["mm", "tr"], act=["aexp", "e", "ln", "beta", "eg"],
                     dve=["neg", "xb", "abs", "sp", "ad", "d", "scan", "tc", "nb"])),
    "ssdg": (1, dict(pe=["g"], dve=["g"])),
    "ssd": (8, dict(pe=["rows", "xt", "y"], act=["fix", "exp"], dve=["sel", "diff", "xdt", "p", "y", "yz"])),
    "ssdn": (2, dict(pe=["ss"], act=["sq", "ln", "rs"], dve=["var", "y"])),
    "gdn": (4, dict(pe=["ss", "rows", "kk", "tr"] + GDN_INV[0] + ["v0", "s", "ks", "v1", "o", "oss"],
                    act=["sq", "ln", "rs", "vfix", "exp", "eg"] + GDN_INV[1]
                    + ["v0", "s", "v1", "oc", "osq", "oln", "ors"],
                    dve=["sel", "eps", "q", "k", "diff", "mt0", "mt", "qkm0", "qkm", "kdec", "bv", "qe"]
                    + GDN_INV[2] + ["r1", "oeps", "on", "oz"])),
    "lora": (1, dict(pe=[x + str(i) for i in range(8) for x in "wag"],
                     act=["act"] + [x + str(i) for i in range(8) for x in "wag"])),
    "rw": (8, dict(pe=["ss", "tr", "sc", "bon", "av"] + RW_INV[0]
                   + [x + str(c) for c in range(NCH) for x in "rus" if not (c == 0 and x == "r")
                      and not (c == NCH - 1 and x == "s")] + ["y", "mean", "var"],
                   act=["sq", "e", "ln", "rs", "fix", "btz", "ktz", "tok"] + RW_INV[1]
                   + ["u" + str(c) for c in range(NCH)] + ["yc", "ysq", "yln", "yrs"],
                   dve=["lw", "kk0", "scan", "mid", "pc", "p0", "ecc", "eps", "kk", "akk", "m", "km", "bt", "kt", "kat",
                        "rt", "rkm0", "rkm", "msk", "bon", "av"] + RW_INV[2]
                   + ["sb0", "r1", "sa1", "sb1", "r2", "sa2", "sb2", "r3"]
                   + ["yc", "veps", "yn", "yw", "yb", "out"])),
    "norm2": (1, NORM),
    "route": (1, dict(pe=["mm", "tr", "rows"], act=["e"],
                      dve=["lg", "mx", "gt", "eq", "eqb", "cnt", "rank", "d", "p1", "p1r", "p2", "c0", "c1", "cr",
                           "sel", "cb"])),
    "normf": (1, dict(pe=["ss"], act=["sq", "ln", "rs"], dve=["var", "h"])),
    "xout": (1, dict(pe=["t0", "t1"], dve=["c0", "c1"])),
}
SMALL = 16 * 26


def trunk(nc, x, attn_norm_w, w_in, conv_w, conv_b, ssm_a_log, ssm_dt_bias, ssm_d, ssm_norm_w,
          gdn_a_log, gdn_dt_bias, gdn_norm_w, rwkv_mu, rwkv_w0, rwkv_w2, rwkv_a0, rwkv_a2,
          rwkv_g2, rwkv_k_k, rwkv_k_a, rwkv_r_k, rwkv_ln_w, rwkv_ln_b, proj_ssm, proj_gdn,
          proj_rwkv, w_out, ffn_norm_w, dense_w_gate, dense_w_up, dense_w_down, moe_router,
          moe_w_gate, moe_w_up, moe_w_down, final_norm_w, out):
    ctx = ExitStack()
    with ctx:
        def sb(name, shape, dt=F32):
            return ctx.enter_context(nc.sbuf_tensor(name, shape, dt))

        def sem(name):
            return ctx.enter_context(nc.semaphore(name))

        xres = sb("xres", [P, KT, SEQ])
        mix = sb("mix", [P, MIX_TILES, SEQ])
        h_hi, h_lo = sb("h_hi", [P, KT, SEQ], F32R), sb("h_lo", [P, KT, SEQ], F32R)
        y_hi, y_lo = sb("y_hi", [P, KT, SEQ], F32R), sb("y_lo", [P, KT, SEQ], F32R)
        w_raw = sb("w_raw", [P, 3, 2048])
        w_hi, w_lo = sb("w_hi", [P, 3, KT, P], F32R), sb("w_lo", [P, 3, KT, P], F32R)
        ident, ones, halves = sb("ident", [P, P]), sb("ones", [P, P]), sb("halves", [P, P])
        tri, tri64, stri64 = sb("tri", [P, 3, P]), sb("tri64", [P, P]), sb("stri64", [P, P])
        level = sb("level", [P, len(LEVELS), P])
        before = sb("before", [P, 8, 8])
        pcol = sb("pcol", [P, 3 * P])
        one_mu, one_ka = sb("one_mu", [P, 26]), sb("one_ka", [P, 8])
        dskip, dheads = sb("dskip", [P, 8]), sb("dheads", [P, SSM_HEADS])
        srow, scol = sb("srow", [P, SEQ]), sb("scol", [P, NT, P])
        wsm = sb("wsm", [P, KT, 96])
        egc, nbeta = sb("egc", [P, NT, 8]), sb("nbeta", [P, NT, 8])
        nha, credit = sb("nha", [96, 1]), sb("credit", [1, 3])
        hb, ha = sb("hb", [96, 1]), sb("ha", [96, 1])
        WORK = 6400
        work = sb("work", [P, WORK])

        def take(state, n, parts=P):
            a, state[0] = state[0], state[0] + n
            assert state[0] <= WORK, state
            return work[0:parts, a:a + n]

        def mtile(state, n):
            a, state[0] = state[0], state[0] + n
            assert state[0] <= QT, state
            return mix[:, a:a + n, :]

        bank = [ctx.enter_context(nc.psum_tensor(f"bank{i}", [P, 512], F32)) for i in range(8)]

        raw_in = [sem(f"raw_in{i}") for i in range(3)]
        hi_done, lo_done = sem("hi_done"), sem("lo_done")
        slot_free = sem("slot_free")
        bank_free = sem("bank_free")
        silu_done = sem("silu_done")
        act_ready = sem("act_ready")
        sg_done = sem("sg_done")
        down_free = sem("down_free")
        gate_done = sem("gate_done")
        y_split = sem("y_split")
        y_hi_done = sem("y_hi_done")
        small_in = sem("small_in")
        x_in, x_out, lora_in = sem("x_in"), sem("x_out"), sem("lora_in")
        link = sem("gate_products")
        conv_link, shift_link = sem("conv_taps"), sem("shift_first")
        ffn_link = sem("ffn_steps")
        pool_link = sem("const_steps")
        router_in = sem("router_in")
        s = {}
        for name, (iters, engines) in PHASES.items():
            s[name] = {e: Steps(sem(f"{name}_{e}"), names, iters) for e, names in engines.items() if names}

        def finished(eng, phase, layer):
            for st in s[phase].values():
                eng.wait_ge(st.sem, (layer + 1) * st.iters * len(st.names))

        IN_TILES, MERGE_TILES, OUT_TILES, FFN_TILES = 78, 48, 8, 6 * FI
        t_in, t_mrg, t_out, t_ffn, at = [], [], [], [], 0
        for layer in range(DEPTH):
            for starts, n in ((t_in, IN_TILES), (t_mrg, MERGE_TILES), (t_out, OUT_TILES),
                              (t_ffn, FFN_TILES * (1 if layer % 2 == 0 else N_EXP))):
                starts.append(at)
                at += n
        T_END = at
        b_in = [layer * (IN_TILES + MERGE_TILES + OUT_TILES) for layer in range(DEPTH)]
        b_mrg = [b + IN_TILES for b in b_in]
        b_out = [b + MERGE_TILES for b in b_mrg]
        f_it = [0, FI]
        s_in = [layer * 52 for layer in range(DEPTH)]

        def cols(w, c0):
            return w.rearrange("(k p) n -> p k n", p=P)[:, :, c0:c0 + 256] if isinstance(c0, int) \
                else w.rearrange("(k p) n -> p k n", p=P)[:, :, bass.ds(c0, 256)]

        def raw_view(base, kind):
            u = w_raw[:, (base // 2) % 3, :]
            if kind == "c":
                return u.rearrange("p (k n) -> p k n", n=256)[:, :, P * (base % 2):P * (base % 2) + P]
            return u.rearrange("p (j n c) -> p j n c", j=2, c=P)[:, base % 2]

        def ffn_kind(base, l):
            return "r" if base >= t_ffn[l] and (base - t_ffn[l]) % 6 >= 4 else "c"

        def v3(ap, c=P):
            return ap.rearrange("p (n c) -> p n c", c=c)

        def flat(ap):
            return ap.rearrange("p n c -> p (n c)")

        mixf = mix[:, :, :]
        hf = mix[:, 0:KT, :]
        nsq, nv, nl, nr = mix[:, 8:16, :], mix[:, 16, :], mix[:, 17, :], mix[:, 18, :]
        prow = work[:, 2048:2048 + 3 * P].rearrange("p (b c) -> p b c", c=P)
        xtok = work[:, 0:2048].rearrange("p (t d) -> p t d", t=NT)

        a = [0]
        sxb, sab, se, sln, ssp, sad, sd = [take(a, SEQ)[0:96, :] for _ in range(7)]

        a = [0]
        d_sel, d_diff, d_exp, d_p = take(a, 512), take(a, 768), take(a, 768), take(a, 768)
        d_x, d_xdt, d_y, d_sq = take(a, 256), take(a, 256), take(a, 256), take(a, 1024)
        d_v, d_l, d_r = take(a, 256), take(a, 256), take(a, 256)
        d_g = mix[:, BT_:BT_ + 3, :].rearrange("p n c -> p (n c)").rearrange("p (g c) -> p g c", g=2)

        a, m = [0], [0]
        g_q, g_k, g_qe, g_v, g_e, g_o = [mtile(m, 2) for _ in range(6)]
        g_sq, g_rs, g_sel = take(a, 1024), take(a, 1024), take(a, 1024)
        g_x, g_xt, g_c, g_pm = g_sq[:, 0:512], g_sq[:, 512:1024], g_rs[:, 0:512], g_rs[:, 512:1024]
        g_osq, g_ov = g_sel[:, 0:512], g_sel[:, 512:1024]
        g_eg, g_mt, g_qk = take(a, 512), take(a, 512), take(a, 512)
        g_kd, g_bv, g_v0, g_v1, g_s, g_r1 = [take(a, n) for n in (256, 512, 256, 256, 256, 256)]

        lw_sb, lg_sb = work[:, 0:1024], work[:, 1024:2048]

        a, m = [0], [0]
        r_e1, r_e2, r_e0, r_kk, r_akk, r_km, r_bt, r_kt, r_kat, r_rt, r_bon, r_v = \
            [mtile(m, 1)[:, 0, :] for _ in range(12)]
        r_lw, r_p, r_pc, r_p0, r_sq, r_rs = [take(a, 256) for _ in range(6)]
        r_x, r_xt, r_pm = work[:, 0:512], work[:, 512:1024], work[:, 1024:1536]
        r_btz, r_ktz = take(a, 512), take(a, 512)
        r_tok = take(a, 768)
        r_btok, r_ktok, r_vtok = [v3(r_tok[:, 256 * n:256 * n + 256]) for n in range(3)]
        r_mt, r_arb, r_ark, r_akv = [take(a, 512) for _ in range(4)]
        r_c = r_akv
        r_av, r_r, r_un, r_sb = v3(take(a, 256)), take(a, 128), v3(take(a, 256)), v3(take(a, 256))
        r_c4, r_ec, r_ecc = take(a, NCH), take(a, NCH), take(a, NCH)

        merged = mix[:, 0:KT, :]
        gate_sb = mix[:, KT:KT + 2, :]
        prod_sb = mix[:, KT + 2:KT + 4, :]
        y_of = (ZT, ZGT, RT)
        f_sg = v3(work[:, 0:512], 256)
        f_act = v3(work[:, 512:1024], 256)
        f_acc = mix[:, 20:28, :]
        cb = mix[:, 28:36, :]
        rt = work[:, 1024:6400]
        q_w = v3(rt[:, 0:64], 8)
        q_l, q_m, q_rank, q_c0, q_c1, q_c = [v3(rt[:, 64 + 16 * n:80 + 16 * n], 8) for n in range(6)]
        q_gt, q_eq = [rt[:, 192 + 128 * n:320 + 128 * n].rearrange("p (t e f) -> p t e f", t=2, e=8) for n in range(2)]
        q_d, q_e, q_p1, q_1, q_p2 = [rt[:, 448 + 2 * n:450 + 2 * n] for n in range(5)]
        q_cr, q_sel = rt[0:8, 512:768], v3(rt[0:8, 768:768 + 2048], 256)
        identb = ident[:, :].rearrange("p (o c) -> p o c", o=1)

        def over(ap, n):
            return ap.rearrange("p (o c) -> p o c", o=1).broadcast_to([ap.shape[0], n, ap.shape[1]])

        block = ctx.enter_context(nc.Block())

        @block.sync
        def _(sp):
            def load(dst, src, arrived):
                sp.dma_start(dst, src).then_inc(arrived, 16)

            def unit(t, src, sub="c"):
                base, rest = t
                u = base // 2
                slot = w_raw[:, u % 3, :]
                if not isinstance(rest, int) or base + rest >= 6:
                    sp.wait_ge(lo_done, rest + (base - 4))
                load(slot.rearrange("p (k n) -> p k n", n=256 if sub == "c" else 1024), src, raw_in[u % 3])

            load(work[:, 0:2048].rearrange("p (t d) -> p t d", t=NT), x[0].rearrange("(t p) d -> p t d", p=P), x_in)

            def parameters(l):
                n = 0
                rows = work[:, 2048:2048 + 3 * P].rearrange("p (b c) -> p b c", c=P)
                for name, src, count in (
                        ("attn_norm_w", attn_norm_w[l], 8), ("ffn_norm_w", ffn_norm_w[l], 8),
                        ("rwkv_mu", rwkv_mu[l], 26), ("rwkv_w0", rwkv_w0[l], 8), ("rwkv_a0", rwkv_a0[l], 8),
                        ("rwkv_k_k", rwkv_k_k[l], 8), ("rwkv_k_a", rwkv_k_a[l], 8),
                        ("rwkv_ln_w", rwkv_ln_w[l], 8), ("rwkv_ln_b", rwkv_ln_b[l], 8),
                        ("ssm_norm_w", ssm_norm_w[l], 8), ("gdn_norm_w", gdn_norm_w[l], 1),
                        ("conv_b", conv_b[l], 36), ("conv_w0", conv_w[l, 0], 36), ("conv_w1", conv_w[l, 1], 36),
                        ("conv_w2", conv_w[l, 2], 36), ("conv_w3", conv_w[l, 3], 36),
                        ("final_norm_w", final_norm_w, 8)):
                    r = PCOL[name]
                    load(rows[r % P:r % P + count, r // P, :], src.rearrange("(n c) -> n c", c=P), small_in)
                    n += 1
                r = PCOL["rwkv_r_k"]
                load(rows[r:r + 8, 0, :], rwkv_r_k[l].rearrange("(n a) d -> n (a d)", a=2), small_in)
                load(dheads[:], ssm_d[l].rearrange("(o n) -> o n", o=1).broadcast_to([P, SSM_HEADS]), small_in)
                for c, src, m in ((0, DT_COL, 16), (32, AB_COL, 8), (64, AB_COL + 8, 8)):
                    load(wsm[:, :, c:c + m],
                         w_in[l].rearrange("(k p) n -> p k n", p=P)[:, :, src:src + m], small_in)
                load(hb[0:16, :], ssm_dt_bias[l].rearrange("(n o) -> n o", o=1), small_in)
                load(hb[32:40, :], gdn_dt_bias[l].rearrange("(n o) -> n o", o=1), small_in)
                load(ha[0:16, :], ssm_a_log[l].rearrange("(n o) -> n o", o=1), small_in)
                load(ha[32:40, :], gdn_a_log[l].rearrange("(n o) -> n o", o=1), small_in)
                return n + 9

            for l in range(DEPTH):
                if l == 0:
                    sp.wait_ge(*s["setup"]["pool"].at(0, "const"))
                else:
                    sp.wait_ge(down_free, 1 + FI)
                assert 16 * parameters(l) == SMALL
                wi = w_in[l]
                for k in range(3):
                    unit((t_in[l] + 2 * k, 0), cols(wi, CONV_COL + 256 * k))
                with sp.Fori(1, N_CONV // 6) as i:
                    for k in range(3):
                        unit((t_in[l] + 2 * k, i * 6), cols(wi, i * 768 + (CONV_COL + 256 * k)))
                t = t_in[l] + N_CONV
                for c in [Z_COL + 256 * i for i in range(4)] + [ZG_COL + 256 * i for i in range(4)] + [LORA_COL]:
                    unit((t, 0), cols(wi, c))
                    t += 2
                with sp.Fori(0, 4) as i:
                    for k in range(3):
                        unit((t + 2 * k, i * 6), cols(wi, i * 768 + (RW_COL + 256 * k)))
                for b, w in enumerate((proj_ssm, proj_gdn, proj_rwkv)):
                    for i in range(4):
                        unit((t_mrg[l] + 16 * b + 4 * i, 0), cols(wi, GATE_COL + 1024 * b + 256 * i))
                        unit((t_mrg[l] + 16 * b + 4 * i + 2, 0), cols(w[l], 256 * i))
                        if b == 0 and i == 0:
                            finished(sp, "gdn", l)
                            load(work[0:64, 0:1024], rwkv_w2[l], lora_in)
                            load(work[64:128, 0:1024], rwkv_a2[l], lora_in)
                            load(work[:, 1024:2048], rwkv_g2[l], lora_in)
                for i in range(4):
                    unit((t_out[l] + 2 * i, 0), cols(w_out[l], 256 * i))
                t = t_ffn[l]
                if l % 2 == 1:
                    finished(sp, "rw", l)
                    load(q_w, moe_router[l // 2].rearrange("(k p) e -> p k e", p=P), router_in)
                if l % 2 == 0:
                    with sp.Fori(0, FI) as i:
                        unit((t, i * 6), cols(dense_w_gate[l // 2], i * 256))
                        unit((t + 2, i * 6), cols(dense_w_up[l // 2], i * 256))
                        unit((t + 4, i * 6), dense_w_down[l // 2].rearrange("(i k p) n -> i p k n", k=2, p=P)[i], "r")
                else:
                    with sp.Fori(0, N_EXP) as e:
                        with sp.Fori(0, FI) as i:
                            it = (e * FI + i) * 6
                            unit((t, it), cols(moe_w_gate[l // 2][e], i * 256))
                            unit((t + 2, it), cols(moe_w_up[l // 2][e], i * 256))
                            unit((t + 4, it),
                                 moe_w_down[l // 2][e].rearrange("(i k p) n -> i p k n", k=2, p=P)[i], "r")
            sp.wait_ge(*s["xout"]["dve"].at(0, "c1"))
            sp.dma_start(out[0].rearrange("(t p) d -> p t d", p=P),
                         work[:, 0:2048].rearrange("p (t d) -> p t d", t=NT)).then_inc(x_out, 16)
            sp.wait_ge(x_out, 16)

        @block.gpsimd
        def _(pool):
            st = s["setup"]["pool"]
            for t in (ident, level, before, wsm, hb, ha, srow):
                nc.gpsimd.memset(t[:], 0.0)
            for t in (ones, tri, halves):
                z = nc.gpsimd.memset(t[:], 1.0)
            z.then_inc(pool_link, 1)
            for c, (free, n) in enumerate(((slot_free, 3), (bank_free, 3), (down_free, 1))):
                nc.gpsimd.memset(credit[:, c:c + 1], 0.0).then_inc(free, n)
            pool.wait_ge(pool_link, 1)
            nc.gpsimd.affine_select(out=ident[:], in_=ident[:], compare_op=ALU.not_equal, fill=1.0, base=0,
                                    pattern=[[-1, P]], channel_multiplier=1)
            for n in (0, 2):
                nc.gpsimd.affine_select(out=tri[:, n, :], in_=tri[:, n, :], compare_op=ALU.is_ge, fill=0.0, base=0,
                                        pattern=[[1, P]], channel_multiplier=-1)
            nc.gpsimd.affine_select(out=halves[:, 0:64], in_=halves[:, 0:64], compare_op=ALU.is_ge, fill=0.0, base=63,
                                    pattern=[[0, 64]], channel_multiplier=-1)
            nc.gpsimd.affine_select(out=halves[:, 64:128], in_=halves[:, 64:128], compare_op=ALU.is_ge, fill=0.0,
                                    base=-64, pattern=[[0, 64]], channel_multiplier=1)
            for n, b in enumerate(LEVELS):
                v = level[:, n, :].rearrange("p (m two c) -> p m two c", two=2, c=b)[:, :, 1, :]
                one = nc.gpsimd.memset(v, 1.0)
            for e in range(1, 8):
                z = nc.gpsimd.memset(before[:, e, 0:e], 1.0)
            z.then_inc(pool_link, 1)
            pool.wait_ge(pool_link, 2)
            for n, b in enumerate(LEVELS):
                v = level[:, n, :].rearrange("p (m two c) -> p m two c", two=2, c=b)[:, :, 1, :]
                nc.gpsimd.affine_select(out=v, in_=v, compare_op=ALU.is_ge, fill=0.0, base=0,
                                        pattern=[[-2 * b, P // (2 * b)], [0, b]], channel_multiplier=1)
            z = nc.gpsimd.tensor_tensor(tri64[:], tri[:, 0, :], halves[:], ALU.mult)
            z.then_inc(pool_link, 1)
            pool.wait_ge(pool_link, 3)
            for n, b in enumerate(LEVELS):
                v = level[:, n, :].rearrange("p (m two c) -> p m two c", two=2, c=b)[:, :, 1, :]
                nc.gpsimd.affine_select(out=v, in_=v, compare_op=ALU.is_ge, fill=0.0, base=b - 1,
                                        pattern=[[2 * b, P // (2 * b)], [0, b]], channel_multiplier=-1)
            z = nc.gpsimd.tensor_tensor(stri64[:], tri64[:], ident[:], ALU.subtract)
            z.then_inc(st.step("const"), 1)

            def split_lo(base, i, kind):
                pool.wait_ge(hi_done, i * 6 + (base + 1))
                nc.gpsimd.tensor_tensor(w_lo[:, base % 3], raw_view(base, kind), w_hi[:, base % 3].bitcast(F32),
                                        ALU.subtract).then_inc(lo_done, 1)

            for l in range(DEPTH):
                with pool.Fori(0, IN_TILES // 6) as i:
                    for j in range(6):
                        split_lo(t_in[l] + j, i, "c")
                for t in range(t_mrg[l], t_ffn[l]):
                    split_lo(t, 0, "c")
                with pool.Fori(0, FI * (1 if l % 2 == 0 else N_EXP)) as i:
                    for j in range(6):
                        split_lo(t_ffn[l] + j, i, "c" if j < 4 else "r")

        @block.scalar
        def _(act):
            def split_hi(base, i, kind):
                u = base // 2
                act.wait_ge(raw_in[u % 3], i * 16 + 16 * (u // 3 + 1))
                act.wait_ge(slot_free, i * 6 + (base + 1))
                nc.scalar.activation(w_hi[:, base % 3], raw_view(base, kind), ACT.Copy).then_inc(hi_done, 1)

            def norm(ph, l, split=True):
                st, it = s[ph], (l if ph != "normf" else 0)
                A, V, T = st["act"], st["dve"], st["pe"]
                nc.scalar.activation(nsq, xres[:], ACT.Square).then_inc(A.step("sq"), 1)
                act.wait_ge(*V.at(it, "var"))
                nc.scalar.activation(nl, nv, ACT.Ln).then_inc(A.step("ln"), 1)
                act.wait_ge(*A.at(it, "ln"))
                nc.scalar.activation(nr, nl, ACT.Exp, scale=-0.5).then_inc(A.step("rs"), 1)
                if split:
                    act.wait_ge(*V.at(it, "h"))
                    nc.scalar.activation(h_hi[:], hf, ACT.Copy).then_inc(A.step("hi"), 1)

            def inverse(st, it, levels, banks, x, pm):
                A, T = st["act"], st["pe"]
                act.wait_ge(*T.at(it, "x1t"))
                nc.scalar.activation(x, bank[banks[0]][:], ACT.Copy).then_inc(A.step("x1"), 1)
                for b in levels[1:]:
                    act.wait_ge(*T.at(it, f"p{b}"))
                    nc.scalar.activation(pm, bank[banks[0]][:], ACT.Copy).then_inc(A.step(f"p{b}"), 1)

            for l in range(DEPTH):
                if l == 0:
                    act.wait_ge(*s["xin"]["dve"].at(0, "c1"))
                else:
                    act.wait_ge(down_free, 1 + FI)
                norm("norm1", l)
                st, it = s["scal"], l
                A, V, T = st["act"], st["dve"], st["pe"]
                act.wait_ge(small_in, SMALL * (l + 1))
                nc.scalar.activation(nha[:], ha[:], ACT.Exp).then_inc(A.step("aexp"), 1)
                act.wait_ge(*V.at(it, "abs"))
                nc.scalar.activation(se, sab, ACT.Exp, scale=-1.0).then_inc(A.step("e"), 1)
                act.wait_ge(*A.at(it, "e"))
                nc.scalar.activation(sln, se, ACT.Ln, bias=1.0).then_inc(A.step("ln"), 1)
                act.wait_ge(*V.at(it, "d"))
                nc.scalar.activation(srow[64:72, :], sd[64:72, :], ACT.Exp).then_inc(A.step("beta"), 1)
                act.wait_ge(*V.at(it, "tc"))
                nc.scalar.activation(egc[:], scol[:, :, 32:40], ACT.Exp).then_inc(A.step("eg"), 1)

                def tile(base, i, silu):
                    split_hi(base + 2, i, ffn_kind(base + 2, l))
                    if silu is not None:
                        n = base - t_in[l]
                        act.wait_ge(bank_free, i * 6 + (3 + b_in[l] + n + 1))
                        nc.scalar.activation(mix[:, silu, :], mix[:, silu, :], ACT.Silu).then_inc(silu_done, 1)

                if l == 0:
                    split_hi(0, 0, "c")
                    split_hi(1, 0, "c")
                with act.Fori(0, N_CONV // 6) as i:
                    for j in range(6):
                        tile(t_in[l] + j, i, i * 6 + j)
                for j in range(18):
                    tile(t_in[l] + N_CONV + j, 0, ZT + j if j < 16 else None)
                with act.Fori(0, 4) as i:
                    for j in range(6):
                        tile(t_in[l] + N_CONV + 18 + j, i, None)

                st = s["ssd"]
                A, V, T = st["act"], st["dve"], st["pe"]
                with act.Fori(0, 8) as i:
                    it = i + 8 * l
                    act.wait_ge(*T.before(it))
                    act.wait_ge(*V.before(it))
                    act.wait_ge(silu_done, s_in[l] + 52)
                    nc.scalar.activation(d_x, mix[:, i, :], ACT.Copy).then_inc(A.step("fix"), 1)
                    act.wait_ge(*V.at(it, "diff"))
                    nc.scalar.activation(d_exp, d_diff, ACT.Exp).then_inc(A.step("exp"), 1)
                st = s["ssdn"]
                A, V, T = st["act"], st["dve"], st["pe"]
                finished(act, "ssd", l)
                for g in range(2):
                    it = 2 * l + g
                    act.wait_ge(*T.before(it))
                    nc.scalar.activation(v3(d_sq, 256), mix[:, ZT + 4 * g:ZT + 4 * g + 4, :], ACT.Square)\
                        .then_inc(A.step("sq"), 1)
                    act.wait_ge(*V.at(it, "var"))
                    nc.scalar.activation(d_l, d_v, ACT.Ln).then_inc(A.step("ln"), 1)
                    act.wait_ge(*A.at(it, "ln"))
                    nc.scalar.activation(d_r, d_l, ACT.Exp, scale=-0.5).then_inc(A.step("rs"), 1)

                st = s["gdn"]
                A, V, T = st["act"], st["dve"], st["pe"]
                finished(act, "ssdn", l)
                with act.Fori(0, 4) as i:
                    it = i + 4 * l
                    act.wait_ge(*T.before(it))
                    act.wait_ge(*V.before(it))
                    nc.scalar.activation(v3(g_sq[:, 0:512], 256), mix[:, bass.ds(i * 2 + QT, 2), :], ACT.Square)
                    nc.scalar.activation(v3(g_sq[:, 512:1024], 256), mix[:, bass.ds(i * 2 + KTL, 2), :], ACT.Square)\
                        .then_inc(A.step("sq"), 1)
                    act.wait_ge(*V.at(it, "eps"))
                    nc.scalar.activation(g_rs, g_rs, ACT.Ln).then_inc(A.step("ln"), 1)
                    act.wait_ge(*A.at(it, "ln"))
                    nc.scalar.activation(g_rs, g_rs, ACT.Exp, scale=-0.5).then_inc(A.step("rs"), 1)
                    nc.scalar.activation(g_v, mix[:, bass.ds(i * 2 + VT, 2), :], ACT.Copy).then_inc(A.step("vfix"), 1)
                    act.wait_ge(*V.at(it, "diff"))
                    nc.scalar.activation(g_e, g_e, ACT.Exp).then_inc(A.step("exp"), 1)
                    nc.scalar.activation(g_eg, bank[5][:], ACT.Exp).then_inc(A.step("eg"), 1)
                    inverse(st, it, GDN_LEVELS, (1,), g_x, g_pm)
                    act.wait_ge(*T.at(it, "v0"))
                    nc.scalar.activation(g_v0, bank[5][:, 0:256], ACT.Copy).then_inc(A.step("v0"), 1)
                    act.wait_ge(*T.at(it, "s"))
                    nc.scalar.activation(g_s, bank[6][:, 0:256], ACT.Copy).then_inc(A.step("s"), 1)
                    act.wait_ge(*T.at(it, "v1"))
                    nc.scalar.activation(g_v1, bank[5][:, 0:256], ACT.Copy).then_inc(A.step("v1"), 1)
                    act.wait_ge(*T.at(it, "o"))
                    nc.scalar.activation(flat(g_o), bank[4][:], ACT.Copy).then_inc(A.step("oc"), 1)
                    act.wait_ge(*A.at(it, "oc"))
                    nc.scalar.activation(g_osq, flat(g_o), ACT.Square).then_inc(A.step("osq"), 1)
                    act.wait_ge(*V.at(it, "oeps"))
                    nc.scalar.activation(g_ov, g_ov, ACT.Ln).then_inc(A.step("oln"), 1)
                    act.wait_ge(*A.at(it, "oln"))
                    nc.scalar.activation(g_ov, g_ov, ACT.Exp, scale=-0.5).then_inc(A.step("ors"), 1)

                st, it = s["lora"], l
                A, T = st["act"], st["pe"]
                finished(act, "gdn", l)
                nc.scalar.activation(mix[0:64, LT, :], mix[0:64, LT, :], ACT.Tanh)
                nc.scalar.activation(mix[:, LT + 1, :], mix[:, LT + 1, :], ACT.Sigmoid).then_inc(A.step("act"), 1)
                for i in range(8):
                    for x, b, dst, bias in (("w", 3, SGW, "rwkv_w0"), ("a", 4, AT, "rwkv_a0"), ("g", 5, GT, None)):
                        act.wait_ge(*T.at(it, f"{x}{i}"))
                        if bias:
                            z = nc.scalar.activation(mix[:, dst + i, :], bank[b][:, 0:256], ACT.Sigmoid,
                                                     bias=pcol[:, PCOL[bias] + i:PCOL[bias] + i + 1])
                        else:
                            z = nc.scalar.activation(mix[:, dst + i, :], bank[b][:, 0:256], ACT.Copy)
                        z.then_inc(A.step(f"{x}{i}"), 1)

                st = s["rw"]
                A, V, T = st["act"], st["dve"], st["pe"]
                finished(act, "lora", l)
                with act.Fori(0, 8) as i:
                    it = i + 8 * l
                    act.wait_ge(*T.before(it))
                    act.wait_ge(*V.at(it, "kk0"))
                    nc.scalar.activation(r_sq, r_kk, ACT.Square).then_inc(A.step("sq"), 1)
                    act.wait_ge(*V.at(it, "p0"))
                    nc.scalar.activation(r_e1, r_pc, ACT.Exp)
                    nc.scalar.activation(r_e2, r_pc, ACT.Exp, scale=-1.0)
                    nc.scalar.activation(r_e0, r_p0, ACT.Exp)
                    nc.scalar.activation(r_ec, r_c4, ACT.Exp).then_inc(A.step("e"), 1)
                    act.wait_ge(*V.at(it, "eps"))
                    nc.scalar.activation(r_rs, r_rs, ACT.Ln).then_inc(A.step("ln"), 1)
                    act.wait_ge(*A.at(it, "ln"))
                    nc.scalar.activation(r_rs, r_rs, ACT.Exp, scale=-0.5).then_inc(A.step("rs"), 1)
                    nc.scalar.activation(r_v, mix[:, i + RVT, :], ACT.Copy).then_inc(A.step("fix"), 1)
                    act.wait_ge(*V.at(it, "bt"))
                    for h in range(2):
                        z = nc.scalar.activation(r_btz[:, 256 * h:256 * h + 256], r_bt, ACT.Copy,
                                                 scale=halves[:, 64 * h:64 * h + 1])
                    z.then_inc(A.step("btz"), 1)
                    act.wait_ge(*V.at(it, "kt"))
                    for h in range(2):
                        z = nc.scalar.activation(r_ktz[:, 256 * h:256 * h + 256], r_kt, ACT.Copy,
                                                 scale=halves[:, 64 * h:64 * h + 1])
                    z.then_inc(A.step("ktz"), 1)
                    act.wait_ge(*T.at(it, "tr"))
                    nc.scalar.activation(r_tok[:, 0:512], bank[4][:], ACT.Copy)
                    nc.scalar.activation(r_tok[:, 512:768], bank[5][:, 0:256], ACT.Copy).then_inc(A.step("tok"), 1)
                    inverse(st, it, RW_LEVELS, (4,), r_x, r_pm)
                    for c in range(NCH):
                        t, o = c // 2, 64 * (c % 2)
                        act.wait_ge(*T.at(it, f"u{c}"))
                        nc.scalar.activation(r_un[o:o + 64, t, :], bank[2][o:o + 64, 0:128], ACT.Copy, scale=-1.0)\
                            .then_inc(A.step(f"u{c}"), 1)
                    act.wait_ge(*T.at(it, "y"))
                    nc.scalar.activation(r_e1, bank[4][:, 0:256], ACT.Copy).then_inc(A.step("yc"), 1)
                    act.wait_ge(*V.at(it, "yc"))
                    nc.scalar.activation(r_e2, r_e0, ACT.Square).then_inc(A.step("ysq"), 1)
                    act.wait_ge(*V.at(it, "veps"))
                    nc.scalar.activation(r_rs, r_rs, ACT.Ln).then_inc(A.step("yln"), 1)
                    act.wait_ge(*A.at(it, "yln"))
                    nc.scalar.activation(r_rs, r_rs, ACT.Exp, scale=-0.5).then_inc(A.step("yrs"), 1)

                finished(act, "rw", l)
                for b in range(4):
                    src = mix[:, y_of[b]:y_of[b] + 8, :] if b < 3 else merged
                    if b > 0:
                        act.wait_ge(slot_free, 3 + t_mrg[l] + 16 * b)
                    if b == 3:
                        act.wait_ge(bank_free, 3 + b_out[l])
                    nc.scalar.activation(y_hi[:], src, ACT.Copy).then_inc(y_hi_done, 1)
                    if b == 3:
                        for j in range(OUT_TILES):
                            split_hi(t_out[l] + j + 2, 0, "c")
                        break
                    for n in range(4):
                        for j in range(4):
                            t = t_mrg[l] + 16 * b + 4 * n + j
                            split_hi(t + 2, 0, "c")
                            if j >= 2:
                                k = b_mrg[l] + 16 * b + 4 * n + j - 2
                                act.wait_ge(bank_free, 3 + k + 1)
                                nc.scalar.activation(gate_sb[:, j - 2, :], gate_sb[:, j - 2, :], ACT.Sigmoid)\
                                    .then_inc(gate_done, 1)

                act.wait_ge(bank_free, 3 + b_out[l] + OUT_TILES)
                norm("norm2", l)
                if l % 2 == 1:
                    act.wait_ge(*s["route"]["dve"].at(l // 2, "d"))
                    nc.scalar.activation(q_e, q_d, ACT.Exp).then_inc(s["route"]["act"].step("e"), 1)

                def ffn(i, last=False):
                    it = i + f_it[l]
                    for j in range(6):
                        if not (last and j >= 4):
                            split_hi(t_ffn[l] + j + 2, i, ffn_kind(t_ffn[l] + j + 2, l) if j < 4 else "c")
                        if j in (2, 3):
                            k = j - 2
                            act.wait_ge(slot_free, i * 6 + (3 + t_ffn[l] + j - 2 + 1))
                            act.wait_ge(act_ready, it * 2)
                            nc.scalar.activation(f_sg[:, k, :], bank[k][:, 0:256], ACT.Silu).then_inc(sg_done, 1)

                n = FI * (1 if l % 2 == 0 else N_EXP)
                with act.Fori(0, n - 1) as i:
                    ffn(i)
                ffn(n - 1, last=(l == DEPTH - 1))
            act.wait_ge(down_free, 1 + FI + FI * N_EXP)
            norm("normf", 0, split=False)

        @block.tensor
        def _(pe):
            def product(dst, base, i, hi, lo, free=None, own=0, start=True):
                pe.wait_ge(lo_done, i * 6 + (base + 1))
                if free is not None:
                    pe.wait_ge(bank_free, free)
                for k in range(KT):
                    wh, wl = w_hi[:, base % 3, k, :], w_lo[:, base % 3, k, :]
                    nc.tensor.matmul(dst, wh, hi[:, k, :], start=(k == 0), stop=False)
                    nc.tensor.matmul(dst, wh, lo[:, k, :], start=False, stop=False)
                    z = nc.tensor.matmul(dst, wl, hi[:, k, :], start=False, stop=(k == KT - 1))
                z.then_inc(slot_free, 1)

            def mm(dst, lhsT, rhs, start=True, stop=True, **kw):
                return nc.tensor.matmul(dst, lhsT, rhs, start=start, stop=stop, **kw)

            def tr(dst, src):
                n = src.shape[0]
                return nc.tensor.transpose(dst, src, ident[0:n, 0:n])

            def norm(ph, l):
                st, it = s[ph], (l if ph != "normf" else 0)
                pe.wait_ge(*st["act"].at(it, "sq"))
                for k in range(KT):
                    z = mm(bank[3][:, 0:256], ones[:], nsq[:, k, :], start=(k == 0), stop=(k == KT - 1))
                z.then_inc(st["pe"].step("ss"), 1)

            def inverse(st, it, levels, banks, c, x, xt, pm):
                A, V, T = st["act"], st["dve"], st["pe"]
                pe.wait_ge(*V.at(it, "xt1"))
                for u in range(4):
                    z = tr(bank[banks[0]][:, P * u:P * u + P], v3(xt)[:, u, :])
                z.then_inc(T.step("x1t"), 1)
                pe.wait_ge(*A.at(it, "x1"))
                for n, b in enumerate(levels[1:]):
                    pe.wait_ge(*V.at(it, f"c{b}"))
                    if n > 0:
                        pe.wait_ge(*V.at(it, f"xt{levels[n]}"))
                    for u in range(4):
                        z = mm(bank[banks[0]][:, P * u:P * u + P], v3(c)[:, u, :], v3(x)[:, u, :])
                    z.then_inc(T.step(f"p{b}"), 1)
                    pe.wait_ge(*A.at(it, f"p{b}"))
                    if b != levels[-1]:
                        for u in range(4):
                            mm(bank[banks[1]][:, P * u:P * u + P], v3(xt)[:, u, :], v3(pm)[:, u, :])
                    for u in range(4):
                        z = mm(bank[banks[2]][:, P * u:P * u + P], v3(pm)[:, u, :], v3(xt)[:, u, :])
                    z.then_inc(T.step(f"q{b}"), 1)

            T = s["xin"]["pe"]
            pe.wait_ge(*s["setup"]["pool"].at(0, "const"))
            pe.wait_ge(x_in, 16)
            for t in range(NT):
                for k in range(KT):
                    z = tr(bank[4 + 2 * t + k // 4][:, P * (k % 4):P * (k % 4) + P], xtok[:, t, P * k:P * k + P])
                z.then_inc(T.step(f"t{t}"), 1)

            for l in range(DEPTH):
                pe.wait_ge(small_in, SMALL * (l + 1))
                for b, n in enumerate((ROWS0, ROWS1, ROWS2)):
                    z = tr(bank[0][:, P * b:P * b + n], prow[0:n, b, :])
                z.then_inc(s["setup"]["pe"].step("t"), 1)
                norm("norm1", l)
                st, it = s["scal"], l
                A, V, T = st["act"], st["dve"], st["pe"]
                pe.wait_ge(*s["norm1"]["dve"].at(l, "h"))
                for k in range(KT):
                    z = mm(bank[4][0:96, 0:256], wsm[:, k, :], hf[:, k, :], start=(k == 0), stop=(k == KT - 1))
                z.then_inc(T.step("mm"), 1)
                pe.wait_ge(*A.at(it, "beta"))
                pe.wait_ge(*V.at(it, "scan"))
                for t in range(NT):
                    z = tr(bank[5][:, P * t:P * t + P], srow[:, P * t:P * t + P])
                z.then_inc(T.step("tr"), 1)

                pe.wait_ge(*s["norm1"]["dve"].at(l, "lo"))
                pe.wait_ge(*s["setup"]["dve"].at(l, "pc"))
                with pe.Fori(0, IN_TILES // 6) as i:
                    for j in range(6):
                        product(bank[(b_in[l] + j) % 3][:, 0:256], t_in[l] + j, i, h_hi, h_lo,
                                free=i * 6 + (b_in[l] + j + 1))

                st = s["ssdg"]
                pe.wait_ge(silu_done, s_in[l] + 52)
                pe.wait_ge(bank_free, 3 + b_in[l] + IN_TILES)
                pe.wait_ge(*s["scal"]["dve"].at(l, "tc"))
                for g in range(2):
                    mm(bank[4 + g][:, 0:256], mix[:, BT_ + g, 0:128], mix[:, CT_ + g, :])
                    z = mm(bank[4 + g][:, 256:384], mix[:, BT_ + g, 128:256], mix[:, CT_ + g, 128:256])
                z.then_inc(st["pe"].step("g"), 1)
                pe.wait_ge(*st["dve"].at(l, "g"))
                st = s["ssd"]
                A, V, T = st["act"], st["dve"], st["pe"]
                with pe.Fori(0, 8) as i:
                    it = i + 8 * l
                    pe.wait_ge(*V.before(it))
                    pe.wait_ge(*V.at(it, "sel"))
                    mm(bank[3][:], ones[:], d_sel).then_inc(T.step("rows"), 1)
                    pe.wait_ge(*A.at(it, "fix"))
                    for t in range(NT):
                        z = tr(bank[4][:, P * t:P * t + P], d_x[:, P * t:P * t + P])
                    z.then_inc(T.step("xt"), 1)
                    pe.wait_ge(*V.at(it, "p"))
                    for h in range(2):
                        o = 64 * h
                        mm(bank[5][o:o + 64, 0:256], d_xdt[:, o:o + 64], d_p[:, 384 * h:384 * h + 256], stop=False)
                        z = mm(bank[5][o:o + 64, 128:256], d_xdt[:, 128 + o:192 + o],
                               d_p[:, 384 * h + 256:384 * h + 384], start=False)
                    z.then_inc(T.step("y"), 1)
                st = s["ssdn"]
                for g in range(2):
                    it = 2 * l + g
                    pe.wait_ge(*st["act"].at(it, "sq"))
                    pe.wait_ge(*st["dve"].before(it))
                    for k in range(4):
                        z = mm(bank[6][:, 0:256], ones[:], d_sq[:, 256 * k:256 * k + 256], start=(k == 0), stop=(k == 3))
                    z.then_inc(st["pe"].step("ss"), 1)

                st = s["gdn"]
                A, V, T = st["act"], st["dve"], st["pe"]
                finished(pe, "ssdn", l)
                with pe.Fori(0, 4) as i:
                    it = i + 4 * l
                    pe.wait_ge(*V.before(it))
                    pe.wait_ge(*A.at(it, "sq"))
                    mm(bank[3][:], ones[:], g_sq[:, 0:512])
                    mm(bank[4][:], ones[:], g_sq[:, 512:1024]).then_inc(T.step("ss"), 1)
                    pe.wait_ge(*V.at(it, "sel"))
                    mm(bank[5][:], ones[:], g_sel[:, 0:512])
                    mm(bank[6][:], ones[:], g_sel[:, 512:1024]).then_inc(T.step("rows"), 1)
                    pe.wait_ge(*V.at(it, "k"))
                    for u in range(4):
                        h, t = u // 2, P * (u % 2)
                        kt = g_k[:, h, t:t + P]
                        mm(bank[3][:, P * u:P * u + P], kt, kt)
                        z = mm(bank[4][:, P * u:P * u + P], kt, g_q[:, h, t:t + P])
                    z.then_inc(T.step("kk"), 1)
                    pe.wait_ge(*A.at(it, "vfix"))
                    for h in range(2):
                        tr(bank[7][:, P * h:P * h + P], g_k[:, h, 0:P])
                    for t in range(NT):
                        for h in range(2):
                            z = tr(bank[0][:, 256 * t + P * h:256 * t + P * h + P], g_v[:, h, P * t:P * t + P])
                    z.then_inc(T.step("tr"), 1)
                    inverse(st, it, GDN_LEVELS, (1, 2, 3), g_c, g_x, g_xt, g_pm)
                    pe.wait_ge(*V.at(it, "xt64"))
                    pe.wait_ge(*A.at(it, "eg"))
                    for h in range(2):
                        z = mm(bank[5][:, P * h:P * h + P], v3(g_xt)[:, 2 * h, :], g_bv[:, P * h:P * h + P])
                    z.then_inc(T.step("v0"), 1)
                    pe.wait_ge(*A.at(it, "v0"))
                    for h in range(2):
                        z = mm(bank[6][:, P * h:P * h + P], g_kd[:, P * h:P * h + P], g_v0[:, P * h:P * h + P])
                    z.then_inc(T.step("s"), 1)
                    pe.wait_ge(*A.at(it, "s"))
                    for h in range(2):
                        z = mm(bank[7][:, P * h:P * h + P], g_k[:, h, P:2 * P], g_s[:, P * h:P * h + P])
                    z.then_inc(T.step("ks"), 1)
                    pe.wait_ge(*V.at(it, "r1"))
                    for h in range(2):
                        z = mm(bank[5][:, P * h:P * h + P], v3(g_xt)[:, 2 * h + 1, :], g_r1[:, P * h:P * h + P])
                    z.then_inc(T.step("v1"), 1)
                    pe.wait_ge(*A.at(it, "v1"))
                    for h in range(2):
                        o = 256 * h
                        mm(bank[4][:, o:o + P], g_v0[:, P * h:P * h + P], v3(g_qk)[:, 2 * h, :])
                        mm(bank[4][:, o + P:o + 256], g_s[:, P * h:P * h + P], g_qe[:, h, P:2 * P], stop=False)
                        z = mm(bank[4][:, o + P:o + 256], g_v1[:, P * h:P * h + P], v3(g_qk)[:, 2 * h + 1, :],
                               start=False)
                    z.then_inc(T.step("o"), 1)
                    pe.wait_ge(*A.at(it, "osq"))
                    mm(bank[6][:], ones[:], g_osq).then_inc(T.step("oss"), 1)

                st, it = s["lora"], l
                A, T = st["act"], st["pe"]
                pe.wait_ge(lora_in, 48 * (l + 1))
                pe.wait_ge(*A.at(it, "act"))
                for i in range(8):
                    c = slice(P * i, P * i + P)
                    for x, b, w, a_ in (("w", 3, lw_sb[0:64, c], mix[0:64, LT, :]),
                                        ("a", 4, lw_sb[64:128, c], mix[64:128, LT, :]),
                                        ("g", 5, lg_sb[:, c], mix[:, LT + 1, :])):
                        if i > 0:
                            pe.wait_ge(*A.at(it, f"{x}{i - 1}"))
                        mm(bank[b][:, 0:256], w, a_).then_inc(T.step(f"{x}{i}"), 1)
                st = s["rw"]
                A, V, T = st["act"], st["dve"], st["pe"]
                finished(pe, "lora", l)
                with pe.Fori(0, 8) as i:
                    it = i + 8 * l
                    pe.wait_ge(*V.before(it))
                    pe.wait_ge(*A.at(it, "sq"))
                    mm(bank[3][:, 0:256], halves[:], r_sq).then_inc(T.step("ss"), 1)
                    pe.wait_ge(*A.at(it, "fix"))
                    pe.wait_ge(*V.at(it, "kt"))
                    for n, src, b in ((0, r_bt, 4), (2, r_kt, 4), (0, r_v, 5)):
                        for t in range(NT):
                            z = tr(bank[b][:, P * (n + t):P * (n + t) + P], src[:, P * t:P * t + P])
                    z.then_inc(T.step("tr"), 1)
                    pe.wait_ge(*A.at(it, "ktz"))
                    pe.wait_ge(*V.at(it, "rt"))
                    for b, lhs, rhs in ((6, r_btz, r_kat), (7, r_ktz, r_kat), (0, r_btz, r_rt), (1, r_ktz, r_rt)):
                        for u in range(4):
                            h, t = u // 2, P * (u % 2)
                            z = mm(bank[b][:, P * u:P * u + P], lhs[:, 256 * h + t:256 * h + t + P], rhs[:, t:t + P])
                    z.then_inc(T.step("sc"), 1)
                    pe.wait_ge(*V.at(it, "rkm"))
                    mm(bank[3][:, 256:512], halves[:], r_bon).then_inc(T.step("bon"), 1)
                    pe.wait_ge(*V.at(it, "msk"))
                    pe.wait_ge(*A.at(it, "tok"))
                    for t in range(NT):
                        for h in range(2):
                            z = mm(bank[2][:, P * t + 64 * h:P * t + 64 * h + 64], v3(r_akv)[:, 2 * h + t, :],
                                   r_vtok[:, t, 64 * h:64 * h + 64])
                    z.then_inc(T.step("av"), 1)
                    inverse(st, it, RW_LEVELS, (4, 6, 7), r_c, r_x, r_xt, r_pm)
                    pe.wait_ge(*V.at(it, "xt32"))
                    for c in range(NCH):
                        t, o = c // 2, 64 * (c % 2)
                        if c > 0:
                            pe.wait_ge(*V.at(it, f"sb{c - 1}"))
                            mm(bank[4][:, P * t + o:P * t + o + 64], r_sb[:, c % 2, :], r_rt[:, P * t + o:P * t + o + 64],
                               start=(c == 1), stop=False, skip_group_check=True)
                            mm(bank[5][:, 0:128], r_kat[:, P * t:P * t + P], r_sb[:, c % 2, :])\
                                .then_inc(T.step(f"r{c}"), 1)
                            pe.wait_ge(*V.at(it, f"r{c}"))
                        for h in range(2):
                            rhs = r_av[:, 0, :] if c == 0 else r_r
                            z = mm(bank[2][:, 64 * h:64 * h + 64], v3(r_xt)[:, 2 * h + t, :],
                                   rhs[:, 64 * h:64 * h + 64])
                        z.then_inc(T.step(f"u{c}"), 1)
                        pe.wait_ge(*A.at(it, f"u{c}"))
                        if c < NCH - 1:
                            mm(bank[1][:, 0:128], r_btok[o:o + 64, t, :], r_un[o:o + 64, t, :], stop=False)
                            mm(bank[1][:, 0:128], r_ktok[o:o + 64, t, :], r_vtok[o:o + 64, t, :], start=False)\
                                .then_inc(T.step(f"s{c}"), 1)
                    for t in range(NT):
                        for h in range(2):
                            dst = bank[4][64 * h:64 * h + 64, P * t:P * t + P]
                            mm(dst, r_un[:, t, 64 * h:64 * h + 64], v3(r_arb)[:, 2 * h + t, :], start=False, stop=False,
                               skip_group_check=True)
                            z = mm(dst, r_vtok[:, t, 64 * h:64 * h + 64], v3(r_ark)[:, 2 * h + t, :], start=False,
                                   stop=True, skip_group_check=True)
                    z.then_inc(T.step("y"), 1)
                    pe.wait_ge(*A.at(it, "yc"))
                    mm(bank[3][:, 0:256], halves[:], r_e1).then_inc(T.step("mean"), 1)
                    pe.wait_ge(*A.at(it, "ysq"))
                    mm(bank[3][:, 256:512], halves[:], r_e2).then_inc(T.step("var"), 1)

                finished(pe, "rw", l)
                for b in range(4):
                    pe.wait_ge(y_split, 4 * l + b + 1)
                    if b == 3:
                        for j in range(OUT_TILES):
                            product(bank[(b_out[l] + j) % 3][:, 0:256], t_out[l] + j, 0, y_hi, y_lo,
                                    free=b_out[l] + j + 1)
                        break
                    for n in range(4):
                        for j in range(4):
                            k = 16 * b + 4 * n + j
                            hi, lo = (h_hi, h_lo) if j < 2 else (y_hi, y_lo)
                            product(bank[(b_mrg[l] + k) % 3][:, 0:256], t_mrg[l] + k, 0, hi, lo,
                                    free=b_mrg[l] + k + 1)

                norm("norm2", l)
                if l % 2 == 1:
                    st, it = s["route"], l // 2
                    A, V, T = st["act"], st["dve"], st["pe"]
                    pe.wait_ge(*s["norm2"]["dve"].at(l, "h"))
                    pe.wait_ge(*st["dve"].before(it))
                    pe.wait_ge(router_in, 16 * (it + 1))
                    for t in range(NT):
                        for k in range(KT):
                            z = mm(bank[4][:, 8 * t:8 * t + 8], hf[:, k, P * t:P * t + P], q_w[:, k, :],
                                   start=(k == 0), stop=(k == KT - 1))
                    z.then_inc(T.step("mm"), 1)
                    pe.wait_ge(*V.at(it, "c1"))
                    for t in range(NT):
                        z = tr(bank[5][0:8, P * t:P * t + P], q_c[:, t, :])
                    z.then_inc(T.step("tr"), 1)
                    pe.wait_ge(*V.at(it, "sel"))
                    for e in range(N_EXP):
                        z = mm(bank[4 + e // 2][:, 256 * (e % 2):256 * (e % 2) + 256], ones[0:8, :], q_sel[:, e, :])
                    z.then_inc(T.step("rows"), 1)
                    pe.wait_ge(*V.at(it, "cb"))
                pe.wait_ge(*s["norm2"]["dve"].at(l, "lo"))
                pe.wait_ge(bank_free, 3 + b_out[l] + OUT_TILES)
                with pe.Fori(0, FI * (1 if l % 2 == 0 else N_EXP)) as i:
                    it = i + f_it[l]
                    for j in range(4):
                        product(bank[j][:, 0:256], t_ffn[l] + j, i, h_hi, h_lo)
                    for j in range(2):
                        base = t_ffn[l] + 4 + j
                        pe.wait_ge(lo_done, i * 6 + (base + 1))
                        pe.wait_ge(act_ready, it * 2 + (j + 1))
                        if j == 0:
                            pe.wait_ge(down_free, it + 1)
                        for k in range(KT):
                            dst = bank[4 + k // 2][:, 256 * (k % 2):256 * (k % 2) + 256]
                            wh, wl = w_hi[:, base % 3, k, :], w_lo[:, base % 3, k, :]
                            mm(dst, wh, y_hi[:, j, :], start=(j == 0 and k % 2 == 0), stop=False, skip_group_check=True)
                            mm(dst, wh, y_lo[:, j, :], start=False, stop=False, skip_group_check=True)
                            z = mm(dst, wl, y_hi[:, j, :], start=False, stop=(j == 1), skip_group_check=True)
                        z.then_inc(slot_free, 1)
            norm("normf", 0)
            T = s["xout"]["pe"]
            pe.wait_ge(*s["normf"]["dve"].at(0, "h"))
            for t in range(NT):
                for k in range(KT):
                    z = tr(bank[4 + 2 * t + k // 4][:, P * (k % 4):P * (k % 4) + P], hf[:, k, P * t:P * t + P])
                z.then_inc(T.step(f"t{t}"), 1)

        @block.vector
        def _(dve):
            v = nc.vector

            def column(name, n=0):
                return pcol[:, bass.ds(n + PCOL[name], 1)] if not isinstance(n, int) \
                    else pcol[:, PCOL[name] + n:PCOL[name] + n + 1]

            def norm(ph, l, weight):
                st, it = s[ph], (l if ph != "normf" else 0)
                A, V, T = st["act"], st["dve"], st["pe"]
                dve.wait_ge(*T.at(it, "ss"))
                v.tensor_scalar(nv, bank[3][:, 0:256], 1.0 / D_MODEL, EPS, ALU.mult, ALU.add).then_inc(V.step("var"), 1)
                dve.wait_ge(*A.at(it, "rs"))
                for k in range(KT):
                    z = v.scalar_tensor_tensor(out=hf[:, k, :], in0=xres[:, k, :], scalar=column(weight, k), in1=nr,
                                               op0=ALU.mult, op1=ALU.mult)
                z.then_inc(V.step("h"), 1)
                if ph != "normf":
                    dve.wait_ge(*A.at(it, "hi"))
                    v.tensor_tensor(h_lo[:], hf, h_hi[:].bitcast(F32), ALU.subtract).then_inc(V.step("lo"), 1)

            def inverse(st, it, levels, banks, mt, c, x, xt):
                A, V, T = st["act"], st["dve"], st["pe"]
                v.tensor_tensor(v3(c), v3(mt), over(level[:, 0, :], 4), ALU.mult).then_inc(V.step("c1"), 1)
                dve.wait_ge(*V.at(it, "c1"))
                v.tensor_tensor(v3(xt), over(ident[:], 4), v3(c), ALU.subtract).then_inc(V.step("xt1"), 1)
                for n, b in enumerate(levels[1:]):
                    if n == 0:
                        dve.wait_ge(*V.at(it, "xt1"))
                    else:
                        dve.wait_ge(*T.at(it, f"p{levels[n]}"))
                    v.tensor_tensor(v3(c), v3(mt), over(level[:, n + 1, :], 4), ALU.mult).then_inc(V.step(f"c{b}"), 1)
                    dve.wait_ge(*T.at(it, f"q{b}"))
                    if b != levels[-1]:
                        v.tensor_tensor(x, x, bank[banks[1]][:], ALU.subtract).then_inc(V.step(f"x{b}"), 1)
                    v.tensor_tensor(xt, xt, bank[banks[2]][:], ALU.subtract).then_inc(V.step(f"xt{b}"), 1)

            V, T = s["xin"]["dve"], s["xin"]["pe"]
            for t in range(NT):
                dve.wait_ge(*T.at(0, f"t{t}"))
                for q in range(2):
                    z = v.tensor_copy(xres[:, 4 * q:4 * q + 4, P * t:P * t + P], v3(bank[4 + 2 * t + q][:]))
                z.then_inc(V.step(f"c{t}"), 1)
            products = 0

            for l in range(DEPTH):
                V, T = s["setup"]["dve"], s["setup"]["pe"]
                dve.wait_ge(*T.at(l, "t"))
                for b, n in enumerate((ROWS0, ROWS1, ROWS2)):
                    z = v.tensor_copy(pcol[:, P * b:P * b + n], bank[0][:, P * b:P * b + n])
                z.then_inc(V.step("pc"), 1)
                dve.wait_ge(*V.at(l, "pc"))
                r = PCOL["rwkv_mu"]
                v.tensor_scalar(one_mu[:], pcol[:, r:r + 26], -1.0, 1.0, ALU.mult, ALU.add).then_inc(V.step("mu1"), 1)
                for h in range(2):
                    o = slice(64 * h, 64 * h + 64)
                    v.tensor_copy(dskip[o, :], dheads[o, :].rearrange("p (n a) -> p n a", a=2)[:, :, h])
                r = PCOL["rwkv_k_a"]
                v.tensor_scalar(one_ka[:], pcol[:, r:r + 8], -1.0, 1.0, ALU.mult, ALU.add).then_inc(V.step("ka1"), 1)
                norm("norm1", l, "attn_norm_w")

                st, it = s["scal"], l
                A, V, T = st["act"], st["dve"], st["pe"]
                dve.wait_ge(*A.at(it, "aexp"))
                v.tensor_scalar(nha[:], nha[:], -1.0, None, ALU.mult).then_inc(V.step("neg"), 1)
                dve.wait_ge(*T.at(it, "mm"))
                v.tensor_scalar(sxb, bank[4][0:96, 0:256], hb[:, 0:1], None, ALU.add).then_inc(V.step("xb"), 1)
                dve.wait_ge(*V.at(it, "xb"))
                v.scalar_tensor_tensor(out=sab, in0=sxb, scalar=-1.0, in1=sxb, op0=ALU.mult, op1=ALU.max)\
                    .then_inc(V.step("abs"), 1)
                dve.wait_ge(*A.at(it, "ln"))
                v.scalar_tensor_tensor(out=ssp, in0=sxb, scalar=0.0, in1=sln, op0=ALU.max, op1=ALU.add)\
                    .then_inc(V.step("sp"), 1)
                dve.wait_ge(*V.at(it, "sp"))
                v.tensor_scalar(sad, ssp, nha[:, 0:1], None, ALU.mult).then_inc(V.step("ad"), 1)
                v.tensor_tensor(sd, sxb, ssp, ALU.subtract).then_inc(V.step("d"), 1)
                dve.wait_ge(*V.at(it, "ad"))
                v.tensor_copy(srow[96:112, :], ssp[0:16, :])
                v.tensor_tensor_scan(srow[0:16, :], ones[0:16, 0:1].broadcast_to([16, SEQ]), sad[0:16, :], 0.0,
                                     ALU.mult, ALU.add)
                for t in range(NT):
                    c = slice(P * t, P * t + P)
                    z = v.tensor_tensor_scan(srow[32:40, c], ones[32:40, :], sad[32:40, c], 0.0, ALU.mult, ALU.add)
                z.then_inc(V.step("scan"), 1)
                dve.wait_ge(*T.at(it, "tr"))
                v.tensor_copy(scol[:], v3(bank[5][:, 0:256])).then_inc(V.step("tc"), 1)
                dve.wait_ge(*A.at(it, "eg"))
                v.scalar_tensor_tensor(out=nbeta[:], in0=scol[:, :, 64:72], scalar=-1.0, in1=egc[:],
                                       op0=ALU.mult, op1=ALU.mult).then_inc(V.step("nb"), 1)

                def conv(j, i):
                    n = i * 6 + j
                    src, dst = bank[(b_in[l] + j) % 3][:, 0:256], mix[:, n, :]
                    dve.wait_ge(slot_free, i * 6 + (3 + t_in[l] + j + 1))
                    z = v.tensor_scalar(dst, src, column("conv_w3", n), column("conv_b", n), ALU.mult, ALU.add)
                    z.then_inc(conv_link, 1)
                    for k in (1, 2, 3):
                        dve.wait_ge(conv_link, i * 18 + (l * 3 * N_CONV + 3 * j + k))
                        z = v.scalar_tensor_tensor(out=mix[:, n, k:], in0=src[:, 0:SEQ - k],
                                                   scalar=column(f"conv_w{3 - k}", n), in1=mix[:, n, k:],
                                                   op0=ALU.mult, op1=ALU.add)
                        z.then_inc(conv_link if k < 3 else bank_free, 1)

                def shift(j, i, base, n, dst):
                    src = bank[(b_in[l] + base + j) % 3][:, 0:256]
                    dve.wait_ge(slot_free, i * 6 + (3 + t_in[l] + base + j + 1))
                    v.tensor_scalar(mix[:, dst, :], src, one_mu[:, bass.ds(n, 1)], None, ALU.mult)\
                        .then_inc(shift_link, 1)
                    dve.wait_ge(shift_link, (n - 24 + 1 if isinstance(n, int) else n + 3) + 26 * l)
                    v.scalar_tensor_tensor(out=mix[:, dst, 1:], in0=src[:, 0:SEQ - 1], scalar=column("rwkv_mu", n),
                                           in1=mix[:, dst, 1:], op0=ALU.mult, op1=ALU.add).then_inc(bank_free, 1)

                dve.wait_ge(*T.at(it, "tr"))
                dve.wait_ge(*V.at(it, "sp"))
                dve.wait_ge(*s["norm1"]["dve"].at(l, "lo"))
                with dve.Fori(0, N_CONV // 6) as i:
                    for j in range(6):
                        conv(j, i)
                for j in range(16):
                    n = N_CONV + j
                    dve.wait_ge(slot_free, 3 + t_in[l] + n + 1)
                    v.tensor_copy(mix[:, ZT + j, :], bank[(b_in[l] + n) % 3][:, 0:256]).then_inc(bank_free, 1)
                for j in range(2):
                    shift(j, 0, N_CONV + 16, 24 + j, LT + j)
                with dve.Fori(0, 4) as i:
                    for j in range(6):
                        shift(j, i, N_CONV + 18, i * 6 + j, i * 6 + (RT + j))

                dve.wait_ge(*s["ssdg"]["pe"].at(l, "g"))
                for g in range(2):
                    z = v.tensor_tensor(d_g[:, g, :], bank[4 + g][:, 0:384], flat(tri[:]), ALU.mult)
                z.then_inc(s["ssdg"]["dve"].step("g"), 1)
                st = s["ssd"]
                A, V, T = st["act"], st["dve"], st["pe"]
                finished(dve, "ssdg", l)
                for g in range(2):
                    with dve.Fori(0, 4) as i:
                        n = i + 4 * g
                        it = n + 8 * l
                        dve.wait_ge(*T.before(it))
                        dve.wait_ge(*V.before(it))
                        for h in range(2):
                            z = v.tensor_scalar(d_sel[:, 256 * h:256 * h + 256], srow[:],
                                                ident[:, bass.ds(n * 2 + h, 1)], None, ALU.mult)
                        z.then_inc(V.step("sel"), 1)
                        dve.wait_ge(*T.at(it, "rows"))
                        for h in range(2):
                            for t in range(NT):
                                o = 384 * h + 256 * t
                                z = v.tensor_scalar(d_diff[:, o:o + 256 - P * t],
                                                    bank[3][:, 256 * h + P * t:256 * h + 256],
                                                    scol[:, t, bass.ds(n * 2 + h, 1)], 0.0, ALU.subtract, ALU.min)
                        z.then_inc(V.step("diff"), 1)
                        dve.wait_ge(*T.at(it, "xt"))
                        for t in range(NT):
                            for h in range(2):
                                o = P * t + 64 * h
                                z = v.tensor_scalar(d_xdt[:, o:o + 64], bank[4][:, o:o + 64],
                                                    scol[:, t, bass.ds(n * 2 + (96 + h), 1)], None, ALU.mult)
                        z.then_inc(V.step("xdt"), 1)
                        dve.wait_ge(*A.at(it, "exp"))
                        v.tensor_tensor(v3(d_p, 384), v3(d_exp, 384), over(d_g[:, g, :], 2), ALU.mult)\
                            .then_inc(V.step("p"), 1)
                        dve.wait_ge(*T.at(it, "y"))
                        v.scalar_tensor_tensor(out=d_y, in0=d_x, scalar=dskip[:, bass.ds(n, 1)],
                                               in1=bank[5][:, 0:256], op0=ALU.mult, op1=ALU.add)\
                            .then_inc(V.step("y"), 1)
                        dve.wait_ge(*V.at(it, "y"))
                        v.tensor_tensor(mix[:, n + ZT, :], d_y, mix[:, n + ZT, :], ALU.mult).then_inc(V.step("yz"), 1)
                st = s["ssdn"]
                A, V, T = st["act"], st["dve"], st["pe"]
                for g in range(2):
                    it = 2 * l + g
                    dve.wait_ge(*T.at(it, "ss"))
                    dve.wait_ge(*V.before(it))
                    v.tensor_scalar(d_v, bank[6][:, 0:256], 1.0 / 512, EPS, ALU.mult, ALU.add)\
                        .then_inc(V.step("var"), 1)
                    dve.wait_ge(*A.at(it, "rs"))
                    for k in range(4):
                        n = ZT + 4 * g + k
                        z = v.scalar_tensor_tensor(out=mix[:, n, :], in0=mix[:, n, :],
                                                   scalar=column("ssm_norm_w", 4 * g + k), in1=d_r,
                                                   op0=ALU.mult, op1=ALU.mult)
                    z.then_inc(V.step("y"), 1)

                st = s["gdn"]
                A, V, T = st["act"], st["dve"], st["pe"]
                finished(dve, "ssdn", l)
                with dve.Fori(0, 4) as i:
                    it = i + 4 * l
                    dve.wait_ge(*T.before(it))
                    dve.wait_ge(*A.before(it))
                    dve.wait_ge(*V.before(it))
                    for r, o in ((32, 0), (64, 512)):
                        for h in range(2):
                            z = v.tensor_scalar(g_sel[:, o + 256 * h:o + 256 * h + 256], srow[:],
                                                ident[:, bass.ds(i * 2 + (r + h), 1)], None, ALU.mult)
                    z.then_inc(V.step("sel"), 1)
                    dve.wait_ge(*T.at(it, "ss"))
                    for n in range(2):
                        z = v.tensor_scalar(g_rs[:, 512 * n:512 * n + 512], bank[3 + n][:], 1e-6, None, ALU.add)
                    z.then_inc(V.step("eps"), 1)
                    dve.wait_ge(*A.at(it, "rs"))
                    v.scalar_tensor_tensor(out=flat(g_q), in0=flat(mix[:, bass.ds(i * 2 + QT, 2), :]),
                                           scalar=GDN_D ** -0.5, in1=g_rs[:, 0:512], op0=ALU.mult, op1=ALU.mult)\
                        .then_inc(V.step("q"), 1)
                    v.tensor_tensor(flat(g_k), flat(mix[:, bass.ds(i * 2 + KTL, 2), :]), g_rs[:, 512:1024], ALU.mult)\
                        .then_inc(V.step("k"), 1)
                    dve.wait_ge(*T.at(it, "rows"))
                    for h in range(2):
                        for t in range(NT):
                            z = v.tensor_scalar(g_e[:, h, P * t:P * t + P],
                                                bank[5][:, 256 * h + P * t:256 * h + P * t + P],
                                                scol[:, t, bass.ds(i * 2 + (32 + h), 1)], 0.0, ALU.subtract, ALU.min)
                    z.then_inc(V.step("diff"), 1)
                    dve.wait_ge(*T.at(it, "kk"))
                    dve.wait_ge(*A.at(it, "exp"))
                    v.tensor_tensor(g_mt, flat(g_e), bank[3][:], ALU.mult).then_inc(V.step("mt0"), 1)
                    dve.wait_ge(*V.at(it, "mt0"))
                    v.tensor_tensor(g_mt, g_mt, bank[6][:], ALU.mult).then_inc(V.step("mt"), 1)
                    v.tensor_tensor(g_qk, flat(g_e), bank[4][:], ALU.mult).then_inc(V.step("qkm0"), 1)
                    dve.wait_ge(*V.at(it, "qkm0"))
                    v.tensor_tensor(v3(g_qk), v3(g_qk), over(tri[:, 0, :], 4), ALU.mult).then_inc(V.step("qkm"), 1)
                    dve.wait_ge(*T.at(it, "tr"))
                    for h in range(2):
                        z = v.tensor_scalar(g_kd[:, P * h:P * h + P], bank[7][:, P * h:P * h + P],
                                            g_e[:, h, P - 1:P], None, ALU.mult)
                    z.then_inc(V.step("kdec"), 1)
                    for t in range(NT):
                        for h in range(2):
                            o = 256 * t + P * h
                            z = v.tensor_scalar(g_bv[:, o:o + P], bank[0][:, o:o + P],
                                                scol[:, t, bass.ds(i * 2 + (64 + h), 1)], None, ALU.mult)
                    z.then_inc(V.step("bv"), 1)
                    dve.wait_ge(*A.at(it, "eg"))
                    v.tensor_tensor(flat(g_qe), flat(g_q), g_eg, ALU.mult).then_inc(V.step("qe"), 1)
                    inverse(st, it, GDN_LEVELS, (1, 2, 3), g_mt, g_c, g_x, g_xt)
                    dve.wait_ge(*T.at(it, "ks"))
                    for h in range(2):
                        z = v.scalar_tensor_tensor(out=g_r1[:, P * h:P * h + P], in0=bank[7][:, P * h:P * h + P],
                                                   scalar=nbeta[:, 1, bass.ds(i * 2 + h, 1)],
                                                   in1=g_bv[:, 256 + P * h:256 + P * h + P], op0=ALU.mult, op1=ALU.add)
                    z.then_inc(V.step("r1"), 1)
                    dve.wait_ge(*T.at(it, "oss"))
                    v.tensor_scalar(g_ov, bank[6][:], 1.0 / GDN_D, EPS, ALU.mult, ALU.add).then_inc(V.step("oeps"), 1)
                    dve.wait_ge(*A.at(it, "ors"))
                    v.scalar_tensor_tensor(out=flat(g_o), in0=flat(g_o), scalar=column("gdn_norm_w"), in1=g_ov,
                                           op0=ALU.mult, op1=ALU.mult).then_inc(V.step("on"), 1)
                    dve.wait_ge(*V.at(it, "on"))
                    z = flat(mix[:, bass.ds(i * 2 + ZGT, 2), :])
                    v.tensor_tensor(z, flat(g_o), z, ALU.mult).then_inc(V.step("oz"), 1)

                st = s["rw"]
                A, V, T = st["act"], st["dve"], st["pe"]
                finished(dve, "lora", l)
                with dve.Fori(0, 8) as i:
                    it = i + 8 * l
                    dve.wait_ge(*T.before(it))
                    dve.wait_ge(*A.before(it))
                    dve.wait_ge(*V.before(it))
                    v.tensor_scalar(r_lw, mix[:, i + SGW, :], DECAY, None, ALU.mult).then_inc(V.step("lw"), 1)
                    v.tensor_scalar(r_kk, mix[:, i + RKT, :], column("rwkv_k_k", i), None, ALU.mult)\
                        .then_inc(V.step("kk0"), 1)
                    dve.wait_ge(*V.at(it, "lw"))
                    for c in range(NCH):
                        k = slice(64 * c, 64 * c + 64)
                        z = v.tensor_tensor_scan(r_p[:, k], ones[:, 0:64], r_lw[:, k], 0.0, ALU.mult, ALU.add)
                    z.then_inc(V.step("scan"), 1)
                    dve.wait_ge(*V.at(it, "scan"))
                    v.tensor_scalar(r_c4, v3(r_p, 64)[:, :, 63], 0.5, None, ALU.mult).then_inc(V.step("mid"), 1)
                    dve.wait_ge(*V.at(it, "mid"))
                    c4 = r_c4.rearrange("p (n o) -> p n o", o=1).broadcast_to([P, NCH, 64])
                    v.tensor_tensor(v3(r_pc, 64), v3(r_p, 64), c4, ALU.subtract).then_inc(V.step("pc"), 1)
                    dve.wait_ge(*V.at(it, "pc"))
                    v.tensor_tensor(r_p0, r_pc, r_lw, ALU.subtract).then_inc(V.step("p0"), 1)
                    dve.wait_ge(*A.at(it, "e"))
                    v.tensor_tensor(r_ecc[:, 0:3], r_ec[:, 0:3], r_ec[:, 1:4], ALU.mult).then_inc(V.step("ecc"), 1)
                    dve.wait_ge(*T.at(it, "ss"))
                    v.tensor_scalar(r_rs, bank[3][:, 0:256], 1e-6, None, ALU.add).then_inc(V.step("eps"), 1)
                    dve.wait_ge(*A.at(it, "rs"))
                    v.tensor_tensor(r_kk, r_kk, r_rs, ALU.mult).then_inc(V.step("kk"), 1)
                    dve.wait_ge(*V.at(it, "kk"))
                    v.tensor_tensor(r_akk, r_kk, mix[:, i + AT, :], ALU.mult).then_inc(V.step("akk"), 1)
                    v.tensor_scalar(r_km, mix[:, i + AT, :], column("rwkv_k_a", i), one_ka[:, bass.ds(i, 1)],
                                    ALU.mult, ALU.add).then_inc(V.step("m"), 1)
                    dve.wait_ge(*V.at(it, "m"))
                    v.tensor_tensor(r_km, r_km, mix[:, i + RKT, :], ALU.mult).then_inc(V.step("km"), 1)
                    v.tensor_tensor(r_bt, r_akk, r_e2, ALU.mult).then_inc(V.step("bt"), 1)
                    dve.wait_ge(*V.at(it, "km"))
                    v.tensor_tensor(r_kt, r_km, r_e2, ALU.mult).then_inc(V.step("kt"), 1)
                    v.tensor_tensor(r_kat, r_kk, r_e0, ALU.mult).then_inc(V.step("kat"), 1)
                    v.tensor_tensor(r_rt, mix[:, i + RT, :], r_e1, ALU.mult).then_inc(V.step("rt"), 1)
                    v.tensor_scalar(r_bon, mix[:, i + RT, :], column("rwkv_r_k", i), None, ALU.mult)\
                        .then_inc(V.step("rkm0"), 1)
                    dve.wait_ge(*V.at(it, "rkm0"))
                    v.tensor_tensor(r_bon, r_bon, r_km, ALU.mult).then_inc(V.step("rkm"), 1)
                    dve.wait_ge(*T.at(it, "sc"))
                    v.tensor_copy(r_mt, bank[6][:])
                    v.tensor_tensor(v3(r_akv), v3(bank[7][:]), over(stri64[:], 4), ALU.mult)
                    v.tensor_tensor(v3(r_arb), v3(bank[0][:]), over(tri64[:], 4), ALU.mult)
                    v.tensor_tensor(v3(r_ark), v3(bank[1][:]), over(tri64[:], 4), ALU.mult).then_inc(V.step("msk"), 1)
                    dve.wait_ge(*T.at(it, "bon"))
                    v.tensor_tensor(r_bon, r_v, bank[3][:, 256:512], ALU.mult).then_inc(V.step("bon"), 1)
                    dve.wait_ge(*T.at(it, "av"))
                    v.tensor_copy(r_av, v3(bank[2][:, 0:256])).then_inc(V.step("av"), 1)
                    dve.wait_ge(*V.at(it, "msk"))
                    inverse(st, it, RW_LEVELS, (4, 6, 7), r_mt, r_c, r_x, r_xt)
                    for c in range(NCH - 1):
                        dve.wait_ge(*T.at(it, f"s{c}"))
                        e = r_ecc[:, c:c + 1]
                        if c == 0:
                            v.scalar_tensor_tensor(out=r_sb[:, 1, :], in0=bank[1][:, 0:128], scalar=e, in1=halves[:],
                                                   op0=ALU.mult, op1=ALU.mult).then_inc(V.step("sb0"), 1)
                        else:
                            new = r_sb[:, (c + 1) % 2, :]
                            v.scalar_tensor_tensor(out=new, in0=bank[1][:, 0:128], scalar=e, in1=halves[:],
                                                   op0=ALU.mult, op1=ALU.mult).then_inc(V.step(f"sa{c}"), 1)
                            dve.wait_ge(*V.at(it, f"sa{c}"))
                            v.scalar_tensor_tensor(out=new, in0=r_sb[:, c % 2, :], scalar=e, in1=new,
                                                   op0=ALU.mult, op1=ALU.add).then_inc(V.step(f"sb{c}"), 1)
                        dve.wait_ge(*T.at(it, f"r{c + 1}"))
                        v.tensor_tensor(r_r, r_av[:, (c + 1) // 2, :], bank[5][:, 0:128], ALU.add)\
                            .then_inc(V.step(f"r{c + 1}"), 1)
                    dve.wait_ge(*T.at(it, "mean"))
                    v.scalar_tensor_tensor(out=r_e0, in0=bank[3][:, 0:256], scalar=-1.0 / RW_D, in1=r_e1,
                                           op0=ALU.mult, op1=ALU.add).then_inc(V.step("yc"), 1)
                    dve.wait_ge(*T.at(it, "var"))
                    v.tensor_scalar(r_rs, bank[3][:, 256:512], 1.0 / RW_D, GN_EPS, ALU.mult, ALU.add)\
                        .then_inc(V.step("veps"), 1)
                    dve.wait_ge(*A.at(it, "yrs"))
                    v.tensor_tensor(r_e0, r_e0, r_rs, ALU.mult).then_inc(V.step("yn"), 1)
                    dve.wait_ge(*V.at(it, "yn"))
                    v.tensor_scalar(r_e0, r_e0, column("rwkv_ln_w", i), column("rwkv_ln_b", i), ALU.mult, ALU.add)\
                        .then_inc(V.step("yw"), 1)
                    dve.wait_ge(*V.at(it, "yw"))
                    v.tensor_tensor(r_e0, r_e0, r_bon, ALU.add).then_inc(V.step("yb"), 1)
                    dve.wait_ge(*V.at(it, "yb"))
                    v.tensor_tensor(mix[:, i + RT, :], r_e0, mix[:, i + GT, :], ALU.mult).then_inc(V.step("out"), 1)

                finished(dve, "rw", l)
                for b in range(4):
                    src = mix[:, y_of[b]:y_of[b] + 8, :] if b < 3 else merged
                    dve.wait_ge(y_hi_done, 4 * l + b + 1)
                    v.tensor_tensor(y_lo[:], src, y_hi[:].bitcast(F32), ALU.subtract).then_inc(y_split, 1)
                    if b == 3:
                        for j in range(OUT_TILES):
                            dve.wait_ge(slot_free, 3 + t_out[l] + j + 1)
                            v.tensor_tensor(xres[:, j, :], xres[:, j, :], bank[(b_out[l] + j) % 3][:, 0:256], ALU.add)\
                                .then_inc(bank_free, 1)
                        break
                    for n in range(4):
                        for j in range(4):
                            k = 16 * b + 4 * n + j
                            src = bank[(b_mrg[l] + k) % 3][:, 0:256]
                            dve.wait_ge(slot_free, 3 + t_mrg[l] + k + 1)
                            if j < 2:
                                if k >= 4:
                                    dve.wait_ge(bank_free, 3 + b_mrg[l] + k - 2 + 1)
                                v.tensor_copy(gate_sb[:, j, :], src).then_inc(bank_free, 1)
                                continue
                            m = merged[:, 2 * n + j - 2, :]
                            dve.wait_ge(gate_done, 24 * l + 8 * b + 2 * n + j - 1)
                            if b == 0:
                                v.tensor_tensor(m, gate_sb[:, j - 2, :], src, ALU.mult).then_inc(bank_free, 1)
                            else:
                                dve.wait_ge(bank_free, 3 + b_mrg[l] + k - 16 + 1)
                                products += 1
                                v.tensor_tensor(prod_sb[:, j - 2, :], gate_sb[:, j - 2, :], src, ALU.mult)\
                                    .then_inc(link, 1)
                                dve.wait_ge(link, products)
                                v.tensor_tensor(m, m, prod_sb[:, j - 2, :], ALU.add).then_inc(bank_free, 1)

                norm("norm2", l, "ffn_norm_w")
                if l % 2 == 1:
                    st, it = s["route"], l // 2
                    A, V, T = st["act"], st["dve"], st["pe"]
                    dve.wait_ge(*T.at(it, "mm"))
                    v.tensor_copy(q_l, v3(bank[4][:, 0:16], 8)).then_inc(V.step("lg"), 1)
                    dve.wait_ge(*V.at(it, "lg"))
                    for t in range(NT):
                        z = v.max(q_m[:, t, :], q_l[:, t, :])
                    z.then_inc(V.step("mx"), 1)
                    shape = [P, NT, 8, 8]
                    other = q_l.rearrange("p t (o f) -> p t o f", o=1).broadcast_to(shape)
                    own = q_l.rearrange("p t (e o) -> p t e o", o=1).broadcast_to(shape)
                    v.tensor_tensor(q_gt, other, own, ALU.is_gt).then_inc(V.step("gt"), 1)
                    v.tensor_tensor(q_eq, other, own, ALU.is_equal).then_inc(V.step("eq"), 1)
                    dve.wait_ge(*V.at(it, "eq"))
                    v.tensor_tensor(q_eq, q_eq, before[:].rearrange("p (o e) f -> p o e f", o=1).broadcast_to(shape),
                                    ALU.mult).then_inc(V.step("eqb"), 1)
                    dve.wait_ge(*V.at(it, "eqb"))
                    v.tensor_tensor(q_gt, q_gt, q_eq, ALU.add).then_inc(V.step("cnt"), 1)
                    dve.wait_ge(*V.at(it, "cnt"))
                    v.tensor_reduce(q_rank, q_gt, AX.X, ALU.add).then_inc(V.step("rank"), 1)
                    v.tensor_tensor(q_d, q_m[:, :, 1], q_m[:, :, 0], ALU.subtract).then_inc(V.step("d"), 1)
                    dve.wait_ge(*A.at(it, "e"))
                    v.tensor_scalar(q_1, q_e, 1.0, None, ALU.add).then_inc(V.step("p1"), 1)
                    dve.wait_ge(*V.at(it, "p1"))
                    v.reciprocal(q_p1, q_1).then_inc(V.step("p1r"), 1)
                    dve.wait_ge(*V.at(it, "p1r"))
                    v.tensor_tensor(q_p2, q_e, q_p1, ALU.mult).then_inc(V.step("p2"), 1)
                    dve.wait_ge(*V.at(it, "p2"))
                    for t in range(NT):
                        v.tensor_scalar(q_c0[:, t, :], q_rank[:, t, :], 0.0, q_p1[:, t:t + 1], ALU.is_equal, ALU.mult)
                        z = v.tensor_scalar(q_c1[:, t, :], q_rank[:, t, :], 1.0, q_p2[:, t:t + 1], ALU.is_equal,
                                            ALU.mult)
                    z.then_inc(V.step("c0"), 1)
                    dve.wait_ge(*V.at(it, "c0"))
                    v.tensor_tensor(q_c, q_c0, q_c1, ALU.add).then_inc(V.step("c1"), 1)
                    dve.wait_ge(*T.at(it, "tr"))
                    v.tensor_copy(q_cr, bank[5][0:8, 0:256]).then_inc(V.step("cr"), 1)
                    dve.wait_ge(*V.at(it, "cr"))
                    v.tensor_tensor(q_sel, over(q_cr, 8),
                                    ident[0:8, 0:8].rearrange("p (e o) -> p e o", o=1).broadcast_to([8, 8, 256]),
                                    ALU.mult).then_inc(V.step("sel"), 1)
                    dve.wait_ge(*T.at(it, "rows"))
                    for q in range(4):
                        z = v.tensor_copy(cb[:, 2 * q:2 * q + 2, :], v3(bank[4 + q][:], 256))
                    z.then_inc(V.step("cb"), 1)
                    dve.wait_ge(*V.at(it, "cb"))

                experts = 1 if l % 2 == 0 else N_EXP
                with dve.Fori(0, experts) as e:
                    with dve.Fori(0, FI) as i:
                        n = e * FI + i
                        it = n + f_it[l]
                        for j in range(2):
                            dve.wait_ge(sg_done, it * 2 + (j + 1))
                            dve.wait_ge(slot_free, n * 6 + (3 + t_ffn[l] + 2 + j + 1))
                            dve.wait_ge(act_ready, it * 2 + j)
                            v.tensor_tensor(f_act[:, j, :], f_sg[:, j, :], bank[2 + j][:, 0:256], ALU.mult)\
                                .then_inc(ffn_link, 1)
                            dve.wait_ge(ffn_link, it * 6 + (3 * j + 1))
                            if experts > 1:
                                z = v.tensor_tensor(f_act[:, j, :], f_act[:, j, :], cb[:, e, :], ALU.mult)
                            else:
                                z = v.tensor_copy(f_act[:, j, :], f_act[:, j, :])
                            z.then_inc(ffn_link, 1)
                            dve.wait_ge(ffn_link, it * 6 + (3 * j + 2))
                            if j == 0:
                                dve.wait_ge(slot_free, n * 6 + (3 + t_ffn[l]))
                            v.tensor_copy(y_hi[:, j, :], f_act[:, j, :]).then_inc(ffn_link, 1)
                            dve.wait_ge(ffn_link, it * 6 + (3 * j + 3))
                            v.tensor_tensor(y_lo[:, j, :], f_act[:, j, :], y_hi[:, j, :].bitcast(F32), ALU.subtract)\
                                .then_inc(act_ready, 1)
                        dve.wait_ge(slot_free, n * 6 + (3 + t_ffn[l] + 6))
                        dve.wait_ge(down_free, it + 1)
                        for q in range(4):
                            z = v.tensor_tensor(flat(xres[:, 2 * q:2 * q + 2, :]), flat(xres[:, 2 * q:2 * q + 2, :]),
                                                bank[4 + q][:], ALU.add)
                        z.then_inc(down_free, 1)
                dve.wait_ge(down_free, 1 + f_it[l] + FI * experts)
            norm("normf", 0, "final_norm_w")
            V, T = s["xout"]["dve"], s["xout"]["pe"]
            for t in range(NT):
                dve.wait_ge(*T.at(0, f"t{t}"))
                for q in range(2):
                    z = v.tensor_copy(v3(xtok[:, t, :])[:, 4 * q:4 * q + 4, :], v3(bank[4 + 2 * t + q][:]))
                z.then_inc(V.step(f"c{t}"), 1)


_INS = ['x', 'attn_norm_w', 'w_in', 'conv_w', 'conv_b', 'ssm_a_log', 'ssm_dt_bias', 'ssm_d', 'ssm_norm_w',
        'gdn_a_log', 'gdn_dt_bias', 'gdn_norm_w', 'rwkv_mu', 'rwkv_w0', 'rwkv_w2', 'rwkv_a0', 'rwkv_a2',
        'rwkv_g2', 'rwkv_k_k', 'rwkv_k_a', 'rwkv_r_k', 'rwkv_ln_w', 'rwkv_ln_b', 'proj_ssm', 'proj_gdn',
        'proj_rwkv', 'w_out', 'ffn_norm_w', 'dense_w_gate', 'dense_w_up', 'dense_w_down', 'moe_router',
        'moe_w_gate', 'moe_w_up', 'moe_w_down', 'final_norm_w']


def kernel(**inputs):
    import numpy as _np
    import concourse.bacc as _bacc
    from concourse import mybir as _mybir
    from concourse.bass_utils import run_bass_kernel_spmd as _run

    nc = _bacc.Bacc("TRN2", target_bir_lowering=False, num_devices=1)
    arrays, args = {}, []
    for name in _INS:
        a = _np.ascontiguousarray(inputs[name])
        arrays[f"in_{name}_dram"] = a
        args.append(nc.dram_tensor(f"in_{name}_dram", a.shape, _mybir.dt.from_np(a.dtype), kind="ExternalInput").ap())
    args.append(nc.dram_tensor("out_0_dram", (1, SEQ, D_MODEL), F32, kind="ExternalOutput").ap())
    trunk(nc, *args)
    r = _run(nc, [arrays], core_ids=[0])
    return r.results[0]["out_0_dram"]
```

```python
import math
from contextlib import ExitStack

import concourse.bass as bass
from concourse import mybir

F32 = mybir.dt.float32
F32R = mybir.dt.float32r
ALU = mybir.AluOpType
ACT = mybir.ActivationFunctionType
AX = mybir.AxisListType

P = 128
D_MODEL, SEQ, DEPTH = 1024, 256, 2
KT = D_MODEL // P
NT = SEQ // P
SSM_HEADS, SSM_P, SSM_GROUPS = 16, 64, 2
GDN_HEADS, GDN_D = 8, 128
RW_HEADS, RW_D, RW_CHUNK = 16, 64, 64
NCH = SEQ // RW_CHUNK
FFN, N_EXP = 2816, 8
FI = FFN // 256
EPS, GN_EPS = 1e-6, 64e-5
LN_EXP_SET, SILU_SET = 6, 18
DECAY = -math.exp(-0.5)

CONV_COL, Z_COL, DT_COL = 0, 4608, 5632
ZG_COL, AB_COL, RW_COL = 5648, 6672, 6688
LORA_COL, GATE_COL = RW_COL + 3072, RW_COL + 3328
XS, BT_, CT_, QT, KTL, VT, ZT, ZGT, LT, RT, RKT, RVT, MIX_TILES = 0, 8, 10, 12, 20, 28, 36, 44, 52, 54, 62, 70, 78
SGW, AT, GT = QT, KTL, VT
N_CONV = 36

PCOL, _rows = {}, 0
for _name, _n in (("attn_norm_w", 8), ("ffn_norm_w", 8), ("rwkv_mu", 26), ("rwkv_w0", 8), ("rwkv_a0", 8),
                  ("rwkv_k_k", 8), ("rwkv_k_a", 8), ("rwkv_r_k", 8), ("rwkv_ln_w", 8), ("rwkv_ln_b", 8),
                  ("ssm_norm_w", 8), ("gdn_norm_w", 1)):
    PCOL[_name] = _rows
    _rows += _n
ROWS0 = _rows
PCOL["conv_b"], PCOL["conv_w0"], PCOL["conv_w1"], PCOL["final_norm_w"] = P, P + 36, P + 72, P + 108
ROWS1 = 116
PCOL["conv_w2"], PCOL["conv_w3"] = 2 * P, 2 * P + 36
ROWS2 = 72

GROUPS = "AB"
LEVELS = (1, 2, 4, 8, 16, 32, 64)


class Scratch:
    pass


class Steps:

    def __init__(self, sem, names, iters):
        assert len(set(names)) == len(names), names
        self.sem, self.names, self.iters, self.next = sem, list(names), iters, 0

    def at(self, it, name, g=None):
        name = name if g is None else name + GROUPS[g]
        return self.sem, it * len(self.names) + (self.names.index(name) + 2)

    def before(self, it):
        return self.sem, it * len(self.names) + 1

    def step(self, name, g=None):
        name = name if g is None else name + GROUPS[g]
        assert self.names[self.next] == name, (self.names[self.next], name)
        self.next = (self.next + 1) % len(self.names)
        return self.sem


def both(*names):
    return [n + g for name in names for g in GROUPS for n in name.split()]


def inverse_steps(levels, pe_first, pe_mid, dve_mid, dve_late):
    pe, act, dve = both("x1t") + pe_first, both("x1"), both("c1", "xt1", "c2", *dve_mid)
    for n, b in enumerate(levels[1:]):
        pe += both(f"p{b}", *(pe_mid if n == 0 else []), f"q{b}")
        act += both(f"p{b}")
        dve += both(*[f"c{c}" for c in levels[n + 2:n + 3]], f"xt{b}", *(dve_late if n == 0 else []))
    return pe, act, dve


GDN_LEVELS, RW_LEVELS = LEVELS, LEVELS[:-1]
GDN_INV = inverse_steps(GDN_LEVELS, [], ["tr"], ["kdec bv"], ["qkm", "qe"])
RW_INV = inverse_steps(RW_LEVELS, ["scB"], ["bon av"], ["msk"], ["av", "bon"])
NORM = dict(pe=["ss"], act=["sq0", "sq", "ln", "rs", "hi0", "hi"], dve=["h0", "h", "lo0", "lo"])
PHASES = {
    "setup": (1, dict(pe=["t"], dve=["pc", "mu1", "ka1"], pool=["const"])),
    "xin": (1, dict(pe=["t0", "t1"], dve=["c0", "c1"])),
    "norm1": (1, NORM),
    "scal": (1, dict(pe=["mm", "tr"], act=["aexp", "e", "ln", "beta", "eg"],
                     dve=["neg", "xb", "abs", "sp", "ad", "d", "scan", "tc", "nb"])),
    "ssdg": (1, dict(pe=["g"], dve=["g"])),
    "ssd": (4, dict(pe=both("rows", "xt", "y"), act=both("fix", "exp"),
                    dve=both("sel", "diff", "xdt", "p", "y", "yz"))),
    "ssdn": (2, dict(pe=["ss"], act=["sq", "ln", "rs"], dve=["y"])),
    "gdn": (2, dict(pe=both("ss", "rows", "kk") + GDN_INV[0] + both("v0", "s", "ks", "v1", "o", "oss"),
                    act=both("sq", "ln rs", "vfix", "exp", "eg") + GDN_INV[1]
                    + both("v0", "s", "v1", "oc", "osq", "oln", "ors"),
                    dve=both("sel", "q k", "diff", "mt0 mt qkm0")
                    + GDN_INV[2] + both("r1", "on", "oz"))),
    "lora": (1, dict(pe=[x + str(i) for i in range(8) for x in "wag"],
                     act=["act"] + [x + str(i) for i in range(8) for x in "wag"])),
    "rw": (4, dict(pe=both("ss", "tr", "sc0") + ["scA"] + RW_INV[0]
                   + both(*[x + str(c) for c in range(NCH) for x in "rus" if not (c == 0 and x == "r")
                            and not (c == NCH - 1 and x == "s")], "y", "yc", "var"),
                   act=both("sq", "e", "ln", "rs", "fix", "ktz", "btz", "tok", "mt") + RW_INV[1]
                   + both(*["u" + str(c) for c in range(NCH)], "y", "ysq", "yln", "yrs"),
                   dve=both("scan", "mid", "pc", "p0", "m", "km", "rkm", "ecc", "rt", "kt", "kk", "akk", "bt", "kat")
                   + RW_INV[2]
                   + both("sb0", "r1", "sa1", "sb1", "r2", "sa2", "sb2", "r3")
                   + both("yn", "yb", "out"))),
    "norm2": (1, NORM),
    "route": (1, dict(pe=["mm", "tr", "rows"], act=["e"],
                      dve=["lg", "mx", "gt", "eq", "eqb", "cnt", "rank", "d", "p1", "p1r", "p2", "c0", "c1", "cr",
                           "sel", "cb"])),
    "normf": (1, dict(pe=["ss"], act=["sq0", "sq", "ln", "rs"], dve=["h0", "h"])),
    "xout": (1, dict(pe=["t0", "t1"], dve=["c0", "c1"])),
}
SMALL = 16 * 26


def trunk(nc, x, attn_norm_w, w_in, conv_w, conv_b, ssm_a_log, ssm_dt_bias, ssm_d, ssm_norm_w,
          gdn_a_log, gdn_dt_bias, gdn_norm_w, rwkv_mu, rwkv_w0, rwkv_w2, rwkv_a0, rwkv_a2,
          rwkv_g2, rwkv_k_k, rwkv_k_a, rwkv_r_k, rwkv_ln_w, rwkv_ln_b, proj_ssm, proj_gdn,
          proj_rwkv, w_out, ffn_norm_w, dense_w_gate, dense_w_up, dense_w_down, moe_router,
          moe_w_gate, moe_w_up, moe_w_down, final_norm_w, out):
    ctx = ExitStack()
    with ctx:
        def sb(name, shape, dt=F32):
            return ctx.enter_context(nc.sbuf_tensor(name, shape, dt))

        def sem(name):
            return ctx.enter_context(nc.semaphore(name))

        xres = sb("xres", [P, KT, SEQ])
        mix = sb("mix", [P, MIX_TILES, SEQ])
        h_hi, h_lo = sb("h_hi", [P, KT, SEQ], F32R), sb("h_lo", [P, KT, SEQ], F32R)
        y_hi, y_lo = sb("y_hi", [P, KT, SEQ], F32R), sb("y_lo", [P, KT, SEQ], F32R)
        w_raw = sb("w_raw", [P, 3, 2048])
        w_hi, w_lo = sb("w_hi", [P, 3, KT, P], F32R), sb("w_lo", [P, 3, KT, P], F32R)
        ident, ones, halves = sb("ident", [P, P]), sb("ones", [P, P]), sb("halves", [P, P])
        tri, tri64, stri64 = sb("tri", [P, 3, P]), sb("tri64", [P, P]), sb("stri64", [P, P])
        level = sb("level", [P, len(LEVELS), P])
        before = sb("before", [P, 8, 8])
        pcol = sb("pcol", [P, 3 * P])
        one_mu, one_ka = sb("one_mu", [P, 26]), sb("one_ka", [P, 8])
        dskip, dheads = sb("dskip", [P, 8]), sb("dheads", [P, SSM_HEADS])
        srow, scol = sb("srow", [P, SEQ]), sb("scol", [P, NT, P])
        wsm = sb("wsm", [P, KT, 96])
        egc, nbeta = sb("egc", [P, NT, 8]), sb("nbeta", [P, NT, 8])
        nha, credit = sb("nha", [96, 1]), sb("credit", [1, 4])
        centre = sb("centre", [P, P])
        eps = sb("eps", [P, 2])
        hb, ha = sb("hb", [96, 1]), sb("ha", [96, 1])
        WORK = 6400
        work = sb("work", [P, WORK])

        def take(state, n, parts=P):
            a, state[0] = state[0], state[0] + n
            assert state[0] <= WORK, state
            return work[0:parts, a:a + n]

        bank = [ctx.enter_context(nc.psum_tensor(f"bank{i}", [P, 512], F32)) for i in range(8)]

        raw_in = [sem(f"raw_in{i}") for i in range(3)]
        hi_done, lo_done = sem("hi_done"), sem("lo_done")
        slot_free = sem("slot_free")
        bank_free = sem("bank_free")
        silu_done = sem("silu_done")
        act_ready = sem("act_ready")
        sg_done = sem("sg_done")
        down_free = sem("down_free")
        gate_done = sem("gate_done")
        y_split = sem("y_split")
        y_hi_done = sem("y_hi_done")
        small_in = sem("small_in")
        x_in, x_out, lora_in = sem("x_in"), sem("x_out"), sem("lora_in")
        link = sem("gate_products")
        conv_link, shift_link = sem("conv_taps"), sem("shift_first")
        ffn_link = sem("ffn_steps")
        pool_link = sem("const_steps")
        router_in = sem("router_in")
        s = {}
        for name, (iters, engines) in PHASES.items():
            s[name] = {e: Steps(sem(f"{name}_{e}"), names, iters) for e, names in engines.items() if names}

        def finished(eng, phase, layer):
            for st in s[phase].values():
                eng.wait_ge(*st.before((layer + 1) * st.iters))

        IN_TILES, MERGE_TILES, OUT_TILES, FFN_TILES = 78, 48, 8, 6 * FI
        t_in, t_mrg, t_out, t_ffn, at = [], [], [], [], 0
        for layer in range(DEPTH):
            for starts, n in ((t_in, IN_TILES), (t_mrg, MERGE_TILES), (t_out, OUT_TILES),
                              (t_ffn, FFN_TILES * (1 if layer % 2 == 0 else N_EXP))):
                starts.append(at)
                at += n
        b_in = [layer * (IN_TILES + MERGE_TILES + OUT_TILES) for layer in range(DEPTH)]
        b_mrg = [b + IN_TILES for b in b_in]
        b_out = [b + MERGE_TILES for b in b_mrg]
        f_it = [0, FI]
        s_in = [layer * 52 for layer in range(DEPTH)]

        def cols(w, c0):
            return w.rearrange("(k p) n -> p k n", p=P)[:, :, c0:c0 + 256] if isinstance(c0, int) \
                else w.rearrange("(k p) n -> p k n", p=P)[:, :, bass.ds(c0, 256)]

        def raw_view(base, kind):
            u = w_raw[:, (base // 2) % 3, :]
            if kind == "c":
                return u.rearrange("p (k n) -> p k n", n=256)[:, :, P * (base % 2):P * (base % 2) + P]
            return u.rearrange("p (j n c) -> p j n c", j=2, c=P)[:, base % 2]

        def ffn_kind(base, l):
            return "r" if base >= t_ffn[l] and (base - t_ffn[l]) % 6 >= 4 else "c"

        def v3(ap, c=P):
            return ap.rearrange("p (n c) -> p n c", c=c)

        def half(ap, n, side):
            return ap.rearrange("p (m two c) -> p m two c", two=2, c=n)[:, :, side, :]

        def flat(ap):
            return ap.rearrange("p n c -> p (n c)")

        hf = mix[:, 0:KT, :]
        nsq, nl, nr = mix[:, 8:16, :], mix[:, 17, :], mix[:, 18, :]
        prow = work[:, 2048:2048 + 3 * P].rearrange("p (b c) -> p b c", c=P)
        xtok = work[:, 0:2048].rearrange("p (t d) -> p t d", t=NT)

        a = [0]
        sxb, sab, se, sln, ssp, sad, sd = [take(a, SEQ)[0:96, :] for _ in range(7)]

        a, ssd = [0], []
        for g in range(2):
            b = Scratch()
            b.bank = bank[4 * g:4 * g + 3]
            b.sel, b.diff, b.p = take(a, 512), take(a, 768), take(a, 768)
            b.x, b.xdt, b.y = take(a, 256), take(a, 256), take(a, 256)
            ssd.append(b)
        a = [0]
        d_sq, d_l, d_r = take(a, 1024), take(a, 256), take(a, 256)
        d_g = mix[:, BT_:BT_ + 3, :].rearrange("p n c -> p (n c)").rearrange("p (g c) -> p g c", g=2)

        def arena(work_columns):
            return [w_raw[:, :, :].rearrange("p u n -> p (u n)"), flat(mix[:, 0:QT, :]),
                    work[:, 0:work_columns]], [0, 0, 0]

        def room(state, n):
            parts, used = state
            for q in range(3):
                if used[q] + n <= parts[q].shape[1]:
                    used[q] += n
                    return parts[q][:, used[q] - n:used[q]]
            assert False, "scratch is full"

        LORA = WORK - 2048
        memory = arena(LORA)
        gdn = []
        for g in range(2):
            b = Scratch()
            b.bank = bank[4 * g:4 * g + 4]
            b.inv = [b.bank[n] for n in (1, 2, 0)]
            b.sq, b.rs, b.sel = [room(memory, 1024) for _ in range(3)]
            b.x, b.xt = b.sq[:, 0:512], b.sq[:, 512:1024]
            b.c, b.pm = b.rs[:, 0:512], b.rs[:, 512:1024]
            b.osq, b.ov = b.c, b.pm
            b.kd, b.bv, b.v0 = b.sel[:, 0:256], b.sel[:, 256:768], b.sel[:, 768:1024]
            b.mt, b.qk = [room(memory, 512) for _ in range(2)]
            b.k, b.v, b.e = [v3(room(memory, 512), 256) for _ in range(3)]
            b.o = b.v
            b.qe, b.eg = [v3(room(memory, 256)) for _ in range(2)]
            b.v1, b.s = b.mt[:, 0:256], b.mt[:, 256:512]
            b.r1 = room(memory, 256)
            gdn.append(b)

        lw_sb, lg_sb = work[:, LORA:LORA + 1024], work[:, LORA + 1024:]

        memory = arena(WORK)
        rw = []
        for g in range(2):
            b = Scratch()
            b.bank = bank[4 * g:4 * g + 4]
            b.inv = [b.bank[n] for n in (0, 1, 2)]
            early = room(memory, 1536)
            b.p, b.pc, b.p0, b.sq, b.rs = [early[:, 256 * n:256 * n + 256] for n in range(5)]
            b.x, b.xt, b.pm = early[:, 0:512], early[:, 512:1024], early[:, 1024:1536]
            b.btz, b.ktz = room(memory, 512), room(memory, 512)
            b.akv = b.ktz
            b.mt = room(memory, 512)
            b.km, b.e0 = b.mt[:, 0:256], b.mt[:, 256:512]
            b.c = room(memory, 512)
            b.e1, b.e2 = b.c[:, 0:256], b.c[:, 256:512]
            b.tok = room(memory, 768)
            b.btok, b.ktok, b.vtok = [v3(b.tok[:, 256 * n:256 * n + 256]) for n in range(3)]
            b.arb, b.ark = room(memory, 512), room(memory, 512)
            b.kk, b.akk, b.bt, b.kt, b.kat, b.rt, b.bon, b.v = [room(memory, 256) for _ in range(8)]
            b.av, b.un, b.sb, b.r = v3(b.akk), v3(b.bt), v3(b.kt), b.kk[:, 0:128]
            b.c4, b.ec, b.ecc = [room(memory, NCH) for _ in range(3)]
            rw.append(b)

        merged = mix[:, 0:KT, :]
        gate_sb = mix[:, KT:KT + 2, :]
        prod_sb = mix[:, KT + 2:KT + 4, :]
        y_of = (ZT, ZGT, RT)
        f_sg = v3(work[:, 0:512], 256)
        f_act = v3(work[:, 512:1024], 256)
        f_acc = mix[:, 20:28, :]
        cb = mix[:, 28:36, :]
        rt = work[:, 1024:6400]
        q_w = v3(rt[:, 0:64], 8)
        q_l, q_m, q_rank, q_c0, q_c1, q_c = [v3(rt[:, 64 + 16 * n:80 + 16 * n], 8) for n in range(6)]
        q_gt, q_eq = [rt[:, 192 + 128 * n:320 + 128 * n].rearrange("p (t e f) -> p t e f", t=2, e=8) for n in range(2)]
        q_d, q_e, q_p1, q_1, q_p2 = [rt[:, 448 + 2 * n:450 + 2 * n] for n in range(5)]
        q_cr, q_sel = rt[0:8, 512:768], v3(rt[0:8, 768:768 + 2048], 256)
        identb = ident[:, :].rearrange("p (o c) -> p o c", o=1)

        def over(ap, n):
            return ap.rearrange("p (o c) -> p o c", o=1).broadcast_to([ap.shape[0], n, ap.shape[1]])

        block = ctx.enter_context(nc.Block())

        @block.sync
        def _(sp):
            def load(dst, src, arrived):
                sp.dma_start(dst, src).then_inc(arrived, 16)

            def unit(t, src, sub="c"):
                base, rest = t
                u = base // 2
                slot = w_raw[:, u % 3, :]
                if not isinstance(rest, int) or base + rest >= 6:
                    sp.wait_ge(lo_done, rest + (base - 4))
                load(slot.rearrange("p (k n) -> p k n", n=256 if sub == "c" else 1024), src, raw_in[u % 3])

            load(work[:, 0:2048].rearrange("p (t d) -> p t d", t=NT), x[0].rearrange("(t p) d -> p t d", p=P), x_in)

            def parameters(l):
                n = 0
                rows = work[:, 2048:2048 + 3 * P].rearrange("p (b c) -> p b c", c=P)
                for name, src, count in (
                        ("attn_norm_w", attn_norm_w[l], 8), ("ffn_norm_w", ffn_norm_w[l], 8),
                        ("rwkv_mu", rwkv_mu[l], 26), ("rwkv_w0", rwkv_w0[l], 8), ("rwkv_a0", rwkv_a0[l], 8),
                        ("rwkv_k_k", rwkv_k_k[l], 8), ("rwkv_k_a", rwkv_k_a[l], 8),
                        ("rwkv_ln_w", rwkv_ln_w[l], 8), ("rwkv_ln_b", rwkv_ln_b[l], 8),
                        ("ssm_norm_w", ssm_norm_w[l], 8), ("gdn_norm_w", gdn_norm_w[l], 1),
                        ("conv_b", conv_b[l], 36), ("conv_w0", conv_w[l, 0], 36), ("conv_w1", conv_w[l, 1], 36),
                        ("conv_w2", conv_w[l, 2], 36), ("conv_w3", conv_w[l, 3], 36),
                        ("final_norm_w", final_norm_w, 8)):
                    r = PCOL[name]
                    load(rows[r % P:r % P + count, r // P, :], src.rearrange("(n c) -> n c", c=P), small_in)
                    n += 1
                r = PCOL["rwkv_r_k"]
                load(rows[r:r + 8, 0, :], rwkv_r_k[l].rearrange("(n a) d -> n (a d)", a=2), small_in)
                load(dheads[:], ssm_d[l].rearrange("(o n) -> o n", o=1).broadcast_to([P, SSM_HEADS]), small_in)
                for c, src, m in ((0, DT_COL, 16), (32, AB_COL, 8), (64, AB_COL + 8, 8)):
                    load(wsm[:, :, c:c + m],
                         w_in[l].rearrange("(k p) n -> p k n", p=P)[:, :, src:src + m], small_in)
                load(hb[0:16, :], ssm_dt_bias[l].rearrange("(n o) -> n o", o=1), small_in)
                load(hb[32:40, :], gdn_dt_bias[l].rearrange("(n o) -> n o", o=1), small_in)
                load(ha[0:16, :], ssm_a_log[l].rearrange("(n o) -> n o", o=1), small_in)
                load(ha[32:40, :], gdn_a_log[l].rearrange("(n o) -> n o", o=1), small_in)
                return n + 9

            for l in range(DEPTH):
                if l == 0:
                    sp.wait_ge(*s["setup"]["pool"].at(0, "const"))
                    assert 16 * parameters(l) == SMALL
                wi = w_in[l]
                for k in range(3):
                    unit((t_in[l] + 2 * k, 0), cols(wi, CONV_COL + 256 * k))
                with sp.Fori(1, N_CONV // 6) as i:
                    for k in range(3):
                        unit((t_in[l] + 2 * k, i * 6), cols(wi, i * 768 + (CONV_COL + 256 * k)))
                t = t_in[l] + N_CONV
                for c in [Z_COL + 256 * i for i in range(4)] + [ZG_COL + 256 * i for i in range(4)] + [LORA_COL]:
                    unit((t, 0), cols(wi, c))
                    t += 2
                with sp.Fori(0, 4) as i:
                    for k in range(3):
                        unit((t + 2 * k, i * 6), cols(wi, i * 768 + (RW_COL + 256 * k)))
                for b, w in enumerate((proj_ssm, proj_gdn, proj_rwkv)):
                    for i in range(4):
                        unit((t_mrg[l] + 16 * b + 4 * i, 0), cols(wi, GATE_COL + 1024 * b + 256 * i))
                        if b == 0 and i == 0:
                            finished(sp, "ssdn", l)
                            load(lw_sb[0:64, :], rwkv_w2[l], lora_in)
                            load(lw_sb[64:128, :], rwkv_a2[l], lora_in)
                            load(lg_sb, rwkv_g2[l], lora_in)
                            finished(sp, "rw", l)
                        unit((t_mrg[l] + 16 * b + 4 * i + 2, 0), cols(w[l], 256 * i))
                for i in range(4):
                    unit((t_out[l] + 2 * i, 0), cols(w_out[l], 256 * i))
                if l + 1 < DEPTH:
                    parameters(l + 1)
                t = t_ffn[l]
                if l % 2 == 1:
                    finished(sp, "rw", l)
                    load(q_w, moe_router[l // 2].rearrange("(k p) e -> p k e", p=P), router_in)
                if l % 2 == 0:
                    with sp.Fori(0, FI) as i:
                        unit((t, i * 6), cols(dense_w_gate[l // 2], i * 256))
                        unit((t + 2, i * 6), cols(dense_w_up[l // 2], i * 256))
                        unit((t + 4, i * 6), dense_w_down[l // 2].rearrange("(i k p) n -> i p k n", k=2, p=P)[i], "r")
                else:
                    with sp.Fori(0, N_EXP) as e:
                        with sp.Fori(0, FI) as i:
                            it = (e * FI + i) * 6
                            unit((t, it), cols(moe_w_gate[l // 2][e], i * 256))
                            unit((t + 2, it), cols(moe_w_up[l // 2][e], i * 256))
                            unit((t + 4, it),
                                 moe_w_down[l // 2][e].rearrange("(i k p) n -> i p k n", k=2, p=P)[i], "r")
            sp.wait_ge(*s["xout"]["dve"].at(0, "c1"))
            sp.dma_start(out[0].rearrange("(t p) d -> p t d", p=P),
                         work[:, 0:2048].rearrange("p (t d) -> p t d", t=NT)).then_inc(x_out, 16)
            sp.wait_ge(x_out, 16)

        @block.gpsimd
        def _(pool):
            st = s["setup"]["pool"]
            for t in (ident, level, before, wsm, hb, ha, srow):
                nc.gpsimd.memset(t[:], 0.0)
            nc.gpsimd.memset(eps[:, 0:1], EPS)
            nc.gpsimd.memset(eps[:, 1:2], GN_EPS)
            for t in (ones, tri, halves):
                z = nc.gpsimd.memset(t[:], 1.0)
            z.then_inc(pool_link, 1)
            for steps in s.values():
                for st_ in steps.values():
                    pool.sem_inc(st_.sem, 1)
            for c, (free, n) in enumerate(((slot_free, 3), (bank_free, 3), (down_free, 1), (act_ready, 2))):
                nc.gpsimd.memset(credit[:, c:c + 1], 0.0).then_inc(free, n)
            pool.wait_ge(pool_link, 1)
            nc.gpsimd.affine_select(out=ident[:], in_=ident[:], compare_op=ALU.not_equal, fill=1.0, base=0,
                                    pattern=[[-1, P]], channel_multiplier=1)
            for n in (0, 2):
                nc.gpsimd.affine_select(out=tri[:, n, :], in_=tri[:, n, :], compare_op=ALU.is_ge, fill=0.0, base=0,
                                        pattern=[[1, P]], channel_multiplier=-1)
            nc.gpsimd.affine_select(out=halves[:, 0:64], in_=halves[:, 0:64], compare_op=ALU.is_ge, fill=0.0, base=63,
                                    pattern=[[0, 64]], channel_multiplier=-1)
            nc.gpsimd.affine_select(out=halves[:, 64:128], in_=halves[:, 64:128], compare_op=ALU.is_ge, fill=0.0,
                                    base=-64, pattern=[[0, 64]], channel_multiplier=1)
            for n, b in enumerate(LEVELS):
                v = level[:, n, :].rearrange("p (m two c) -> p m two c", two=2, c=b)[:, :, 1, :]
                one = nc.gpsimd.memset(v, 1.0)
            for e in range(1, 8):
                z = nc.gpsimd.memset(before[:, e, 0:e], 1.0)
            z.then_inc(pool_link, 1)
            pool.wait_ge(pool_link, 2)
            for n, b in enumerate(LEVELS):
                v = level[:, n, :].rearrange("p (m two c) -> p m two c", two=2, c=b)[:, :, 1, :]
                nc.gpsimd.affine_select(out=v, in_=v, compare_op=ALU.is_ge, fill=0.0, base=0,
                                        pattern=[[-2 * b, P // (2 * b)], [0, b]], channel_multiplier=1)
            z = nc.gpsimd.tensor_tensor(tri64[:], tri[:, 0, :], halves[:], ALU.mult)
            z.then_inc(pool_link, 1)
            pool.wait_ge(pool_link, 3)
            for n, b in enumerate(LEVELS):
                v = level[:, n, :].rearrange("p (m two c) -> p m two c", two=2, c=b)[:, :, 1, :]
                nc.gpsimd.affine_select(out=v, in_=v, compare_op=ALU.is_ge, fill=0.0, base=b - 1,
                                        pattern=[[2 * b, P // (2 * b)], [0, b]], channel_multiplier=-1)
            z = nc.gpsimd.tensor_tensor(stri64[:], tri64[:], ident[:], ALU.subtract)
            z.then_inc(st.step("const"), 1)

            def split_lo(base, i, kind):
                pool.wait_ge(hi_done, i * 6 + (base + 1))
                nc.gpsimd.tensor_tensor(w_lo[:, base % 3], raw_view(base, kind), w_hi[:, base % 3].bitcast(F32),
                                        ALU.subtract).then_inc(lo_done, 1)

            for l in range(DEPTH):
                with pool.Fori(0, IN_TILES // 6) as i:
                    for j in range(6):
                        split_lo(t_in[l] + j, i, "c")
                for t in range(t_mrg[l], t_ffn[l]):
                    split_lo(t, 0, "c")
                with pool.Fori(0, FI * (1 if l % 2 == 0 else N_EXP)) as i:
                    for j in range(6):
                        split_lo(t_ffn[l] + j, i, "c" if j < 4 else "r")

        @block.scalar
        def _(act):
            def split_hi(base, i, kind):
                u = base // 2
                act.wait_ge(raw_in[u % 3], i * 16 + 16 * (u // 3 + 1))
                act.wait_ge(slot_free, i * 6 + (base + 1))
                nc.scalar.activation(w_hi[:, base % 3], raw_view(base, kind), ACT.Copy).then_inc(hi_done, 1)

            def load_tables(table_set=LN_EXP_SET):
                act.add_instruction(mybir.InstLoadActFuncSet(
                    name=nc.get_next_instruction_name(), act_func_set_id=table_set,
                    engine=mybir.EngineType.Activation, ins=[], outs=[]))

            def norm(ph, l, first, rest, split=True):
                st, it = s[ph], (l if ph != "normf" else 0)
                A, V, T = st["act"], st["dve"], st["pe"]
                load_tables()
                act.wait_ge(*first)
                nc.scalar.activation(nsq[:, 0:4, :], xres[:, 0:4, :], ACT.Square).then_inc(A.step("sq0"), 1)
                act.wait_ge(*rest)
                nc.scalar.activation(nsq[:, 4:8, :], xres[:, 4:8, :], ACT.Square).then_inc(A.step("sq"), 1)
                act.wait_ge(*T.at(it, "ss"))
                nc.scalar.activation(nl, bank[3][:, 0:256], ACT.Ln, scale=1.0 / D_MODEL, bias=eps[:, 0:1])\
                    .then_inc(A.step("ln"), 1)
                act.wait_ge(*A.at(it, "ln"))
                nc.scalar.activation(nr, nl, ACT.Exp, scale=-0.5).then_inc(A.step("rs"), 1)
                if split:
                    for name, q, k in (("hi0", "h0", slice(0, 4)), ("hi", "h", slice(4, 8))):
                        act.wait_ge(*V.at(it, q))
                        nc.scalar.activation(h_hi[:, k, :], hf[:, k, :], ACT.Copy).then_inc(A.step(name), 1)

            def inverse(st, it, levels, groups):
                A, T = st["act"], st["pe"]
                for g, b in enumerate(groups):
                    act.wait_ge(*T.at(it, "x1t", g))
                    nc.scalar.activation(b.x, b.inv[0][:], ACT.Copy).then_inc(A.step("x1", g), 1)
                for n in levels[1:]:
                    for g, b in enumerate(groups):
                        act.wait_ge(*T.at(it, f"p{n}", g))
                        nc.scalar.activation(b.pm, b.inv[0][:], ACT.Copy).then_inc(A.step(f"p{n}", g), 1)

            for l in range(DEPTH):
                ready = s["xin"]["dve"].at(0, "c1") if l == 0 else (down_free, 1 + FI)
                norm("norm1", l, ready, ready)
                st, it = s["scal"], l
                A, V, T = st["act"], st["dve"], st["pe"]
                act.wait_ge(small_in, SMALL * (l + 1))
                nc.scalar.activation(nha[:], ha[:], ACT.Exp).then_inc(A.step("aexp"), 1)
                act.wait_ge(*V.at(it, "abs"))
                nc.scalar.activation(se, sab, ACT.Exp, scale=-1.0).then_inc(A.step("e"), 1)
                act.wait_ge(*A.at(it, "e"))
                nc.scalar.activation(sln, se, ACT.Ln, bias=1.0).then_inc(A.step("ln"), 1)
                act.wait_ge(*V.at(it, "d"))
                nc.scalar.activation(srow[64:72, :], sd[64:72, :], ACT.Exp).then_inc(A.step("beta"), 1)

                def silu(n, i, dst):
                    act.wait_ge(bank_free, i * 6 + (3 + b_in[l] + n + 1))
                    nc.scalar.activation(mix[:, dst, :], mix[:, dst, :], ACT.Silu).then_inc(silu_done, 1)

                if l == 0:
                    split_hi(0, 0, "c")
                    split_hi(1, 0, "c")
                load_tables(SILU_SET)
                for j in range(6):
                    split_hi(t_in[l] + j + 2, 0, "c")
                    if j > 0:
                        silu(j - 1, 0, j - 1)
                with act.Fori(1, N_CONV // 6) as i:
                    load_tables(SILU_SET)
                    for j in range(6):
                        split_hi(t_in[l] + j + 2, i, "c")
                        silu(j - 1, i, i * 6 + (j - 1))
                for j in range(18):
                    split_hi(t_in[l] + N_CONV + j + 2, 0, "c")
                    if j <= 16:
                        silu(N_CONV + j - 1, 0, ZT + j - 1 if j > 0 else N_CONV - 1)
                with act.Fori(0, 4) as i:
                    for j in range(6):
                        split_hi(t_in[l] + N_CONV + 18 + j + 2, i, "c")
                load_tables()
                act.wait_ge(*V.at(it, "tc"))
                nc.scalar.activation(egc[:], scol[:, :, 32:40], ACT.Exp).then_inc(A.step("eg"), 1)

                st = s["ssd"]
                A, V, T = st["act"], st["dve"], st["pe"]
                with act.Fori(0, 4) as i:
                    it = i + 4 * l
                    act.wait_ge(*T.before(it))
                    act.wait_ge(*V.before(it))
                    act.wait_ge(silu_done, s_in[l] + 52)
                    for g, b in enumerate(ssd):
                        nc.scalar.activation(b.x, mix[:, i + (XS + 4 * g), :], ACT.Copy).then_inc(A.step("fix", g), 1)
                    for g, b in enumerate(ssd):
                        act.wait_ge(*V.at(it, "diff", g))
                        nc.scalar.activation(b.diff, b.diff, ACT.Exp).then_inc(A.step("exp", g), 1)
                st = s["ssdn"]
                A, V, T = st["act"], st["dve"], st["pe"]
                finished(act, "ssd", l)
                for g in range(2):
                    it = 2 * l + g
                    act.wait_ge(*T.before(it))
                    nc.scalar.activation(v3(d_sq, 256), mix[:, ZT + 4 * g:ZT + 4 * g + 4, :], ACT.Square)\
                        .then_inc(A.step("sq"), 1)
                    act.wait_ge(*T.at(it, "ss"))
                    nc.scalar.activation(d_l, bank[6][:, 0:256], ACT.Ln, scale=1.0 / 512, bias=eps[:, 0:1])\
                        .then_inc(A.step("ln"), 1)
                    act.wait_ge(*A.at(it, "ln"))
                    nc.scalar.activation(d_r, d_l, ACT.Exp, scale=-0.5).then_inc(A.step("rs"), 1)

                st = s["gdn"]
                A, V, T = st["act"], st["dve"], st["pe"]
                finished(act, "ssdn", l)
                act.wait_ge(lo_done, t_mrg[l] + 2)
                with act.Fori(0, 2) as i:
                    it = i + 2 * l
                    act.wait_ge(*T.before(it))
                    act.wait_ge(*V.before(it))
                    for g, b in enumerate(gdn):
                        nc.scalar.activation(v3(b.sq[:, 0:512], 256), mix[:, bass.ds(i * 4 + (QT + 2 * g), 2), :],
                                             ACT.Square)
                        nc.scalar.activation(v3(b.sq[:, 512:1024], 256), mix[:, bass.ds(i * 4 + (KTL + 2 * g), 2), :],
                                             ACT.Square).then_inc(A.step("sq", g), 1)
                    for g, b in enumerate(gdn):
                        act.wait_ge(*T.at(it, "ss", g))
                        for n in range(2):
                            z = nc.scalar.activation(b.rs[:, 512 * n:512 * n + 512], b.bank[n][:], ACT.Ln,
                                                     bias=eps[:, 0:1])
                        z.then_inc(A.step("ln", g), 1)
                        act.wait_ge(*A.at(it, "ln", g))
                        nc.scalar.activation(b.rs, b.rs, ACT.Exp, scale=-0.5).then_inc(A.step("rs", g), 1)
                    for g, b in enumerate(gdn):
                        nc.scalar.activation(b.v, mix[:, bass.ds(i * 4 + (VT + 2 * g), 2), :], ACT.Copy)\
                            .then_inc(A.step("vfix", g), 1)
                    for g, b in enumerate(gdn):
                        act.wait_ge(*V.at(it, "diff", g))
                        nc.scalar.activation(b.e, b.e, ACT.Exp).then_inc(A.step("exp", g), 1)
                    for g, b in enumerate(gdn):
                        nc.scalar.activation(b.eg, v3(b.bank[2][:], 256)[:, :, P:2 * P], ACT.Exp)\
                            .then_inc(A.step("eg", g), 1)
                    inverse(st, it, GDN_LEVELS, gdn)
                    for name, n, dst in (("v0", 3, [b.v0 for b in gdn]), ("s", 1, [b.s for b in gdn]),
                                         ("v1", 3, [b.v1 for b in gdn])):
                        for g, b in enumerate(gdn):
                            act.wait_ge(*T.at(it, name, g))
                            nc.scalar.activation(dst[g], b.bank[n][:, 0:256], ACT.Copy).then_inc(A.step(name, g), 1)
                    for g, b in enumerate(gdn):
                        act.wait_ge(*T.at(it, "o", g))
                        nc.scalar.activation(flat(b.o), b.bank[2][:], ACT.Copy).then_inc(A.step("oc", g), 1)
                    for g, b in enumerate(gdn):
                        act.wait_ge(*A.at(it, "oc", g))
                        nc.scalar.activation(b.osq, flat(b.o), ACT.Square).then_inc(A.step("osq", g), 1)
                    for g, b in enumerate(gdn):
                        act.wait_ge(*T.at(it, "oss", g))
                        nc.scalar.activation(b.ov, b.bank[1][:], ACT.Ln, scale=1.0 / GDN_D, bias=eps[:, 0:1])\
                            .then_inc(A.step("oln", g), 1)
                    for g, b in enumerate(gdn):
                        act.wait_ge(*A.at(it, "oln", g))
                        nc.scalar.activation(b.ov, b.ov, ACT.Exp, scale=-0.5).then_inc(A.step("ors", g), 1)

                st, it = s["lora"], l
                A, T = st["act"], st["pe"]
                finished(act, "gdn", l)
                nc.scalar.activation(mix[:, LT + 1, :], mix[:, LT + 1, :], ACT.Sigmoid)
                nc.scalar.activation(mix[0:64, LT, :], mix[0:64, LT, :], ACT.Tanh).then_inc(A.step("act"), 1)
                for i in range(8):
                    for x, b, dst, bias in (("w", 0, SGW, "rwkv_w0"), ("a", 1, AT, "rwkv_a0"), ("g", 2, GT, None)):
                        act.wait_ge(*T.at(it, f"{x}{i}"))
                        if bias:
                            z = nc.scalar.activation(mix[:, dst + i, :], bank[b + 3 * (i % 2)][:, 0:256], ACT.Sigmoid,
                                                     bias=pcol[:, PCOL[bias] + i:PCOL[bias] + i + 1])
                        else:
                            z = nc.scalar.activation(mix[:, dst + i, :], bank[b + 3 * (i % 2)][:, 0:256], ACT.Copy)
                        z.then_inc(A.step(f"{x}{i}"), 1)

                st = s["rw"]
                A, V, T = st["act"], st["dve"], st["pe"]
                finished(act, "lora", l)
                load_tables()
                with act.Fori(0, 4) as i:
                    it = i + 4 * l
                    act.wait_ge(*T.before(it))
                    act.wait_ge(*V.before(it))
                    for g, b in enumerate(rw):
                        nc.scalar.activation(b.sq, mix[:, i * 2 + (RKT + g), :], ACT.Square,
                                             scale=pcol[:, bass.ds(i * 2 + (PCOL["rwkv_k_k"] + g), 1)])\
                            .then_inc(A.step("sq", g), 1)
                    for g, b in enumerate(rw):
                        act.wait_ge(*V.at(it, "p0", g))
                        nc.scalar.activation(b.e1, b.pc, ACT.Exp, scale=DECAY)
                        nc.scalar.activation(b.e2, b.pc, ACT.Exp, scale=-DECAY)
                        nc.scalar.activation(b.e0, b.p0, ACT.Exp, scale=DECAY)
                        nc.scalar.activation(b.ec, b.c4, ACT.Exp, scale=DECAY).then_inc(A.step("e", g), 1)
                    for g, b in enumerate(rw):
                        act.wait_ge(*T.at(it, "ss", g))
                        nc.scalar.activation(b.rs, b.bank[3][:, 0:256], ACT.Ln, bias=eps[:, 0:1])\
                            .then_inc(A.step("ln", g), 1)
                    for g, b in enumerate(rw):
                        act.wait_ge(*A.at(it, "ln", g))
                        nc.scalar.activation(b.rs, b.rs, ACT.Exp, scale=-0.5).then_inc(A.step("rs", g), 1)
                    for g, b in enumerate(rw):
                        nc.scalar.activation(b.v, mix[:, i * 2 + (RVT + g), :], ACT.Copy).then_inc(A.step("fix", g), 1)
                    for name, src, dst in (("kt", [b.kt for b in rw], [b.ktz for b in rw]),
                                           ("bt", [b.bt for b in rw], [b.btz for b in rw])):
                        for g in range(2):
                            act.wait_ge(*V.at(it, name, g))
                            for h in range(2):
                                z = nc.scalar.activation(dst[g][:, 256 * h:256 * h + 256], src[g], ACT.Copy,
                                                         scale=halves[:, 64 * h:64 * h + 1])
                            z.then_inc(A.step(name + "z", g), 1)
                    for g, b in enumerate(rw):
                        act.wait_ge(*T.at(it, "tr", g))
                        nc.scalar.activation(b.tok[:, 0:512], b.bank[2][:], ACT.Copy)
                        nc.scalar.activation(b.tok[:, 512:768], b.bank[3][:, 256:512], ACT.Copy)\
                            .then_inc(A.step("tok", g), 1)
                    for g, b in enumerate(rw):
                        act.wait_ge(*T.at(it, "sc0", g))
                        nc.scalar.activation(b.mt, b.bank[0][:], ACT.Copy).then_inc(A.step("mt", g), 1)
                    inverse(st, it, RW_LEVELS, rw)
                    for c in range(NCH):
                        t, o = c // 2, 64 * (c % 2)
                        for g, b in enumerate(rw):
                            act.wait_ge(*T.at(it, f"u{c}", g))
                            nc.scalar.activation(b.un[o:o + 64, t, :], b.bank[1][o:o + 64, 0:128], ACT.Copy,
                                                 scale=-1.0).then_inc(A.step(f"u{c}", g), 1)
                    for g, b in enumerate(rw):
                        act.wait_ge(*T.at(it, "y", g))
                        nc.scalar.activation(b.e1, b.bank[0][:, 0:256], ACT.Copy).then_inc(A.step("y", g), 1)
                    for g, b in enumerate(rw):
                        act.wait_ge(*T.at(it, "yc", g))
                        nc.scalar.activation(b.e2, b.bank[1][:, 0:256], ACT.Square).then_inc(A.step("ysq", g), 1)
                    for g, b in enumerate(rw):
                        act.wait_ge(*T.at(it, "var", g))
                        nc.scalar.activation(b.rs, b.bank[1][:, 256:512], ACT.Ln, scale=1.0 / RW_D, bias=eps[:, 1:2])\
                            .then_inc(A.step("yln", g), 1)
                    for g, b in enumerate(rw):
                        act.wait_ge(*A.at(it, "yln", g))
                        nc.scalar.activation(b.rs, b.rs, ACT.Exp, scale=-0.5).then_inc(A.step("yrs", g), 1)

                finished(act, "rw", l)
                for b in range(4):
                    src = mix[:, y_of[b]:y_of[b] + 8, :] if b < 3 else merged
                    if b > 0:
                        act.wait_ge(slot_free, 3 + t_mrg[l] + 16 * b)
                    if b == 3:
                        act.wait_ge(bank_free, 3 + b_out[l])
                    nc.scalar.activation(y_hi[:], src, ACT.Copy).then_inc(y_hi_done, 1)
                    if b == 3:
                        for j in range(OUT_TILES):
                            split_hi(t_out[l] + j + 2, 0, "c")
                        break
                    for n in range(4):
                        for j in range(4):
                            t = t_mrg[l] + 16 * b + 4 * n + j
                            split_hi(t + 2, 0, "c")
                            if j >= 2:
                                k = b_mrg[l] + 16 * b + 4 * n + j - 2
                                act.wait_ge(bank_free, 3 + k + 1)
                                nc.scalar.activation(gate_sb[:, j - 2, :], gate_sb[:, j - 2, :], ACT.Sigmoid)\
                                    .then_inc(gate_done, 1)

                norm("norm2", l, (bank_free, 3 + b_out[l] + 4), (bank_free, 3 + b_out[l] + OUT_TILES))

                def ffn(i, last=False, route=False):
                    it = i + f_it[l]
                    for j in range(6):
                        if j == 2 and route:
                            act.wait_ge(*s["route"]["dve"].at(l // 2, "d"))
                            nc.scalar.activation(q_e, q_d, ACT.Exp).then_inc(s["route"]["act"].step("e"), 1)
                        if not (last and j >= 4):
                            split_hi(t_ffn[l] + j + 2, i, ffn_kind(t_ffn[l] + j + 2, l) if j < 4 else "c")
                        if j in (2, 3):
                            k = j - 2
                            act.wait_ge(slot_free, i * 6 + (3 + t_ffn[l] + j - 2 + 1))
                            act.wait_ge(act_ready, it * 2 + 2)
                            nc.scalar.activation(f_sg[:, k, :], bank[k][:, 0:256], ACT.Silu).then_inc(sg_done, 1)

                n = FI * (1 if l % 2 == 0 else N_EXP)
                if l % 2 == 1:
                    ffn(0, route=True)
                with act.Fori(l % 2, n - 1) as i:
                    load_tables(SILU_SET)
                    ffn(i)
                ffn(n - 1, last=(l == DEPTH - 1))
            ready = (down_free, 1 + FI + FI * N_EXP)
            norm("normf", 0, ready, ready, split=False)

        @block.tensor
        def _(pe):
            def product(dst, base, i, hi, lo, free=None):
                pe.wait_ge(lo_done, i * 6 + (base + 1))
                if free is not None:
                    pe.wait_ge(bank_free, free)
                for k in range(KT):
                    wh, wl = w_hi[:, base % 3, k, :], w_lo[:, base % 3, k, :]
                    nc.tensor.matmul(dst, wh, hi[:, k, :], start=(k == 0), stop=False)
                    nc.tensor.matmul(dst, wh, lo[:, k, :], start=False, stop=False)
                    z = nc.tensor.matmul(dst, wl, hi[:, k, :], start=False, stop=(k == KT - 1))
                z.then_inc(slot_free, 1)

            def mm(dst, lhsT, rhs, start=True, stop=True, **kw):
                return nc.tensor.matmul(dst, lhsT, rhs, start=start, stop=stop, **kw)

            def tr(dst, src):
                n = src.shape[0]
                return nc.tensor.transpose(dst, src, ident[0:n, 0:n])

            def norm(ph, l):
                st, it = s[ph], (l if ph != "normf" else 0)
                for k in range(KT):
                    if k % 4 == 0:
                        pe.wait_ge(*st["act"].at(it, "sq0" if k == 0 else "sq"))
                    z = mm(bank[3][:, 0:256], ones[:], nsq[:, k, :], start=(k == 0), stop=(k == KT - 1))
                z.then_inc(st["pe"].step("ss"), 1)

            def inverse(st, it, levels, groups, first, mid, left):
                A, V, T = st["act"], st["dve"], st["pe"]
                for g, b in enumerate(groups):
                    pe.wait_ge(*V.at(it, "xt1", g))
                    for u in range(4):
                        z = tr(b.inv[0][:, P * u:P * u + P], v3(b.xt)[:, u, :])
                    z.then_inc(T.step("x1t", g), 1)
                if first:
                    first()
                for m, n in enumerate(levels[1:]):
                    for g, b in enumerate(groups):
                        if m == 0:
                            pe.wait_ge(*A.at(it, "x1", g))
                            pe.wait_ge(*V.at(it, "c2", g))
                        else:
                            pe.wait_ge(*V.at(it, f"xt{levels[m]}", g))
                        for u in range(4):
                            z = mm(b.inv[0][:, P * u:P * u + P], v3(b.c)[:, u, :], v3(b.x)[:, u, :])
                        z.then_inc(T.step(f"p{n}", g), 1)
                    if m == 0:
                        mid()
                    for g, b in enumerate(groups):
                        if m == 0:
                            pe.wait_ge(*V.at(it, left, g))
                        pe.wait_ge(*A.at(it, f"p{n}", g))
                        if n != levels[-1]:
                            for u in range(4):
                                mm(v3(b.inv[1][:, 64 * u:64 * u + 64], n), v3(b.xt)[:, u, :],
                                   half(v3(b.pm)[:, u, :], n, 0))
                        for u in range(4):
                            z = mm(v3(b.inv[2][:, 64 * u:64 * u + 64], n), v3(b.pm)[:, u, :],
                                   half(v3(b.xt)[:, u, :], n, 1))
                        z.then_inc(T.step(f"q{n}", g), 1)

            T = s["xin"]["pe"]
            pe.wait_ge(*s["setup"]["pool"].at(0, "const"))
            pe.wait_ge(x_in, 16)
            for t in range(NT):
                for k in range(KT):
                    z = tr(bank[4 + 2 * t + k // 4][:, P * (k % 4):P * (k % 4) + P], xtok[:, t, P * k:P * k + P])
                z.then_inc(T.step(f"t{t}"), 1)

            for l in range(DEPTH):
                norm("norm1", l)
                pe.wait_ge(small_in, SMALL * (l + 1))
                for b, n in enumerate((ROWS0, ROWS1, ROWS2)):
                    z = tr(bank[0][:, P * b:P * b + n], prow[0:n, b, :])
                z.then_inc(s["setup"]["pe"].step("t"), 1)
                st, it = s["scal"], l
                A, V, T = st["act"], st["dve"], st["pe"]
                pe.wait_ge(*s["norm1"]["dve"].at(l, "h"))
                for k in range(KT):
                    z = mm(bank[4][0:96, 0:256], wsm[:, k, :], hf[:, k, :], start=(k == 0), stop=(k == KT - 1))
                z.then_inc(T.step("mm"), 1)

                pe.wait_ge(*s["norm1"]["dve"].at(l, "lo"))
                pe.wait_ge(*s["setup"]["dve"].at(l, "pc"))
                with pe.Fori(0, IN_TILES // 6) as i:
                    for j in range(6):
                        product(bank[(b_in[l] + j) % 3][:, 0:256], t_in[l] + j, i, h_hi, h_lo,
                                free=i * 6 + (b_in[l] + j + 1))

                pe.wait_ge(*A.at(it, "beta"))
                pe.wait_ge(*V.at(it, "scan"))
                for t in range(NT):
                    z = tr(bank[5][:, P * t:P * t + P], srow[:, P * t:P * t + P])
                z.then_inc(T.step("tr"), 1)

                st = s["ssdg"]
                pe.wait_ge(silu_done, s_in[l] + 52)
                pe.wait_ge(bank_free, 3 + b_in[l] + IN_TILES)
                pe.wait_ge(*s["scal"]["dve"].at(l, "tc"))
                for g in range(2):
                    mm(bank[4 + g][:, 0:256], mix[:, BT_ + g, 0:128], mix[:, CT_ + g, :])
                    z = mm(bank[4 + g][:, 256:384], mix[:, BT_ + g, 128:256], mix[:, CT_ + g, 128:256])
                z.then_inc(st["pe"].step("g"), 1)
                pe.wait_ge(*st["dve"].at(l, "g"))
                st = s["ssd"]
                A, V, T = st["act"], st["dve"], st["pe"]
                with pe.Fori(0, 4) as i:
                    it = i + 4 * l
                    pe.wait_ge(*V.before(it))
                    for g, b in enumerate(ssd):
                        pe.wait_ge(*V.at(it, "sel", g))
                        mm(b.bank[0][:], ones[:], b.sel).then_inc(T.step("rows", g), 1)
                    for g, b in enumerate(ssd):
                        pe.wait_ge(*A.at(it, "fix", g))
                        for t in range(NT):
                            z = tr(b.bank[1][:, P * t:P * t + P], b.x[:, P * t:P * t + P])
                        z.then_inc(T.step("xt", g), 1)
                    for g, b in enumerate(ssd):
                        pe.wait_ge(*V.at(it, "p", g))
                        for h in range(2):
                            o = 64 * h
                            mm(b.bank[2][o:o + 64, 0:256], b.xdt[:, o:o + 64], b.p[:, 384 * h:384 * h + 256],
                               stop=False)
                            z = mm(b.bank[2][o:o + 64, 128:256], b.xdt[:, 128 + o:192 + o],
                                   b.p[:, 384 * h + 256:384 * h + 384], start=False)
                        z.then_inc(T.step("y", g), 1)
                st = s["ssdn"]
                for g in range(2):
                    it = 2 * l + g
                    pe.wait_ge(*st["act"].at(it, "sq"))
                    pe.wait_ge(*st["dve"].before(it))
                    for k in range(4):
                        z = mm(bank[6][:, 0:256], ones[:], d_sq[:, 256 * k:256 * k + 256], start=(k == 0),
                               stop=(k == 3))
                    z.then_inc(st["pe"].step("ss"), 1)

                st = s["gdn"]
                A, V, T = st["act"], st["dve"], st["pe"]
                finished(pe, "ssdn", l)
                with pe.Fori(0, 2) as i:
                    it = i + 2 * l
                    pe.wait_ge(*V.before(it))
                    pe.wait_ge(*A.before(it))
                    for g, b in enumerate(gdn):
                        pe.wait_ge(*A.at(it, "sq", g))
                        mm(b.bank[0][:], ones[:], b.sq[:, 0:512])
                        mm(b.bank[1][:], ones[:], b.sq[:, 512:1024]).then_inc(T.step("ss", g), 1)
                    for g, b in enumerate(gdn):
                        pe.wait_ge(*V.at(it, "sel", g))
                        mm(b.bank[2][:], ones[:], b.sel[:, 0:512])
                        mm(b.bank[3][:], ones[:], b.sel[:, 512:1024]).then_inc(T.step("rows", g), 1)
                    for g, b in enumerate(gdn):
                        pe.wait_ge(*V.at(it, "k", g))
                        for u in range(4):
                            h, t = u // 2, P * (u % 2)
                            kt = b.k[:, h, t:t + P]
                            mm(b.bank[0][:, P * u:P * u + P], kt, kt)
                            z = mm(b.bank[1][:, P * u:P * u + P], kt, mix[:, i * 4 + (QT + 2 * g + h), t:t + P])
                        z.then_inc(T.step("kk", g), 1)
                    def mid():
                        for g, b in enumerate(gdn):
                            pe.wait_ge(*V.at(it, "qkm0", g))
                            pe.wait_ge(*A.at(it, "vfix", g))
                            for h in range(2):
                                tr(b.bank[0][:, P * h:P * h + P], b.k[:, h, 0:P])
                            for t in range(NT):
                                for h in range(2):
                                    z = tr(b.bank[3][:, 256 * t + P * h:256 * t + P * h + P],
                                           b.v[:, h, P * t:P * t + P])
                            z.then_inc(T.step("tr", g), 1)

                    for g in range(2):
                        pe.wait_ge(*V.at(it, "qkm0", g))
                    inverse(st, it, GDN_LEVELS, gdn, None, mid, "bv")
                    for g, b in enumerate(gdn):
                        pe.wait_ge(*V.at(it, "xt64", g))
                        for h in range(2):
                            z = mm(b.bank[3][:, P * h:P * h + P], v3(b.xt)[:, 2 * h, :], b.bv[:, P * h:P * h + P])
                        z.then_inc(T.step("v0", g), 1)
                    for g, b in enumerate(gdn):
                        pe.wait_ge(*A.at(it, "v0", g))
                        for h in range(2):
                            z = mm(b.bank[1][:, P * h:P * h + P], b.kd[:, P * h:P * h + P], b.v0[:, P * h:P * h + P])
                        z.then_inc(T.step("s", g), 1)
                    for g, b in enumerate(gdn):
                        pe.wait_ge(*A.at(it, "s", g))
                        for h in range(2):
                            z = mm(b.bank[0][:, P * h:P * h + P], b.k[:, h, P:2 * P], b.s[:, P * h:P * h + P])
                        z.then_inc(T.step("ks", g), 1)
                    for g, b in enumerate(gdn):
                        pe.wait_ge(*V.at(it, "r1", g))
                        for h in range(2):
                            z = mm(b.bank[3][:, P * h:P * h + P], v3(b.xt)[:, 2 * h + 1, :], b.r1[:, P * h:P * h + P])
                        z.then_inc(T.step("v1", g), 1)
                    for g, b in enumerate(gdn):
                        pe.wait_ge(*A.at(it, "v1", g))
                        for h in range(2):
                            o = 256 * h
                            mm(b.bank[2][:, o:o + P], b.v0[:, P * h:P * h + P], v3(b.qk)[:, 2 * h, :])
                            mm(b.bank[2][:, o + P:o + 256], b.s[:, P * h:P * h + P], b.qe[:, h, :], stop=False)
                            z = mm(b.bank[2][:, o + P:o + 256], b.v1[:, P * h:P * h + P], v3(b.qk)[:, 2 * h + 1, :],
                                   start=False)
                        z.then_inc(T.step("o", g), 1)
                    for g, b in enumerate(gdn):
                        pe.wait_ge(*A.at(it, "osq", g))
                        mm(b.bank[1][:], ones[:], b.osq).then_inc(T.step("oss", g), 1)

                st, it = s["lora"], l
                A, T = st["act"], st["pe"]
                pe.wait_ge(lora_in, 48 * (l + 1))
                pe.wait_ge(*A.at(it, "act"))
                for i in range(8):
                    c = slice(P * i, P * i + P)
                    for x, b, w, a_ in (("w", 0, lw_sb[0:64, c], mix[0:64, LT, :]),
                                        ("a", 1, lw_sb[64:128, c], mix[64:128, LT, :]),
                                        ("g", 2, lg_sb[:, c], mix[:, LT + 1, :])):
                        if i > 1:
                            pe.wait_ge(*A.at(it, f"{x}{i - 2}"))
                        mm(bank[b + 3 * (i % 2)][:, 0:256], w, a_).then_inc(T.step(f"{x}{i}"), 1)
                st = s["rw"]
                A, V, T = st["act"], st["dve"], st["pe"]
                finished(pe, "lora", l)
                with pe.Fori(0, 4) as i:
                    it = i + 4 * l
                    pe.wait_ge(*V.before(it))
                    pe.wait_ge(*A.before(it))
                    for g, b in enumerate(rw):
                        pe.wait_ge(*A.at(it, "sq", g))
                        mm(b.bank[3][:, 0:256], halves[:], b.sq).then_inc(T.step("ss", g), 1)
                    for g, b in enumerate(rw):
                        pe.wait_ge(*A.at(it, "fix", g))
                        pe.wait_ge(*V.at(it, "bt", g))
                        for n, src, m in ((0, b.bt, 2), (2, b.kt, 2), (2, b.v, 3)):
                            for t in range(NT):
                                z = tr(b.bank[m][:, P * (n + t):P * (n + t) + P], src[:, P * t:P * t + P])
                        z.then_inc(T.step("tr", g), 1)
                    def scores(b, m, lhs, rhs):
                        for u in range(4):
                            h, t = u // 2, P * (u % 2)
                            z = mm(b.bank[m][:, P * u:P * u + P], lhs[:, 256 * h + t:256 * h + t + P], rhs[:, t:t + P])
                        return z

                    for g, b in enumerate(rw):
                        pe.wait_ge(*A.at(it, "btz", g))
                        pe.wait_ge(*V.at(it, "kat", g))
                        scores(b, 0, b.btz, b.kat).then_inc(T.step("sc0", g), 1)

                    def other_scores(g):
                        b = rw[g]
                        pe.wait_ge(*A.at(it, "ktz", g))
                        scores(b, 1, b.ktz, b.kat)
                        pe.wait_ge(*A.at(it, "tok", g))
                        pe.wait_ge(*V.at(it, "rt", g))
                        scores(b, 2, b.btz, b.rt)
                        scores(b, 3, b.ktz, b.rt).then_inc(T.step("sc", g), 1)

                    other_scores(0)

                    def first():
                        other_scores(1)

                    def mid():
                        for g, b in enumerate(rw):
                            pe.wait_ge(*V.at(it, "msk", g))
                            mm(b.bank[3][:, 256:512], halves[:], b.bon).then_inc(T.step("bon", g), 1)
                            for t in range(NT):
                                for h in range(2):
                                    z = mm(b.bank[3][:, P * t + 64 * h:P * t + 64 * h + 64], v3(b.akv)[:, 2 * h + t, :],
                                           b.vtok[:, t, 64 * h:64 * h + 64])
                            z.then_inc(T.step("av", g), 1)

                    inverse(st, it, RW_LEVELS, rw, first, mid, "msk")
                    for c in range(NCH):
                        t, o = c // 2, 64 * (c % 2)
                        if c > 0:
                            for g, b in enumerate(rw):
                                pe.wait_ge(*V.at(it, f"sb{c - 1}", g))
                                mm(b.bank[0][:, P * t + o:P * t + o + 64], b.sb[:, c % 2, :],
                                   b.rt[:, P * t + o:P * t + o + 64], start=False, stop=False, skip_group_check=True)
                                mm(b.bank[3][:, 0:128], b.kat[:, P * t:P * t + P], b.sb[:, c % 2, :])\
                                    .then_inc(T.step(f"r{c}", g), 1)
                        for g, b in enumerate(rw):
                            pe.wait_ge(*(V.at(it, f"r{c}", g) if c > 0 else V.at(it, "xt32", g)))
                            for h in range(2):
                                rhs = b.av[:, 0, :] if c == 0 else b.r
                                z = mm(b.bank[1][:, 64 * h:64 * h + 64], v3(b.xt)[:, 2 * h + t, :],
                                       rhs[:, 64 * h:64 * h + 64])
                            z.then_inc(T.step(f"u{c}", g), 1)
                        if c == 0:
                            for g, b in enumerate(rw):
                                for h in range(2):
                                    for n in range(NT):
                                        mm(b.bank[0][64 * h:64 * h + 64, P * n:P * n + P],
                                           b.vtok[:, n, 64 * h:64 * h + 64], v3(b.ark)[:, 2 * h + n, :],
                                           start=(n == 0), stop=False, skip_group_check=True)
                        for g, b in enumerate(rw):
                            pe.wait_ge(*A.at(it, f"u{c}", g))
                            if c < NCH - 1:
                                mm(b.bank[2][:, 0:128], b.btok[o:o + 64, t, :], b.un[o:o + 64, t, :], stop=False)
                                mm(b.bank[2][:, 0:128], b.ktok[o:o + 64, t, :], b.vtok[o:o + 64, t, :], start=False)\
                                    .then_inc(T.step(f"s{c}", g), 1)
                        if c % 2 == 1:
                            for g, b in enumerate(rw):
                                for h in range(2):
                                    z = mm(b.bank[0][64 * h:64 * h + 64, P * t:P * t + P],
                                           b.un[:, t, 64 * h:64 * h + 64], v3(b.arb)[:, 2 * h + t, :],
                                           start=False, stop=True, skip_group_check=True)
                                if c == NCH - 1:
                                    z.then_inc(T.step("y", g), 1)
                    for g, b in enumerate(rw):
                        pe.wait_ge(*A.at(it, "y", g))
                        mm(b.bank[1][:, 0:256], centre[:], b.e1).then_inc(T.step("yc", g), 1)
                    for g, b in enumerate(rw):
                        pe.wait_ge(*A.at(it, "ysq", g))
                        mm(b.bank[1][:, 256:512], halves[:], b.e2).then_inc(T.step("var", g), 1)

                finished(pe, "rw", l)
                for b in range(4):
                    if b == 3:
                        pe.wait_ge(y_split, 4 * l + b + 1)
                        for j in range(OUT_TILES):
                            product(bank[(b_out[l] + j) % 3][:, 0:256], t_out[l] + j, 0, y_hi, y_lo,
                                    free=b_out[l] + j + 1)
                        break
                    for n in range(4):
                        for j in range(4):
                            k = 16 * b + 4 * n + j
                            hi, lo = (h_hi, h_lo) if j < 2 else (y_hi, y_lo)
                            if (n, j) == (0, 2):
                                pe.wait_ge(y_split, 4 * l + b + 1)
                            product(bank[(b_mrg[l] + k) % 3][:, 0:256], t_mrg[l] + k, 0, hi, lo,
                                    free=b_mrg[l] + k + 1)

                norm("norm2", l)
                if l % 2 == 1:
                    st, it = s["route"], l // 2
                    A, V, T = st["act"], st["dve"], st["pe"]
                    pe.wait_ge(*s["norm2"]["dve"].at(l, "h"))
                    pe.wait_ge(*st["dve"].before(it))
                    pe.wait_ge(router_in, 16 * (it + 1))
                    for t in range(NT):
                        for k in range(KT):
                            z = mm(bank[4][:, 8 * t:8 * t + 8], hf[:, k, P * t:P * t + P], q_w[:, k, :],
                                   start=(k == 0), stop=(k == KT - 1))
                    z.then_inc(T.step("mm"), 1)

                def shares():
                    it = l // 2
                    V, T = s["route"]["dve"], s["route"]["pe"]
                    pe.wait_ge(*V.at(it, "c1"))
                    for t in range(NT):
                        z = tr(bank[5][0:8, P * t:P * t + P], q_c[:, t, :])
                    z.then_inc(T.step("tr"), 1)
                    pe.wait_ge(*V.at(it, "sel"))
                    for e in range(N_EXP):
                        z = mm(bank[4 + e // 2][:, 256 * (e % 2):256 * (e % 2) + 256], ones[0:8, :], q_sel[:, e, :])
                    z.then_inc(T.step("rows"), 1)
                    pe.wait_ge(*V.at(it, "cb"))

                def ffn(i, between=None):
                    it = i + f_it[l]
                    for j in range(4):
                        product(bank[j][:, 0:256], t_ffn[l] + j, i, h_hi, h_lo)
                    if between:
                        between()
                    for j in range(2):
                        base = t_ffn[l] + 4 + j
                        pe.wait_ge(lo_done, i * 6 + (base + 1))
                        pe.wait_ge(act_ready, it * 2 + (2 + j + 1))
                        if j == 0:
                            pe.wait_ge(down_free, it + 1)
                        for k in range(KT):
                            dst = bank[4 + k // 2][:, 256 * (k % 2):256 * (k % 2) + 256]
                            wh, wl = w_hi[:, base % 3, k, :], w_lo[:, base % 3, k, :]
                            mm(dst, wh, y_hi[:, j, :], start=(j == 0 and k % 2 == 0), stop=False, skip_group_check=True)
                            mm(dst, wh, y_lo[:, j, :], start=False, stop=False, skip_group_check=True)
                            z = mm(dst, wl, y_hi[:, j, :], start=False, stop=(j == 1), skip_group_check=True)
                        z.then_inc(slot_free, 1)

                pe.wait_ge(*s["norm2"]["dve"].at(l, "lo"))
                pe.wait_ge(bank_free, 3 + b_out[l] + OUT_TILES)
                if l % 2 == 0:
                    with pe.Fori(0, FI) as i:
                        ffn(i)
                else:
                    ffn(0, between=shares)
                    with pe.Fori(1, FI * N_EXP) as i:
                        ffn(i)
            norm("normf", 0)
            T = s["xout"]["pe"]
            pe.wait_ge(*s["normf"]["dve"].at(0, "h"))
            for t in range(NT):
                for k in range(KT):
                    z = tr(bank[4 + 2 * t + k // 4][:, P * (k % 4):P * (k % 4) + P], hf[:, k, P * t:P * t + P])
                z.then_inc(T.step(f"t{t}"), 1)

        @block.vector
        def _(dve):
            v = nc.vector

            def column(name, n=0):
                return pcol[:, bass.ds(n + PCOL[name], 1)] if not isinstance(n, int) \
                    else pcol[:, PCOL[name] + n:PCOL[name] + n + 1]

            def norm(ph, l, weight):
                st, it = s[ph], (l if ph != "normf" else 0)
                A, V, T = st["act"], st["dve"], st["pe"]
                dve.wait_ge(*A.at(it, "rs"))
                for k in range(KT):
                    z = v.scalar_tensor_tensor(out=hf[:, k, :], in0=xres[:, k, :], scalar=column(weight, k), in1=nr,
                                               op0=ALU.mult, op1=ALU.mult)
                    if k % 4 == 3:
                        z.then_inc(V.step("h0" if k == 3 else "h"), 1)
                if ph != "normf":
                    for name, q, k in (("lo0", "hi0", slice(0, 4)), ("lo", "hi", slice(4, 8))):
                        dve.wait_ge(*A.at(it, q))
                        v.tensor_tensor(h_lo[:, k, :], hf[:, k, :], h_hi[:, k, :].bitcast(F32), ALU.subtract)\
                            .then_inc(V.step(name), 1)

            def inverse(st, it, levels, groups, maker, mid, late):
                A, V, T = st["act"], st["dve"], st["pe"]
                for g, b in enumerate(groups):
                    dve.wait_ge(*maker.at(it, "mt", g))
                    v.tensor_tensor(v3(b.c), v3(b.mt), over(level[:, 0, :], 4), ALU.mult).then_inc(V.step("c1", g), 1)
                for g, b in enumerate(groups):
                    dve.wait_ge(*V.at(it, "c1", g))
                    v.tensor_tensor(v3(b.xt), over(ident[:], 4), v3(b.c), ALU.subtract).then_inc(V.step("xt1", g), 1)
                for g, b in enumerate(groups):
                    dve.wait_ge(*V.at(it, "xt1", g))
                    v.tensor_tensor(v3(b.c), v3(b.mt), over(level[:, 1, :], 4), ALU.mult).then_inc(V.step("c2", g), 1)
                mid()
                for m, n in enumerate(levels[1:]):
                    if n != levels[-1]:
                        for g, b in enumerate(groups):
                            dve.wait_ge(*T.at(it, f"p{n}", g))
                            v.tensor_tensor(v3(b.c), v3(b.mt), over(level[:, m + 2, :], 4), ALU.mult)\
                                .then_inc(V.step(f"c{levels[m + 2]}", g), 1)
                    for g, b in enumerate(groups):
                        dve.wait_ge(*T.at(it, f"q{n}", g))
                        if n != levels[-1]:
                            x = half(b.x, n, 0)
                            v.tensor_tensor(x, x, v3(b.inv[1][:, 0:256], n), ALU.subtract)
                        xt = half(b.xt, n, 1)
                        v.tensor_tensor(xt, xt, v3(b.inv[2][:, 0:256], n), ALU.subtract)\
                            .then_inc(V.step(f"xt{n}", g), 1)
                    if m == 0:
                        late()

            V, T = s["xin"]["dve"], s["xin"]["pe"]
            for t in range(NT):
                dve.wait_ge(*T.at(0, f"t{t}"))
                for q in range(2):
                    z = v.tensor_copy(xres[:, 4 * q:4 * q + 4, P * t:P * t + P], v3(bank[4 + 2 * t + q][:]))
                z.then_inc(V.step(f"c{t}"), 1)
            products = 0

            for l in range(DEPTH):
                V, T = s["setup"]["dve"], s["setup"]["pe"]
                dve.wait_ge(*T.at(l, "t"))
                for b, n in enumerate((ROWS0, ROWS1, ROWS2)):
                    z = v.tensor_copy(pcol[:, P * b:P * b + n], bank[0][:, P * b:P * b + n])
                z.then_inc(V.step("pc"), 1)
                if l == 0:
                    dve.wait_ge(*s["setup"]["pool"].at(0, "const"))
                    v.scalar_tensor_tensor(out=centre[:], in0=halves[:], scalar=-1.0 / RW_D, in1=ident[:],
                                           op0=ALU.mult, op1=ALU.add)
                dve.wait_ge(*V.at(l, "pc"))
                r = PCOL["rwkv_mu"]
                v.tensor_scalar(one_mu[:], pcol[:, r:r + 26], -1.0, 1.0, ALU.mult, ALU.add).then_inc(V.step("mu1"), 1)
                for h in range(2):
                    o = slice(64 * h, 64 * h + 64)
                    v.tensor_copy(dskip[o, :], dheads[o, :].rearrange("p (n a) -> p n a", a=2)[:, :, h])
                r = PCOL["rwkv_k_a"]
                v.tensor_scalar(one_ka[:], pcol[:, r:r + 8], -1.0, 1.0, ALU.mult, ALU.add).then_inc(V.step("ka1"), 1)
                norm("norm1", l, "attn_norm_w")

                st, it = s["scal"], l
                A, V, T = st["act"], st["dve"], st["pe"]
                dve.wait_ge(*A.at(it, "aexp"))
                v.tensor_scalar(nha[:], nha[:], -1.0, None, ALU.mult).then_inc(V.step("neg"), 1)
                dve.wait_ge(*T.at(it, "mm"))
                v.tensor_scalar(sxb, bank[4][0:96, 0:256], hb[:, 0:1], None, ALU.add).then_inc(V.step("xb"), 1)
                dve.wait_ge(*V.at(it, "xb"))
                v.scalar_tensor_tensor(out=sab, in0=sxb, scalar=-1.0, in1=sxb, op0=ALU.mult, op1=ALU.max)\
                    .then_inc(V.step("abs"), 1)
                dve.wait_ge(*A.at(it, "ln"))
                v.scalar_tensor_tensor(out=ssp, in0=sxb, scalar=0.0, in1=sln, op0=ALU.max, op1=ALU.add)\
                    .then_inc(V.step("sp"), 1)
                dve.wait_ge(*V.at(it, "sp"))
                v.tensor_scalar(sad, ssp, nha[:, 0:1], None, ALU.mult).then_inc(V.step("ad"), 1)
                v.tensor_tensor(sd, sxb, ssp, ALU.subtract).then_inc(V.step("d"), 1)
                dve.wait_ge(*V.at(it, "ad"))
                v.tensor_copy(srow[96:112, :], ssp[0:16, :])
                v.tensor_tensor_scan(srow[0:16, :], ones[0:16, 0:1].broadcast_to([16, SEQ]), sad[0:16, :], 0.0,
                                     ALU.mult, ALU.add)
                for t in range(NT):
                    c = slice(P * t, P * t + P)
                    z = v.tensor_tensor_scan(srow[32:40, c], ones[32:40, :], sad[32:40, c], 0.0, ALU.mult, ALU.add)
                z.then_inc(V.step("scan"), 1)

                def conv(j, i):
                    n = i * 6 + j
                    src, dst = bank[(b_in[l] + j) % 3][:, 0:256], mix[:, n, :]
                    dve.wait_ge(slot_free, i * 6 + (3 + t_in[l] + j + 1))
                    z = v.tensor_scalar(dst, src, column("conv_w3", n), column("conv_b", n), ALU.mult, ALU.add)
                    z.then_inc(conv_link, 1)
                    for k in (1, 2, 3):
                        dve.wait_ge(conv_link, i * 18 + (l * 3 * N_CONV + 3 * j + k))
                        z = v.scalar_tensor_tensor(out=mix[:, n, k:], in0=src[:, 0:SEQ - k],
                                                   scalar=column(f"conv_w{3 - k}", n), in1=mix[:, n, k:],
                                                   op0=ALU.mult, op1=ALU.add)
                        z.then_inc(conv_link if k < 3 else bank_free, 1)

                def shift(j, i, base, n, dst):
                    src = bank[(b_in[l] + base + j) % 3][:, 0:256]
                    dve.wait_ge(slot_free, i * 6 + (3 + t_in[l] + base + j + 1))
                    v.tensor_scalar(mix[:, dst, :], src, one_mu[:, bass.ds(n, 1)], None, ALU.mult)\
                        .then_inc(shift_link, 1)
                    dve.wait_ge(shift_link, (n - 24 + 1 if isinstance(n, int) else n + 3) + 26 * l)
                    v.scalar_tensor_tensor(out=mix[:, dst, 1:], in0=src[:, 0:SEQ - 1], scalar=column("rwkv_mu", n),
                                           in1=mix[:, dst, 1:], op0=ALU.mult, op1=ALU.add).then_inc(bank_free, 1)

                dve.wait_ge(*V.at(it, "sp"))
                dve.wait_ge(*s["norm1"]["dve"].at(l, "lo"))
                with dve.Fori(0, N_CONV // 6) as i:
                    for j in range(6):
                        conv(j, i)
                for j in range(16):
                    n = N_CONV + j
                    dve.wait_ge(slot_free, 3 + t_in[l] + n + 1)
                    v.tensor_copy(mix[:, ZT + j, :], bank[(b_in[l] + n) % 3][:, 0:256]).then_inc(bank_free, 1)
                for j in range(2):
                    shift(j, 0, N_CONV + 16, 24 + j, LT + j)
                with dve.Fori(0, 4) as i:
                    for j in range(6):
                        shift(j, i, N_CONV + 18, i * 6 + j, i * 6 + (RT + j))

                dve.wait_ge(*T.at(it, "tr"))
                v.tensor_copy(scol[:], v3(bank[5][:, 0:256])).then_inc(V.step("tc"), 1)
                dve.wait_ge(*A.at(it, "eg"))
                v.scalar_tensor_tensor(out=nbeta[:], in0=scol[:, :, 64:72], scalar=-1.0, in1=egc[:],
                                       op0=ALU.mult, op1=ALU.mult).then_inc(V.step("nb"), 1)

                dve.wait_ge(*s["ssdg"]["pe"].at(l, "g"))
                for g in range(2):
                    z = v.tensor_tensor(d_g[:, g, :], bank[4 + g][:, 0:384], flat(tri[:]), ALU.mult)
                z.then_inc(s["ssdg"]["dve"].step("g"), 1)
                st = s["ssd"]
                A, V, T = st["act"], st["dve"], st["pe"]
                finished(dve, "ssdg", l)
                with dve.Fori(0, 4) as i:
                    it = i + 4 * l
                    dve.wait_ge(*T.before(it))
                    dve.wait_ge(*V.before(it))
                    for g, b in enumerate(ssd):
                        for h in range(2):
                            z = v.tensor_scalar(b.sel[:, 256 * h:256 * h + 256], srow[:],
                                                ident[:, bass.ds(i * 2 + (8 * g + h), 1)], None, ALU.mult)
                        z.then_inc(V.step("sel", g), 1)
                    for g, b in enumerate(ssd):
                        dve.wait_ge(*T.at(it, "rows", g))
                        for h in range(2):
                            for t in range(NT):
                                o = 384 * h + 256 * t
                                z = v.tensor_scalar(b.diff[:, o:o + 256 - P * t],
                                                    b.bank[0][:, 256 * h + P * t:256 * h + 256],
                                                    scol[:, t, bass.ds(i * 2 + (8 * g + h), 1)], 0.0,
                                                    ALU.subtract, ALU.min)
                        z.then_inc(V.step("diff", g), 1)
                    for g, b in enumerate(ssd):
                        dve.wait_ge(*T.at(it, "xt", g))
                        for t in range(NT):
                            for h in range(2):
                                o = P * t + 64 * h
                                z = v.tensor_scalar(b.xdt[:, o:o + 64], b.bank[1][:, o:o + 64],
                                                    scol[:, t, bass.ds(i * 2 + (96 + 8 * g + h), 1)], None, ALU.mult)
                        z.then_inc(V.step("xdt", g), 1)
                    for g, b in enumerate(ssd):
                        dve.wait_ge(*A.at(it, "exp", g))
                        v.tensor_tensor(v3(b.p, 384), v3(b.diff, 384), over(d_g[:, g, :], 2), ALU.mult)\
                            .then_inc(V.step("p", g), 1)
                    for g, b in enumerate(ssd):
                        dve.wait_ge(*T.at(it, "y", g))
                        v.scalar_tensor_tensor(out=b.y, in0=b.x, scalar=dskip[:, bass.ds(i + 4 * g, 1)],
                                               in1=b.bank[2][:, 0:256], op0=ALU.mult, op1=ALU.add)\
                            .then_inc(V.step("y", g), 1)
                    for g, b in enumerate(ssd):
                        dve.wait_ge(*V.at(it, "y", g))
                        z = mix[:, i + (ZT + 4 * g), :]
                        v.tensor_tensor(z, b.y, z, ALU.mult).then_inc(V.step("yz", g), 1)
                st = s["ssdn"]
                A, V, T = st["act"], st["dve"], st["pe"]
                for g in range(2):
                    it = 2 * l + g
                    dve.wait_ge(*A.at(it, "rs"))
                    for k in range(4):
                        n = ZT + 4 * g + k
                        z = v.scalar_tensor_tensor(out=mix[:, n, :], in0=mix[:, n, :],
                                                   scalar=column("ssm_norm_w", 4 * g + k), in1=d_r,
                                                   op0=ALU.mult, op1=ALU.mult)
                    z.then_inc(V.step("y"), 1)

                st = s["gdn"]
                A, V, T = st["act"], st["dve"], st["pe"]
                finished(dve, "ssdn", l)
                dve.wait_ge(lo_done, t_mrg[l] + 2)
                with dve.Fori(0, 2) as i:
                    it = i + 2 * l
                    dve.wait_ge(*T.before(it))
                    dve.wait_ge(*A.before(it))
                    dve.wait_ge(*V.before(it))
                    for g, b in enumerate(gdn):
                        for r, o in ((32, 0), (64, 512)):
                            for h in range(2):
                                z = v.tensor_scalar(b.sel[:, o + 256 * h:o + 256 * h + 256], srow[:],
                                                    ident[:, bass.ds(i * 4 + (r + 2 * g + h), 1)], None, ALU.mult)
                        z.then_inc(V.step("sel", g), 1)
                    for g, b in enumerate(gdn):
                        dve.wait_ge(*A.at(it, "rs", g))
                        q = flat(mix[:, bass.ds(i * 4 + (QT + 2 * g), 2), :])
                        v.scalar_tensor_tensor(out=q, in0=q, scalar=GDN_D ** -0.5, in1=b.rs[:, 0:512],
                                               op0=ALU.mult, op1=ALU.mult).then_inc(V.step("q", g), 1)
                        v.tensor_tensor(flat(b.k), flat(mix[:, bass.ds(i * 4 + (KTL + 2 * g), 2), :]),
                                        b.rs[:, 512:1024], ALU.mult).then_inc(V.step("k", g), 1)
                    for g, b in enumerate(gdn):
                        dve.wait_ge(*T.at(it, "rows", g))
                        for h in range(2):
                            for t in range(NT):
                                z = v.tensor_scalar(b.e[:, h, P * t:P * t + P],
                                                    b.bank[2][:, 256 * h + P * t:256 * h + P * t + P],
                                                    scol[:, t, bass.ds(i * 4 + (32 + 2 * g + h), 1)], 0.0,
                                                    ALU.subtract, ALU.min)
                        z.then_inc(V.step("diff", g), 1)
                    for g, b in enumerate(gdn):
                        dve.wait_ge(*T.at(it, "kk", g))
                        dve.wait_ge(*A.at(it, "exp", g))
                        v.tensor_tensor(b.mt, flat(b.e), b.bank[0][:], ALU.mult).then_inc(V.step("mt0", g), 1)
                        dve.wait_ge(*V.at(it, "mt0", g))
                        v.tensor_tensor(b.mt, b.mt, b.bank[3][:], ALU.mult).then_inc(V.step("mt", g), 1)
                        v.tensor_tensor(b.qk, flat(b.e), b.bank[1][:], ALU.mult).then_inc(V.step("qkm0", g), 1)
                    def mid():
                        for g, b in enumerate(gdn):
                            dve.wait_ge(*T.at(it, "tr", g))
                            for h in range(2):
                                z = v.tensor_scalar(b.kd[:, P * h:P * h + P], b.bank[0][:, P * h:P * h + P],
                                                    b.e[:, h, P - 1:P], None, ALU.mult)
                            z.then_inc(V.step("kdec", g), 1)
                            for t in range(NT):
                                for h in range(2):
                                    o = 256 * t + P * h
                                    z = v.tensor_scalar(b.bv[:, o:o + P], b.bank[3][:, o:o + P],
                                                        scol[:, t, bass.ds(i * 4 + (64 + 2 * g + h), 1)], None,
                                                        ALU.mult)
                            z.then_inc(V.step("bv", g), 1)

                    def late():
                        for g, b in enumerate(gdn):
                            dve.wait_ge(*V.at(it, "qkm0", g))
                            v.tensor_tensor(v3(b.qk), v3(b.qk), over(tri[:, 0, :], 4), ALU.mult)\
                                .then_inc(V.step("qkm", g), 1)
                        for g, b in enumerate(gdn):
                            dve.wait_ge(*A.at(it, "eg", g))
                            v.tensor_tensor(b.qe, mix[:, bass.ds(i * 4 + (QT + 2 * g), 2), P:2 * P], b.eg, ALU.mult)\
                                .then_inc(V.step("qe", g), 1)

                    inverse(st, it, GDN_LEVELS, gdn, V, mid, late)
                    for g, b in enumerate(gdn):
                        dve.wait_ge(*T.at(it, "ks", g))
                        for h in range(2):
                            z = v.scalar_tensor_tensor(out=b.r1[:, P * h:P * h + P], in0=b.bank[0][:, P * h:P * h + P],
                                                       scalar=nbeta[:, 1, bass.ds(i * 4 + (2 * g + h), 1)],
                                                       in1=b.bv[:, 256 + P * h:256 + P * h + P], op0=ALU.mult,
                                                       op1=ALU.add)
                        z.then_inc(V.step("r1", g), 1)
                    for g, b in enumerate(gdn):
                        dve.wait_ge(*A.at(it, "ors", g))
                        v.scalar_tensor_tensor(out=flat(b.o), in0=flat(b.o), scalar=column("gdn_norm_w"), in1=b.ov,
                                               op0=ALU.mult, op1=ALU.mult).then_inc(V.step("on", g), 1)
                    for g, b in enumerate(gdn):
                        dve.wait_ge(*V.at(it, "on", g))
                        z = flat(mix[:, bass.ds(i * 4 + (ZGT + 2 * g), 2), :])
                        v.tensor_tensor(z, flat(b.o), z, ALU.mult).then_inc(V.step("oz", g), 1)

                st = s["rw"]
                A, V, T = st["act"], st["dve"], st["pe"]
                finished(dve, "lora", l)
                with dve.Fori(0, 4) as i:
                    it = i + 4 * l
                    dve.wait_ge(*T.before(it))
                    dve.wait_ge(*A.before(it))
                    dve.wait_ge(*V.before(it))
                    for g, b in enumerate(rw):
                        for c in range(NCH):
                            k = slice(64 * c, 64 * c + 64)
                            z = v.tensor_tensor_scan(b.p[:, k], ones[:, 0:64], mix[:, i * 2 + (SGW + g), k], 0.0,
                                                     ALU.mult, ALU.add)
                        z.then_inc(V.step("scan", g), 1)
                    for g, b in enumerate(rw):
                        dve.wait_ge(*V.at(it, "scan", g))
                        v.tensor_scalar(b.c4, v3(b.p, 64)[:, :, 63], 0.5, None, ALU.mult).then_inc(V.step("mid", g), 1)
                    for g, b in enumerate(rw):
                        dve.wait_ge(*V.at(it, "mid", g))
                        c4 = b.c4.rearrange("p (n o) -> p n o", o=1).broadcast_to([P, NCH, 64])
                        v.tensor_tensor(v3(b.pc, 64), v3(b.p, 64), c4, ALU.subtract).then_inc(V.step("pc", g), 1)
                    for g, b in enumerate(rw):
                        dve.wait_ge(*V.at(it, "pc", g))
                        v.tensor_tensor(b.p0, b.pc, mix[:, i * 2 + (SGW + g), :], ALU.subtract)\
                            .then_inc(V.step("p0", g), 1)
                    for g, b in enumerate(rw):
                        v.tensor_scalar(b.km, mix[:, i * 2 + (AT + g), :], column("rwkv_k_a", i * 2 + g),
                                        one_ka[:, bass.ds(i * 2 + g, 1)], ALU.mult, ALU.add).then_inc(V.step("m", g), 1)
                    for g, b in enumerate(rw):
                        dve.wait_ge(*V.at(it, "m", g))
                        v.tensor_tensor(b.km, b.km, mix[:, i * 2 + (RKT + g), :], ALU.mult).then_inc(V.step("km", g), 1)
                    for g, b in enumerate(rw):
                        dve.wait_ge(*V.at(it, "km", g))
                        v.scalar_tensor_tensor(out=b.bon, in0=mix[:, i * 2 + (RT + g), :],
                                               scalar=column("rwkv_r_k", i * 2 + g), in1=b.km, op0=ALU.mult,
                                               op1=ALU.mult).then_inc(V.step("rkm", g), 1)
                    for g, b in enumerate(rw):
                        dve.wait_ge(*A.at(it, "e", g))
                        v.tensor_tensor(b.ecc[:, 0:3], b.ec[:, 0:3], b.ec[:, 1:4], ALU.mult)\
                            .then_inc(V.step("ecc", g), 1)
                    for g, b in enumerate(rw):
                        v.tensor_tensor(b.rt, mix[:, i * 2 + (RT + g), :], b.e1, ALU.mult).then_inc(V.step("rt", g), 1)
                    for g, b in enumerate(rw):
                        dve.wait_ge(*V.at(it, "km", g))
                        v.tensor_tensor(b.kt, b.km, b.e2, ALU.mult).then_inc(V.step("kt", g), 1)
                    for g, b in enumerate(rw):
                        dve.wait_ge(*A.at(it, "rs", g))
                        v.scalar_tensor_tensor(out=b.kk, in0=mix[:, i * 2 + (RKT + g), :],
                                               scalar=column("rwkv_k_k", i * 2 + g), in1=b.rs, op0=ALU.mult,
                                               op1=ALU.mult).then_inc(V.step("kk", g), 1)
                    for g, b in enumerate(rw):
                        dve.wait_ge(*V.at(it, "kk", g))
                        v.tensor_tensor(b.akk, b.kk, mix[:, i * 2 + (AT + g), :], ALU.mult)\
                            .then_inc(V.step("akk", g), 1)
                    for g, b in enumerate(rw):
                        dve.wait_ge(*V.at(it, "akk", g))
                        v.tensor_tensor(b.bt, b.akk, b.e2, ALU.mult).then_inc(V.step("bt", g), 1)
                    for g, b in enumerate(rw):
                        v.tensor_tensor(b.kat, b.kk, b.e0, ALU.mult).then_inc(V.step("kat", g), 1)
                    def mid():
                        for g, b in enumerate(rw):
                            dve.wait_ge(*T.at(it, "sc", g))
                            v.tensor_tensor(v3(b.akv), v3(b.bank[1][:]), over(stri64[:], 4), ALU.mult)
                            v.tensor_tensor(v3(b.arb), v3(b.bank[2][:]), over(tri64[:], 4), ALU.mult)
                            v.tensor_tensor(v3(b.ark), v3(b.bank[3][:]), over(tri64[:], 4), ALU.mult)\
                                .then_inc(V.step("msk", g), 1)

                    def late():
                        for g, b in enumerate(rw):
                            dve.wait_ge(*T.at(it, "av", g))
                            v.tensor_copy(b.av, v3(b.bank[3][:, 0:256])).then_inc(V.step("av", g), 1)
                        for g, b in enumerate(rw):
                            v.tensor_tensor(b.bon, b.v, b.bank[3][:, 256:512], ALU.mult).then_inc(V.step("bon", g), 1)

                    dve.wait_ge(*V.at(it, "kat", 1))
                    inverse(st, it, RW_LEVELS, rw, A, mid, late)
                    for c in range(NCH - 1):
                        for g, b in enumerate(rw):
                            dve.wait_ge(*T.at(it, f"s{c}", g))
                            new = b.sb[:, (c + 1) % 2, :]
                            v.scalar_tensor_tensor(out=new, in0=b.bank[2][:, 0:128], scalar=b.ecc[:, c:c + 1],
                                                   in1=halves[:], op0=ALU.mult, op1=ALU.mult)\
                                .then_inc(V.step(f"sa{c}" if c > 0 else "sb0", g), 1)
                        if c > 0:
                            for g, b in enumerate(rw):
                                dve.wait_ge(*V.at(it, f"sa{c}", g))
                                new = b.sb[:, (c + 1) % 2, :]
                                v.scalar_tensor_tensor(out=new, in0=b.sb[:, c % 2, :], scalar=b.ecc[:, c:c + 1],
                                                       in1=new, op0=ALU.mult, op1=ALU.add).then_inc(V.step(f"sb{c}", g), 1)
                        for g, b in enumerate(rw):
                            dve.wait_ge(*T.at(it, f"r{c + 1}", g))
                            v.tensor_tensor(b.r, b.av[:, (c + 1) // 2, :], b.bank[3][:, 0:128], ALU.add)\
                                .then_inc(V.step(f"r{c + 1}", g), 1)
                    for g, b in enumerate(rw):
                        dve.wait_ge(*A.at(it, "yrs", g))
                        v.scalar_tensor_tensor(out=b.e0, in0=b.bank[1][:, 0:256],
                                               scalar=column("rwkv_ln_w", i * 2 + g), in1=b.rs,
                                               op0=ALU.mult, op1=ALU.mult).then_inc(V.step("yn", g), 1)
                    for g, b in enumerate(rw):
                        dve.wait_ge(*V.at(it, "yn", g))
                        v.scalar_tensor_tensor(out=b.e0, in0=b.e0, scalar=column("rwkv_ln_b", i * 2 + g), in1=b.bon,
                                               op0=ALU.add, op1=ALU.add).then_inc(V.step("yb", g), 1)
                    for g, b in enumerate(rw):
                        dve.wait_ge(*V.at(it, "yb", g))
                        v.tensor_tensor(mix[:, i * 2 + (RT + g), :], b.e0, mix[:, i * 2 + (GT + g), :], ALU.mult)\
                            .then_inc(V.step("out", g), 1)

                finished(dve, "rw", l)
                for b in range(4):
                    src = mix[:, y_of[b]:y_of[b] + 8, :] if b < 3 else merged
                    dve.wait_ge(y_hi_done, 4 * l + b + 1)
                    v.tensor_tensor(y_lo[:], src, y_hi[:].bitcast(F32), ALU.subtract).then_inc(y_split, 1)
                    if b == 3:
                        for j in range(OUT_TILES):
                            dve.wait_ge(slot_free, 3 + t_out[l] + j + 1)
                            v.tensor_tensor(xres[:, j, :], xres[:, j, :], bank[(b_out[l] + j) % 3][:, 0:256], ALU.add)\
                                .then_inc(bank_free, 1)
                        break
                    for n in range(4):
                        for j in range(4):
                            k = 16 * b + 4 * n + j
                            src = bank[(b_mrg[l] + k) % 3][:, 0:256]
                            dve.wait_ge(slot_free, 3 + t_mrg[l] + k + 1)
                            if j < 2:
                                if k >= 4:
                                    dve.wait_ge(bank_free, 3 + b_mrg[l] + k - 2 + 1)
                                v.tensor_copy(gate_sb[:, j, :], src).then_inc(bank_free, 1)
                                continue
                            m = merged[:, 2 * n + j - 2, :]
                            dve.wait_ge(gate_done, 24 * l + 8 * b + 2 * n + j - 1)
                            if b == 0:
                                v.tensor_tensor(m, gate_sb[:, j - 2, :], src, ALU.mult).then_inc(bank_free, 1)
                            else:
                                dve.wait_ge(bank_free, 3 + b_mrg[l] + k - 16 + 1)
                                products += 1
                                v.tensor_tensor(prod_sb[:, j - 2, :], gate_sb[:, j - 2, :], src, ALU.mult)\
                                    .then_inc(link, 1)
                                dve.wait_ge(link, products)
                                v.tensor_tensor(m, m, prod_sb[:, j - 2, :], ALU.add).then_inc(bank_free, 1)

                norm("norm2", l, "ffn_norm_w")
                if l % 2 == 1:
                    st, it = s["route"], l // 2
                    A, V, T = st["act"], st["dve"], st["pe"]
                    dve.wait_ge(*T.at(it, "mm"))
                    v.tensor_copy(q_l, v3(bank[4][:, 0:16], 8)).then_inc(V.step("lg"), 1)
                    dve.wait_ge(*V.at(it, "lg"))
                    for t in range(NT):
                        z = v.max(q_m[:, t, :], q_l[:, t, :])
                    z.then_inc(V.step("mx"), 1)
                    shape = [P, NT, 8, 8]
                    other = q_l.rearrange("p t (o f) -> p t o f", o=1).broadcast_to(shape)
                    own = q_l.rearrange("p t (e o) -> p t e o", o=1).broadcast_to(shape)
                    v.tensor_tensor(q_gt, other, own, ALU.is_gt).then_inc(V.step("gt"), 1)
                    v.tensor_tensor(q_eq, other, own, ALU.is_equal).then_inc(V.step("eq"), 1)
                    dve.wait_ge(*V.at(it, "eq"))
                    v.tensor_tensor(q_eq, q_eq, before[:].rearrange("p (o e) f -> p o e f", o=1).broadcast_to(shape),
                                    ALU.mult).then_inc(V.step("eqb"), 1)
                    dve.wait_ge(*V.at(it, "eqb"))
                    v.tensor_tensor(q_gt, q_gt, q_eq, ALU.add).then_inc(V.step("cnt"), 1)
                    dve.wait_ge(*V.at(it, "cnt"))
                    v.tensor_reduce(q_rank, q_gt, AX.X, ALU.add).then_inc(V.step("rank"), 1)
                    v.tensor_tensor(q_d, q_m[:, :, 1], q_m[:, :, 0], ALU.subtract).then_inc(V.step("d"), 1)
                    dve.wait_ge(*A.at(it, "e"))
                    v.tensor_scalar(q_1, q_e, 1.0, None, ALU.add).then_inc(V.step("p1"), 1)
                    dve.wait_ge(*V.at(it, "p1"))
                    v.reciprocal(q_p1, q_1).then_inc(V.step("p1r"), 1)
                    dve.wait_ge(*V.at(it, "p1r"))
                    v.tensor_tensor(q_p2, q_e, q_p1, ALU.mult).then_inc(V.step("p2"), 1)
                    dve.wait_ge(*V.at(it, "p2"))
                    for t in range(NT):
                        v.tensor_scalar(q_c0[:, t, :], q_rank[:, t, :], 0.0, q_p1[:, t:t + 1], ALU.is_equal, ALU.mult)
                        z = v.tensor_scalar(q_c1[:, t, :], q_rank[:, t, :], 1.0, q_p2[:, t:t + 1], ALU.is_equal,
                                            ALU.mult)
                    z.then_inc(V.step("c0"), 1)
                    dve.wait_ge(*V.at(it, "c0"))
                    v.tensor_tensor(q_c, q_c0, q_c1, ALU.add).then_inc(V.step("c1"), 1)
                    dve.wait_ge(*T.at(it, "tr"))
                    v.tensor_copy(q_cr, bank[5][0:8, 0:256]).then_inc(V.step("cr"), 1)
                    dve.wait_ge(*V.at(it, "cr"))
                    v.tensor_tensor(q_sel, over(q_cr, 8),
                                    ident[0:8, 0:8].rearrange("p (e o) -> p e o", o=1).broadcast_to([8, 8, 256]),
                                    ALU.mult).then_inc(V.step("sel"), 1)
                    dve.wait_ge(*T.at(it, "rows"))
                    for q in range(4):
                        z = v.tensor_copy(cb[:, 2 * q:2 * q + 2, :], v3(bank[4 + q][:], 256))
                    z.then_inc(V.step("cb"), 1)
                    dve.wait_ge(*V.at(it, "cb"))

                experts = 1 if l % 2 == 0 else N_EXP
                with dve.Fori(0, experts) as e:
                    with dve.Fori(0, FI) as i:
                        n = e * FI + i
                        it = n + f_it[l]
                        for j in range(2):
                            dve.wait_ge(sg_done, it * 2 + (j + 1))
                            dve.wait_ge(slot_free, n * 6 + (3 + t_ffn[l] + 2 + j + 1))
                            dve.wait_ge(act_ready, it * 2 + (2 + j))
                            v.tensor_tensor(f_act[:, j, :], f_sg[:, j, :], bank[2 + j][:, 0:256], ALU.mult)\
                                .then_inc(ffn_link, 1)
                            dve.wait_ge(ffn_link, it * 6 + (3 * j + 1))
                            if experts > 1:
                                z = v.tensor_tensor(f_act[:, j, :], f_act[:, j, :], cb[:, e, :], ALU.mult)
                            else:
                                z = v.tensor_copy(f_act[:, j, :], f_act[:, j, :])
                            z.then_inc(ffn_link, 1)
                            dve.wait_ge(ffn_link, it * 6 + (3 * j + 2))
                            if j == 0:
                                dve.wait_ge(slot_free, n * 6 + (3 + t_ffn[l]))
                            v.tensor_copy(y_hi[:, j, :], f_act[:, j, :]).then_inc(ffn_link, 1)
                            dve.wait_ge(ffn_link, it * 6 + (3 * j + 3))
                            v.tensor_tensor(y_lo[:, j, :], f_act[:, j, :], y_hi[:, j, :].bitcast(F32), ALU.subtract)\
                                .then_inc(act_ready, 1)
                        dve.wait_ge(slot_free, n * 6 + (3 + t_ffn[l] + 6))
                        dve.wait_ge(down_free, it + 1)
                        for q in range(4):
                            z = v.tensor_tensor(flat(xres[:, 2 * q:2 * q + 2, :]), flat(xres[:, 2 * q:2 * q + 2, :]),
                                                bank[4 + q][:], ALU.add)
                        z.then_inc(down_free, 1)
                dve.wait_ge(down_free, 1 + f_it[l] + FI * experts)
            norm("normf", 0, "final_norm_w")
            V, T = s["xout"]["dve"], s["xout"]["pe"]
            for t in range(NT):
                dve.wait_ge(*T.at(0, f"t{t}"))
                for q in range(2):
                    z = v.tensor_copy(v3(xtok[:, t, :])[:, 4 * q:4 * q + 4, :], v3(bank[4 + 2 * t + q][:]))
                z.then_inc(V.step(f"c{t}"), 1)


_INS = ['x', 'attn_norm_w', 'w_in', 'conv_w', 'conv_b', 'ssm_a_log', 'ssm_dt_bias', 'ssm_d', 'ssm_norm_w',
        'gdn_a_log', 'gdn_dt_bias', 'gdn_norm_w', 'rwkv_mu', 'rwkv_w0', 'rwkv_w2', 'rwkv_a0', 'rwkv_a2',
        'rwkv_g2', 'rwkv_k_k', 'rwkv_k_a', 'rwkv_r_k', 'rwkv_ln_w', 'rwkv_ln_b', 'proj_ssm', 'proj_gdn',
        'proj_rwkv', 'w_out', 'ffn_norm_w', 'dense_w_gate', 'dense_w_up', 'dense_w_down', 'moe_router',
        'moe_w_gate', 'moe_w_up', 'moe_w_down', 'final_norm_w']


def kernel(**inputs):
    import numpy as _np
    import concourse.bacc as _bacc
    from concourse import mybir as _mybir
    from concourse.bass_utils import run_bass_kernel_spmd as _run

    nc = _bacc.Bacc("TRN2", target_bir_lowering=False, num_devices=1)
    arrays, args = {}, []
    for name in _INS:
        a = _np.ascontiguousarray(inputs[name])
        arrays[f"in_{name}_dram"] = a
        args.append(nc.dram_tensor(f"in_{name}_dram", a.shape, _mybir.dt.from_np(a.dtype), kind="ExternalInput").ap())
    args.append(nc.dram_tensor("out_0_dram", (1, SEQ, D_MODEL), F32, kind="ExternalOutput").ap())
    trunk(nc, *args)
    r = _run(nc, [arrays], core_ids=[0])
    return r.results[0]["out_0_dram"]
```
